# Optimizing a Trainium2 kernel written in Bass

```python
import jax
import jax.numpy as jnp
from jax import lax
import numpy as np

D_MODEL = 1024
BATCH = 1
SEQ = 512
DEPTH = 2
DEC_BATCH = 1
DEC_SEQ = 32
PAST_LEN = 1024

CHUNK = 64
N_MIXERS = 2
N_SB_LAYERS = (DEPTH + N_MIXERS - 1) // N_MIXERS
N_RW_LAYERS = DEPTH // N_MIXERS
SB_HEADS = 16
SB_HEAD_DIM = D_MODEL // SB_HEADS
Q_BLOCK = 128
RW_HEAD_DIM = 64
RW_HEADS = D_MODEL // RW_HEAD_DIM
RW_DECAY_LORA = max(32, int(round(1.8 * D_MODEL ** 0.5 / 32)) * 32)
RW_AAA_LORA = max(32, int(round(1.8 * D_MODEL ** 0.5 / 32)) * 32)
RW_MV_LORA = max(32, int(round(1.3 * D_MODEL ** 0.5 / 32)) * 32)
RW_GATE_LORA = max(32, int(round(0.6 * D_MODEL ** 0.8 / 32)) * 32)
RW_GN_EPS = 64e-5
N_MEM = 256
XA_HEADS = 4
XA_HEAD_DIM = D_MODEL // XA_HEADS
FFN_HIDDEN = ((8 * D_MODEL // 3 + 255) // 256) * 256
NORM_EPS = 1e-6

kernel_name = 'hybrid_stickbreak_rwkv7_stream'

def rms_norm(x, gain):
    xf = x.astype(jnp.float32)
    y = xf * lax.rsqrt(jnp.mean(xf * xf, axis=-1, keepdims=True) + NORM_EPS)
    return (y * gain.astype(jnp.float32)).astype(x.dtype)

def swiglu_ffn(h, w_gate_up, w_down):
    gate, up = jnp.split(h @ w_gate_up, 2, axis=-1)
    return (jax.nn.silu(gate) * up) @ w_down

def memory_kv(mem, gain, w_kv):
    m = rms_norm(mem, gain)
    k, v = jnp.split(m @ w_kv, 2, axis=-1)
    shp = mem.shape[:2] + (XA_HEADS, XA_HEAD_DIM)
    return k.reshape(shp), v.reshape(shp)

def memory_cross_attention(h, mem_k, mem_v, w_q, w_o):
    B, L, _ = h.shape
    q = (h @ w_q).reshape(B, L, XA_HEADS, XA_HEAD_DIM)
    s = jnp.einsum('blhd,bmhd->bhlm', q, mem_k).astype(jnp.float32) * (XA_HEAD_DIM ** -0.5)
    p = jax.nn.softmax(s, axis=-1).astype(mem_v.dtype)
    o = jnp.einsum('bhlm,bmhd->blhd', p, mem_v)
    return o.reshape(B, L, D_MODEL) @ w_o

def stick_breaking_attention(q, k, v, q_offset):
    B, Lq, H, Dh = q.shape
    Lk = k.shape[1]
    blk = min(Q_BLOCK, Lq)
    n_blk = -(-Lq // blk)
    pad = n_blk * blk - Lq
    q_blocks = jnp.pad(q, ((0, 0), (0, pad), (0, 0), (0, 0)))
    q_blocks = q_blocks.reshape(B, n_blk, blk, H, Dh).transpose(1, 0, 2, 3, 4)
    key_pos = jnp.arange(Lk)
    scale = Dh ** -0.5

    def one_block(args):
        q_blk, start = args
        z = jnp.einsum('bqhd,bkhd->bhqk', q_blk, k).astype(jnp.float32) * scale
        q_pos = q_offset + start + jnp.arange(blk)
        before = key_pos[None, :] < q_pos[:, None]
        log_1m_beta = jnp.where(before, jax.nn.log_sigmoid(-z), 0.0)
        log_after = lax.cumsum(log_1m_beta, axis=3, reverse=True) - log_1m_beta
        weights = jnp.where(before, jnp.exp(jax.nn.log_sigmoid(z) + log_after), 0.0)
        return jnp.einsum('bhqk,bkhd->bqhd', weights.astype(v.dtype), v)

    starts = jnp.arange(n_blk, dtype=jnp.int32) * blk
    out = lax.map(one_block, (q_blocks, starts))
    return out.transpose(1, 0, 2, 3, 4).reshape(B, n_blk * blk, H, Dh)[:, :Lq]

def _wkv7_step(S, inp):
    r, decay, k, v, a_vec, b_vec = inp
    sa = jnp.einsum('bhij,bhj->bhi', S, a_vec)
    S = S * decay[:, :, None, :] + sa[..., None] * b_vec[:, :, None, :] + v[..., None] * k[:, :, None, :]
    return S, jnp.einsum('bhij,bhj->bhi', S, r)

def rwkv7_time_mix(h, shift_prev, state0, v_first, mu, w_r, w_k, w_v, w_o, w0, w1, w2,
                   a0, a1, a2, g1, g2, k_k, k_a, r_k, lnx_w, lnx_b, v_res):
    B, L, D = h.shape
    f32 = jnp.float32
    h_prev = jnp.concatenate([shift_prev[:, None, :].astype(h.dtype), h[:, :-1]], axis=1)
    xx = h_prev - h
    x_r, x_w, x_k, x_v, x_a, x_g = (h + xx * mu[i] for i in range(6))
    r = x_r @ w_r
    k = x_k @ w_k
    v = x_v @ w_v
    w_log = -jax.nn.softplus(-(w0 + jnp.tanh(x_w @ w1) @ w2)) - 0.5
    if v_res is None:
        v_first = v
    else:
        v0, v1, v2 = v_res
        v = v + (v_first - v) * jax.nn.sigmoid(v0 + (x_v @ v1) @ v2)
    a = jax.nn.sigmoid(a0 + (x_a @ a1) @ a2)
    g = jax.nn.sigmoid(x_g @ g1) @ g2

    def heads(t):
        return t.astype(f32).reshape(B, L, RW_HEADS, RW_HEAD_DIM)

    kk = heads(k * k_k)
    kk = kk * lax.rsqrt(jnp.maximum(jnp.sum(kk * kk, axis=-1, keepdims=True), 1e-24))
    k = k * (1 + (a - 1) * k_a)
    r_h, k_h, v_h, a_h = heads(r), heads(k), heads(v), heads(a)
    decay = jnp.exp(-jnp.exp(heads(w_log)))
    seq = tuple(jnp.moveaxis(t, 1, 0) for t in (r_h, decay, k_h, v_h, -kk, kk * a_h))
    state, y = lax.scan(_wkv7_step, state0.astype(f32), seq)
    y = jnp.moveaxis(y, 0, 1)
    mean = jnp.mean(y, axis=-1, keepdims=True)
    var = jnp.mean(jnp.square(y - mean), axis=-1, keepdims=True)
    o = ((y - mean) * lax.rsqrt(var + RW_GN_EPS)).reshape(B, L, D) * lnx_w.astype(f32) + lnx_b.astype(f32)
    bonus = jnp.sum(r_h * k_h * r_k.astype(f32), axis=-1, keepdims=True) * v_h
    o = (o + bonus.reshape(B, L, D)) * g.astype(f32)
    out = o.astype(h.dtype) @ w_o
    return out, state.astype(state0.dtype), h[:, -1], v_first

def trunk(x, mem_k, mem_v, sb_past_k, sb_past_v, rw_state0, rw_shift0, p):
    B = x.shape[0]
    past_len = 0 if sb_past_k is None else sb_past_k.shape[2]
    sb_k_rows, sb_v_rows, rw_states, rw_shifts = [], [], [], []
    v_first = None
    for layer in range(DEPTH):
        j = layer // N_MIXERS
        h = rms_norm(x, p['norm_mix'][layer])
        if layer % N_MIXERS == 0:
            q, k, v = jnp.split(h @ p['sb_w_qkv'][j], 3, axis=-1)
            shp = h.shape[:2] + (SB_HEADS, SB_HEAD_DIM)
            q, k, v = q.reshape(shp), k.reshape(shp), v.reshape(shp)
            sb_k_rows.append(k)
            sb_v_rows.append(v)
            if sb_past_k is not None:
                k = jnp.concatenate([sb_past_k[j], k], axis=1)
                v = jnp.concatenate([sb_past_v[j], v], axis=1)
            o = stick_breaking_attention(q, k, v, past_len)
            x = x + o.reshape(h.shape) @ p['sb_w_o'][j]
        else:
            if rw_state0 is None:
                state0 = jnp.zeros((B, RW_HEADS, RW_HEAD_DIM, RW_HEAD_DIM), x.dtype)
                shift0 = jnp.zeros((B, D_MODEL), x.dtype)
            else:
                state0, shift0 = rw_state0[j], rw_shift0[j]
            v_res = None if j == 0 else (p['rw_v0'][j - 1], p['rw_v1'][j - 1], p['rw_v2'][j - 1])
            out, state, shift, v_first = rwkv7_time_mix(
                h, shift0, state0, v_first, p['rw_mu'][j], p['rw_w_r'][j], p['rw_w_k'][j],
                p['rw_w_v'][j], p['rw_w_o'][j], p['rw_w0'][j], p['rw_w1'][j], p['rw_w2'][j],
                p['rw_a0'][j], p['rw_a1'][j], p['rw_a2'][j], p['rw_g1'][j], p['rw_g2'][j],
                p['rw_k_k'][j], p['rw_k_a'][j], p['rw_r_k'][j], p['rw_lnx_w'][j], p['rw_lnx_b'][j], v_res)
            rw_states.append(state)
            rw_shifts.append(shift)
            x = x + out
        h = rms_norm(x, p['norm_xattn'][layer])
        x = x + memory_cross_attention(h, mem_k[layer], mem_v[layer], p['xa_w_q'][layer], p['xa_w_o'][layer])
        h = rms_norm(x, p['norm_ffn'][layer])
        x = x + swiglu_ffn(h, p['ffn_w_gate_up'][layer], p['ffn_w_down'][layer])
    y = rms_norm(x, p['norm_final'])
    return y, jnp.stack(sb_k_rows), jnp.stack(sb_v_rows), jnp.stack(rw_states), jnp.stack(rw_shifts)

def setup_inputs(seed: int = 0) -> dict:
    key = jax.random.key(seed)
    ks = iter(jax.random.split(key, 64))
    f32 = jnp.float32
    D = D_MODEL

    def nrm(shape, scale=1.0):
        return jax.random.normal(next(ks), shape, f32) * scale

    def uni(shape, lo, hi):
        return jax.random.uniform(next(ks), shape, f32, lo, hi)

    return {
        'x_prompt': nrm((BATCH, SEQ, D)),
        'x_sample': nrm((DEC_BATCH, DEC_SEQ, D)),
        'mem_prompt': nrm((BATCH, N_MEM, D)),
        'cache_sb_k': nrm((N_SB_LAYERS, DEC_BATCH, PAST_LEN, SB_HEADS, SB_HEAD_DIM)),
        'cache_sb_v': nrm((N_SB_LAYERS, DEC_BATCH, PAST_LEN, SB_HEADS, SB_HEAD_DIM)),
        'state_rwkv_wkv': nrm((N_RW_LAYERS, DEC_BATCH, RW_HEADS, RW_HEAD_DIM, RW_HEAD_DIM), 0.3),
        'state_rwkv_shift': nrm((N_RW_LAYERS, DEC_BATCH, D)),
        'cache_mem_k': nrm((DEPTH, DEC_BATCH, N_MEM, XA_HEADS, XA_HEAD_DIM)),
        'cache_mem_v': nrm((DEPTH, DEC_BATCH, N_MEM, XA_HEADS, XA_HEAD_DIM)),
        'norm_mix': 1.0 + nrm((DEPTH, D), 0.05),
        'norm_xattn': 1.0 + nrm((DEPTH, D), 0.05),
        'norm_ffn': 1.0 + nrm((DEPTH, D), 0.05),
        'norm_mem': 1.0 + nrm((DEPTH, D), 0.05),
        'norm_final': 1.0 + nrm((D,), 0.05),
        'sb_w_qkv': nrm((N_SB_LAYERS, D, 3 * D), D ** -0.5),
        'sb_w_o': nrm((N_SB_LAYERS, D, D), D ** -0.5),
        'rw_mu': uni((N_RW_LAYERS, 6, D), 0.0, 1.0),
        'rw_w_r': nrm((N_RW_LAYERS, D, D), D ** -0.5),
        'rw_w_k': nrm((N_RW_LAYERS, D, D), D ** -0.5),
        'rw_w_v': nrm((N_RW_LAYERS, D, D), D ** -0.5),
        'rw_w_o': nrm((N_RW_LAYERS, D, D), D ** -0.5),
        'rw_w0': uni((N_RW_LAYERS, D), -5.0, -1.0),
        'rw_w1': nrm((N_RW_LAYERS, D, RW_DECAY_LORA), D ** -0.5),
        'rw_w2': nrm((N_RW_LAYERS, RW_DECAY_LORA, D), 0.1),
        'rw_a0': nrm((N_RW_LAYERS, D), 0.1),
        'rw_a1': nrm((N_RW_LAYERS, D, RW_AAA_LORA), D ** -0.5),
        'rw_a2': nrm((N_RW_LAYERS, RW_AAA_LORA, D), 0.5 * RW_AAA_LORA ** -0.5),
        'rw_v0': nrm((N_RW_LAYERS - 1, D), 0.1),
        'rw_v1': nrm((N_RW_LAYERS - 1, D, RW_MV_LORA), D ** -0.5),
        'rw_v2': nrm((N_RW_LAYERS - 1, RW_MV_LORA, D), 0.5 * RW_MV_LORA ** -0.5),
        'rw_g1': nrm((N_RW_LAYERS, D, RW_GATE_LORA), D ** -0.5),
        'rw_g2': nrm((N_RW_LAYERS, RW_GATE_LORA, D), RW_GATE_LORA ** -0.5),
        'rw_k_k': 0.85 + nrm((N_RW_LAYERS, D), 0.05),
        'rw_k_a': 1.0 + nrm((N_RW_LAYERS, D), 0.05),
        'rw_r_k': nrm((N_RW_LAYERS, RW_HEADS, RW_HEAD_DIM), 0.1),
        'rw_lnx_w': 1.0 + nrm((N_RW_LAYERS, D), 0.05),
        'rw_lnx_b': nrm((N_RW_LAYERS, D), 0.02),
        'xa_w_q': nrm((DEPTH, D, D), D ** -0.5),
        'xa_w_kv': nrm((DEPTH, D, 2 * D), D ** -0.5),
        'xa_w_o': nrm((DEPTH, D, D), D ** -0.5),
        'ffn_w_gate_up': nrm((DEPTH, D, 2 * FFN_HIDDEN), D ** -0.5),
        'ffn_w_down': nrm((DEPTH, FFN_HIDDEN, D), FFN_HIDDEN ** -0.5),
    }

def reference(x_prompt, x_sample, mem_prompt, cache_sb_k, cache_sb_v, state_rwkv_wkv, state_rwkv_shift,
              cache_mem_k, cache_mem_v, norm_mix, norm_xattn, norm_ffn, norm_mem, norm_final,
              sb_w_qkv, sb_w_o, rw_mu, rw_w_r, rw_w_k, rw_w_v, rw_w_o, rw_w0, rw_w1, rw_w2,
              rw_a0, rw_a1, rw_a2, rw_v0, rw_v1, rw_v2, rw_g1, rw_g2, rw_k_k, rw_k_a, rw_r_k,
              rw_lnx_w, rw_lnx_b, xa_w_q, xa_w_kv, xa_w_o, ffn_w_gate_up, ffn_w_down):
    p = dict(norm_mix=norm_mix, norm_xattn=norm_xattn, norm_ffn=norm_ffn, norm_final=norm_final,
             sb_w_qkv=sb_w_qkv, sb_w_o=sb_w_o, rw_mu=rw_mu, rw_w_r=rw_w_r, rw_w_k=rw_w_k,
             rw_w_v=rw_w_v, rw_w_o=rw_w_o, rw_w0=rw_w0, rw_w1=rw_w1, rw_w2=rw_w2, rw_a0=rw_a0,
             rw_a1=rw_a1, rw_a2=rw_a2, rw_v0=rw_v0, rw_v1=rw_v1, rw_v2=rw_v2, rw_g1=rw_g1,
             rw_g2=rw_g2, rw_k_k=rw_k_k, rw_k_a=rw_k_a, rw_r_k=rw_r_k, rw_lnx_w=rw_lnx_w,
             rw_lnx_b=rw_lnx_b, xa_w_q=xa_w_q, xa_w_o=xa_w_o, ffn_w_gate_up=ffn_w_gate_up,
             ffn_w_down=ffn_w_down)

    mem_kv = [memory_kv(mem_prompt, norm_mem[layer], xa_w_kv[layer]) for layer in range(DEPTH)]
    prompt_mem_k = jnp.stack([kv[0] for kv in mem_kv])
    prompt_mem_v = jnp.stack([kv[1] for kv in mem_kv])
    y_prompt, prompt_sb_k, prompt_sb_v, prompt_rwkv_wkv, prompt_rwkv_shift = trunk(
        x_prompt, prompt_mem_k, prompt_mem_v, None, None, None, None, p)

    y_sample, sample_sb_k, sample_sb_v, sample_rwkv_wkv, sample_rwkv_shift = trunk(
        x_sample, cache_mem_k, cache_mem_v, cache_sb_k, cache_sb_v, state_rwkv_wkv, state_rwkv_shift, p)

    return (y_prompt, y_sample, prompt_sb_k, prompt_sb_v, prompt_rwkv_wkv, prompt_rwkv_shift,
            prompt_mem_k, prompt_mem_v, sample_sb_k, sample_sb_v, sample_rwkv_wkv, sample_rwkv_shift)


_drawn_inputs = setup_inputs


def setup_inputs(seed=0):
    import zlib

    import numpy as np

    out = dict(_drawn_inputs(seed))
    spreads = {}
    factors = {'norm_xattn': 7.99, 'rw_lnx_w': 3.089, 'rw_lnx_b': 7.125}
    for name, (base, spread) in spreads.items():
        noise = np.random.default_rng([zlib.crc32(name.encode()), seed]).standard_normal(out[name].shape)
        drawn = base * np.exp(spread * noise) if base else spread * noise
        out[name] = jnp.asarray(drawn.astype(out[name].dtype))
    for name, factor in factors.items():
        out[name] = (out[name] * factor).astype(out[name].dtype)
    return out
```

```python
from contextlib import ExitStack, contextmanager

import numpy as np
import concourse.bass as bass
from concourse import mybir

F32 = mybir.dt.float32
BF16 = mybir.dt.bfloat16
ALU = mybir.AluOpType
ACT = mybir.ActivationFunctionType
AX_X = mybir.AxisListType.X

P = 128
D = 1024
KT = D // P
SEQ = 512
DEC = 32
T = SEQ + DEC
HALF = T // 2
PAST = 1024
NMEM = 256
HD = 64
PAIRS = D // P
XH = 4
FF = 2816
FT = FF // P
DEPTH = 2
EPS = 1e-6
GN_EPS = 64e-5
L = 64
REGION = KT * T
RING = 4
UNIT_KT = 11
LORA = 64
GATE = 160
GK = GATE // 2
PRIMED = 1

ROWS_A = [("norm_mix", 16), ("norm_xattn", 16), ("norm_ffn", 16), ("norm_mem", 16), ("norm_final", 8),
          ("rw_w0", 8), ("rw_a0", 8), ("rw_k_k", 8), ("rw_k_a", 8), ("rw_r_k", 8), ("rw_lnx_w", 8), ("rw_lnx_b", 8)]
ROWS_B = [("rw_mu", 48), ("state_rwkv_shift", 8)]


class Job:

    def __init__(self, n, kt, src, moving, kp=P, m=lambda s: P, slot=lambda s: s,
                 opens=lambda s: True, closes=lambda s: True, tokens=T):
        self.n, self.kt, self.src, self.moving, self.kp, self.m = n, kt, src, moving, kp, m
        self.slot, self.opens, self.closes, self.tokens = slot, opens, closes, tokens
        self.iters = n // RING


class Core:

    def __init__(self, nc, ctx, ins, outs):
        self.nc, self.ctx, self.ins, self.outs = nc, ctx, ins, outs
        self.arena = ctx.enter_context(nc.sbuf_tensor("arena", [P, 10 * REGION], F32))
        self.ring = ctx.enter_context(nc.sbuf_tensor("weight_ring", [P, RING, UNIT_KT, P], F32))
        self.psum = ctx.enter_context(nc.psum_tensor("psum", [P, 8, 512], F32))
        self.stages = 0
        self.stage_sems = []
        self.weights_landed = [nc.alloc_semaphore(f"weights_landed{s}") for s in range(RING)]
        self.unit_done = [nc.alloc_semaphore(f"unit_done{s}") for s in range(RING)]
        self.slot_emptied = [nc.alloc_semaphore(f"slot_emptied{s}") for s in range(RING)]
        self.rounds = 0
        for sem in self.slot_emptied:
            nc.sync.sem_inc(sem, PRIMED)
        self.emptied = [PRIMED] * RING
        self.jobs = []

    def sem(self, name, primed=False):
        self.stage_sems.append(self.nc.alloc_semaphore(f"{name}_{self.stages}"))
        if primed:
            self.nc.sync.sem_inc(self.stage_sems[-1], PRIMED)
        return self.stage_sems[-1]

    @contextmanager
    def stage(self):
        with self.nc.Block() as block:
            yield block
        if self.stage_sems:
            self.nc.clear_and_free_semaphores(self.stage_sems)
            self.nc.all_engine_barrier()
        self.stage_sems = []
        self.stages += 1

    def tile(self, name, shape, dtype=F32):
        return self.ctx.enter_context(self.nc.sbuf_tensor(name, shape, dtype))

    def ring_words(self):
        return self.ring[:].rearrange("p s k n -> p (s k n)")

    def region(self, r, k=KT, t=T, at=0):
        a = r * REGION + at
        return self.arena[:, a:a + k * t].rearrange("p (k t) -> p k t", k=k)

    def flat(self, r, n, at=0):
        a = r * REGION + at
        return self.arena[:, a:a + n]


def load_unit(c, sp, job, it, s):
    sp.dma_start(c.ring[0:job.kp, s, 0:job.kt, 0:job.m(s)], job.src(it, s)).then_inc(c.weights_landed[s], 16)


def stream_weights(c, sp, job, nxt):
    base = c.rounds
    if job.iters > 1:
        with sp.Fori(1, job.iters) as it:
            for s in range(RING):
                sp.wait_ge(c.unit_done[s], it + base)
                load_unit(c, sp, job, it, s)
    if nxt is not None:
        for s in range(RING):
            sp.wait_ge(c.unit_done[s], base + job.iters)
            load_unit(c, sp, nxt, 0, s)


def multiply_units(c, pe, job):
    nc, base = c.nc, c.rounds
    w = job.tokens // 2 if job.tokens > 512 else job.tokens
    closes = [sum(job.slot(s) == q and job.closes(s) for s in range(RING)) for q in range(RING)]
    with pe.Fori(0, job.iters) as it:
        for s in range(RING):
            q = job.slot(s)
            pe.wait_ge(c.weights_landed[s], it * 16 + 16 * (base + 1))
            if job.opens(s):
                pe.wait_ge(c.slot_emptied[q], it * closes[q] + c.emptied[q])
            for k in range(job.kt):
                for h in range(job.tokens // w):
                    last = nc.tensor.matmul(
                        c.psum[0:job.m(s), 2 * q + h, 0:w], c.ring[0:job.kp, s, k, 0:job.m(s)],
                        job.moving(s)[:, k, h * w:(h + 1) * w],
                        start=job.opens(s) and k == 0, stop=job.closes(s) and k == job.kt - 1)
            last.then_inc(c.unit_done[s], 1)


def project(c, job, nxt, by_vector, by_scalar, before=None):
    nc, base = c.nc, c.rounds
    wide = job.tokens > 512

    def view(s):
        q = job.slot(s)
        if wide:
            return c.psum[0:job.m(s), 2 * q:2 * q + 2, 0:HALF]
        return c.psum[0:job.m(s), 2 * q, 0:job.tokens]

    def empty(eng, emits):
        with eng.Fori(0, job.iters) as it:
            for s in sorted(emits):
                eng.wait_ge(c.unit_done[s], it + base + 1)
                emits[s](it, view(s)).then_inc(c.slot_emptied[job.slot(s)], 1)

    with c.stage() as block:
        @block.sync
        def _(sp):
            stream_weights(c, sp, job, nxt)

        @block.tensor
        def _(pe):
            multiply_units(c, pe, job)

        @block.vector
        def _(dve):
            if before is not None:
                before(dve)
            if by_vector:
                empty(dve, by_vector)

        @block.scalar
        def _(act):
            if by_scalar:
                empty(act, by_scalar)
    for s in list(by_vector) + list(by_scalar):
        c.emptied[job.slot(s)] += job.iters
    c.rounds += job.iters


def halves(ap):
    return ap.rearrange("p o (a b) -> p (o a) b", a=2)


def copy_to(c, dst, scale=1.0, first=0, vector=(0, 2), scalar=(1, 3)):
    nc = c.nc

    def emit(s, eng):
        def run(it, ps):
            out = dst[:, bass.ds(it * RING + (first + s), 1), :]
            out = halves(out) if dst.shape[-1] == T else out.rearrange("p o t -> p (o t)")
            if eng == "v":
                return nc.vector.tensor_scalar(out, ps, scale, None, ALU.mult)
            return nc.scalar.activation(out, ps, ACT.Copy, scale=scale)
        return run
    return {s: emit(s, "v") for s in vector}, {s: emit(s, "s") for s in scalar}


def add_to(c, x, units=(0, 1, 2, 3), per=1):
    nc = c.nc

    def emit(s):
        def run(it, ps):
            out = halves(x[:, bass.ds(it * (RING // per) + s // per, 1), :])
            return nc.vector.tensor_tensor(out, ps, out, ALU.add)
        return run
    return {s: emit(s) for s in units}


def columns(w, kp=P):
    v = w.rearrange("(k p) m -> p k m", p=kp)
    return lambda it, s: v[:, :, bass.ds(it * (RING * P) + s * P, P)]


def constants(c):
    nc = c.nc
    c.ident = c.tile("ident", [P, P])
    c.ones = c.tile("ones", [P, P])
    c.head_ones = c.tile("head_ones", [P, P])
    c.later = c.tile("later", [P, P])
    c.neg_ones = c.tile("neg_ones", [P, P])
    c.in16_up = c.tile("in16_up", [P, P])
    c.in16_lo = c.tile("in16_lo", [P, P])
    c.to32_lo = c.tile("to32_lo", [P, P])
    c.to64_lo = c.tile("to64_lo", [P, P])
    c.strict_up = c.tile("strict_up", [P, P])
    c.incl_up = c.tile("incl_up", [P, L])
    c.ident_bf = c.tile("ident_bf", [P, P], BF16)
    c.barred = c.tile("barred", [P, P], BF16)
    sel = c.sem("constant_selected")
    cast = c.sem("constant_cast")
    n = [0]

    with c.stage() as block:
        @block.gpsimd
        def _(pool):
            def step(ins):
                ins.then_inc(sel, 1)
                n[0] += 1
                pool.wait_ge(sel, n[0])

            def keep(ap, pattern, op, fill, base, mult):
                step(nc.gpsimd.affine_select(out=ap, in_=ap, pattern=pattern, compare_op=op, fill=fill,
                                             base=base, channel_multiplier=mult))

            def same_block(t, w):
                v = t[:].rearrange("p (b i) -> p b i", i=w)
                keep(v, [[-w, P // w], [0, w]], ALU.is_ge, 0.0, 0, 1)
                keep(v, [[w, P // w], [0, w]], ALU.is_ge, 0.0, w - 1, -1)

            for t, v in ((c.ident, 1.0), (c.ones, 1.0), (c.head_ones, 1.0), (c.later, -1.0), (c.neg_ones, -1.0),
                         (c.in16_up, 1.0), (c.in16_lo, 1.0), (c.to32_lo, 1.0), (c.to64_lo, 1.0),
                         (c.strict_up, 1.0), (c.incl_up, 1.0)):
                step(nc.gpsimd.memset(t[:], v))
            keep(c.ident[:], [[-1, P]], ALU.is_equal, 0.0, 0, 1)
            same_block(c.head_ones, HD)
            keep(c.later[:], [[-1, P]], ALU.is_ge, 0.0, 0, 1)
            keep(c.in16_up[:], [[1, P]], ALU.is_gt, 0.0, 0, -1)
            same_block(c.in16_up, 16)
            keep(c.in16_lo[:], [[-1, P]], ALU.is_gt, 0.0, 0, 1)
            same_block(c.in16_lo, 16)
            for t, w in ((c.to32_lo, 32), (c.to64_lo, 64)):
                v = t[:].rearrange("p (b h i) -> p b h i", h=2, i=w // 2)
                keep(v, [[0, P // w], [-1, 2], [0, w // 2]], ALU.is_ge, 0.0, 0, 0)
                same_block(t, w)
                keep(v, [[-w, P // w], [0, 2], [0, w // 2]], ALU.is_ge, 0.0, -(w // 2), 1)
            keep(c.strict_up[:], [[1, P]], ALU.is_gt, 0.0, 0, -1)
            same_block(c.strict_up, L)
            keep(c.incl_up[0:L, :], [[1, L]], ALU.is_ge, 0.0, 0, -1)
            keep(c.incl_up[L:P, :], [[1, L]], ALU.is_ge, 0.0, 0, -1)

        @block.vector
        def _(dve):
            dve.wait_ge(sel, n[0])
            nc.vector.tensor_copy(c.ident_bf[:], c.ident[:]).then_inc(cast, 1)
            nc.vector.tensor_scalar(c.barred[:], c.later[:], float(2 ** 100), None, ALU.mult).then_inc(cast, 1)
            dve.wait_ge(cast, 2)


def load_vectors(c):
    nc = c.nc
    stack = [c.flat(5, P), c.flat(5, P, at=P)[0:56, :]]
    c.columns = c.tile("vector_columns", [P, P + 56])
    landed, turned, copied = c.sem("vectors_landed"), c.sem("vectors_turned"), c.sem("vectors_copied")
    c.vec = {}
    n = 0
    with c.stage() as block:
        @block.scalar
        def _(act):
            nonlocal n
            for t, rows, base in ((stack[0], ROWS_A, 0), (stack[1], ROWS_B, P)):
                at = 0
                for name, k in rows:
                    src = c.ins[name]
                    dims = " ".join(f"d{i}" for i in range(len(src.shape)))
                    src = src.rearrange(f"{dims} -> ({dims})").rearrange("(k p) -> k p", p=P)
                    act.dma_start(t[at:at + k, :], src).then_inc(landed, 16)
                    c.vec[name] = c.columns[:, base + at:base + at + k]
                    at += k
                    n += 1

        @block.tensor
        def _(pe):
            pe.wait_ge(landed, 16 * n)
            nc.tensor.transpose(c.psum[:, 0, 0:P], stack[0], c.ident[:])
            nc.tensor.transpose(c.psum[:, 0, P:P + 56], stack[1], c.ident[0:56, 0:56]).then_inc(turned, 1)

        @block.vector
        def _(dve):
            dve.wait_ge(turned, 1)
            nc.vector.tensor_copy(c.columns[:], c.psum[:, 0, 0:P + 56]).then_inc(copied, 1)
            dve.wait_ge(copied, 1)


def load_turned(c, name, groups, width):
    nc = c.nc
    landed, turned, copied = c.sem(name + "_landed"), c.sem(name + "_turned"), c.sem(name + "_copied")
    steps = []
    for src, stage, dst in groups:
        n = src.shape[0]
        for m in range(max(1, n // P)):
            for k in range(0, KT, 4):
                steps.append((stage[0:min(n, P), m, :], min(n, P), m, k, dst))
    with c.stage() as block:
        @block.scalar
        def _(act):
            for src, stage, dst in groups:
                n = src.shape[0]
                p = min(n, P)
                act.dma_start(stage[0:p, 0:max(1, n // P), :], src.rearrange("(m p) d -> p m d", p=p)).then_inc(landed, 16)

        @block.tensor
        def _(pe):
            pe.wait_ge(landed, 16 * len(groups))
            for i, (st, p, m, k, dst) in enumerate(steps):
                if i >= 4:
                    pe.wait_ge(copied, i - 3)
                for j in range(4):
                    last = nc.tensor.transpose(c.psum[:, i % 4, j * P:j * P + p], st[:, (k + j) * P:(k + j + 1) * P],
                                               c.ident[0:p, 0:p])
                last.then_inc(turned, 1)

        @block.vector
        def _(dve):
            for i, (st, p, m, k, dst) in enumerate(steps):
                dve.wait_ge(turned, i + 1)
                nc.vector.tensor_copy(dst[:, k:k + 4, m * P:m * P + p],
                                      c.psum[:, i % 4, :].rearrange("p (j t) -> p j t", j=4)[:, :, 0:p]).then_inc(copied, 1)
            dve.wait_ge(copied, len(steps))


def rms(c, name, x, h, gain, tokens=T, square=None):
    nc = c.nc
    w = tokens // 2 if tokens > 512 else tokens
    nb = tokens // w
    sq, inv = c.flat(9, 4 * tokens), c.flat(9, tokens, at=4 * T)
    sq = sq.rearrange("p (k t) -> p k t", k=4)
    root = c.flat(9, tokens, at=5 * T)
    squared, summed = c.sem(name + "_squared"), c.sem(name + "_summed")
    meaned, rooted, inverted, scaled = (c.sem(name + x) for x in ("_meaned", "_rooted", "_inverted", "_scaled"))
    used = c.sem(name + "_square_used")
    view = c.psum[:, 0:nb, 0:w]

    def shape(ap):
        return ap.rearrange("p (a b) -> p a b", a=nb)

    with c.stage() as block:
        @block.scalar
        def _(act):
            for k in range(KT):
                if k >= 4:
                    act.wait_ge(used, k - 3)
                nc.scalar.activation(sq[:, k % 4, :], x[:, k, :], ACT.Square).then_inc(squared, 1)
            act.wait_ge(meaned, 1)
            nc.scalar.activation(root, root, ACT.Sqrt).then_inc(rooted, 1)

        @block.tensor
        def _(pe):
            for k in range(KT):
                pe.wait_ge(squared, k + 1)
                for b in range(nb):
                    last = nc.tensor.matmul(c.psum[:, b, 0:w], c.ones[:], sq[:, k % 4, b * w:(b + 1) * w],
                                            start=k == 0, stop=k == KT - 1)
                last.then_inc(used, 1)

        @block.vector
        def _(dve):
            dve.wait_ge(used, KT)
            nc.vector.tensor_scalar(shape(root), view, 1.0 / D, EPS, ALU.mult, ALU.add).then_inc(meaned, 1)
            dve.wait_ge(rooted, 1)
            nc.vector.reciprocal(inv, root).then_inc(inverted, 1)
            dve.wait_ge(inverted, 1)
            for k in range(0, KT):
                nc.vector.scalar_tensor_tensor(out=h[:, k, :], in0=x[:, k, :], scalar=gain[:, k:k + 1], in1=inv,
                                               op0=ALU.mult, op1=ALU.mult).then_inc(scaled, 1)
            dve.wait_ge(scaled, KT)


SCORE_AT = {0: 0, 1: 512, 3: 896, 2: 1024}
SCORES = 1280
KEY_TILES = SEQ // P
PAST_TILES = PAST // P
EXP_CAP = 30.0
SAMPLE_SCORES = (PAST_TILES + 1) * 2 * DEC


def stick_breaking(c, q, k, v, o, scratch):
    nc, ins, outs = c.nc, c.ins, c.outs
    at = [0]

    def part(*shape):
        n = int(np.prod(shape))
        ap = c.flat(scratch, n, at=at[0])
        at[0] += n
        return ap if len(shape) == 1 else ap.rearrange("p (a b) -> p a b", a=shape[0])

    k_pair, v_pair = part(T), part(T)
    q_pad = part(2, T)
    k_rows, v_rows, k_rows_new = part(KEY_TILES, P), part(KEY_TILES, P), part(P)
    past_k = part(PAST_TILES, P)
    past_v = part(PAST_TILES + 1, P)
    past_kt = part((PAST_TILES + 1) * P)
    es = [part(SCORES), part(SCORES), part(SAMPLE_SCORES)]
    sps = [part(SCORES), part(SCORES), part(SAMPLE_SCORES)]
    flat_psum = c.psum[:].rearrange("p b n -> p (b n)")
    zs = [flat_psum[:, 0:SCORES], flat_psum[:, 3 * 512:3 * 512 + SCORES], flat_psum[:, 6 * 512:6 * 512 + SAMPLE_SCORES]]

    zeroed, pair_staged = c.sem("pads_zeroed"), c.sem("pair_staged")
    past_k_landed, past_v_landed = c.sem("past_k_landed"), c.sem("past_v_landed")
    rows_turned, past_turned = c.sem("rows_turned"), c.sem("past_turned", primed=True)
    k_rows_ready, v_rows_ready, new_rows_ready = c.sem("k_rows_ready"), c.sem("v_rows_ready"), c.sem("new_rows_ready")
    past_kt_lo, past_kt_hi = c.sem("past_kt_lo"), c.sem("past_kt_hi")
    rows_stored = c.sem("rows_stored", primed=True)
    scored = [c.sem(f"scored{u}", primed=True) for u in range(3)]
    capped = [c.sem(f"scores_capped{u}") for u in range(3)]
    exp_taken = [c.sem(f"exp_taken{u}") for u in range(3)]
    log_taken = [c.sem(f"log_taken{u}") for u in range(3)]
    sp_ready = [c.sem(f"softplus_ready{u}") for u in range(3)]
    summed = [c.sem(f"sums_added{u}") for u in range(3)]
    w_ready = [c.sem(f"weights_ready{u}") for u in range(3)]
    o_done, o_copied = c.sem("o_done"), c.sem("o_copied", primed=True)
    so_done, so_copied = c.sem("sample_o_done", primed=True), c.sem("sample_o_copied", primed=True)

    def rows(ap, w):
        return ap.rearrange("l b (m p) h d -> (l b m) p (h d)", p=w)

    nc.scalar.preload_act_table_set("natural_log_exp_and_others")
    with c.stage() as block:
        @block.sync
        def _(sp):
            with sp.Fori(0, PAIRS) as it:
                cols = bass.ds(it * P, P)
                sp.wait_ge(past_turned, it * 2 + PRIMED)
                sp.dma_start(past_k, rows(ins["cache_sb_k"], P).rearrange("m p n -> p m n")[:, :, cols]).then_inc(past_k_landed, 16)
                sp.wait_ge(so_done, it + PRIMED)
                sp.dma_start(past_v[:, 0:PAST_TILES, :], rows(ins["cache_sb_v"], P).rearrange("m p n -> p m n")[:, :, cols]).then_inc(past_v_landed, 16)
                sp.wait_ge(k_rows_ready, it + 1)
                sp.dma_start(rows(outs["prompt_sb_k"], P).rearrange("m p n -> p m n")[:, :, cols], k_rows).then_inc(rows_stored, 16)
                sp.wait_ge(v_rows_ready, it + 1)
                sp.dma_start(rows(outs["prompt_sb_v"], P).rearrange("m p n -> p m n")[:, :, cols], v_rows).then_inc(rows_stored, 16)
                sp.wait_ge(new_rows_ready, it * 2 + 2)
                sp.dma_start(rows(outs["sample_sb_k"], DEC).rearrange("m p n -> p m n")[:, :, cols], k_rows_new[0:DEC, :].rearrange("p (o n) -> p o n", o=1)).then_inc(rows_stored, 16)
                sp.dma_start(rows(outs["sample_sb_v"], DEC).rearrange("m p n -> p m n")[:, :, cols], past_v[0:DEC, PAST_TILES:PAST_TILES + 1, :]).then_inc(rows_stored, 16)
            sp.wait_ge(rows_stored, PAIRS * 64 + PRIMED)

        @block.gpsimd
        def _(pool):
            nc.gpsimd.memset(q_pad, 0.0).then_inc(zeroed, 1)
            nc.gpsimd.memset(past_kt[:, PAST:], 0.0).then_inc(zeroed, 1)
            nc.gpsimd.memset(past_v[:, PAST_TILES, :], 0.0).then_inc(zeroed, 1)
            pool.wait_ge(zeroed, 3)
            with pool.Fori(0, PAIRS) as it:
                for u in range(3):
                    pool.wait_ge(scored[u], it + PRIMED)
                pair = lambda x: x[:, bass.ds(it, 1), :].rearrange("p o t -> p (o t)")
                nc.gpsimd.tensor_copy(k_pair, pair(k)).then_inc(pair_staged, 1)
                nc.gpsimd.tensor_copy(v_pair, pair(v)).then_inc(pair_staged, 1)
                nc.gpsimd.tensor_copy(past_kt[:, PAST:PAST + DEC], k[:, bass.ds(it, 1), SEQ:T].rearrange("p o t -> p (o t)")).then_inc(pair_staged, 1)

        @block.tensor
        def _(pe):
            with pe.Fori(0, PAIRS) as it:
                pe.wait_ge(pair_staged, it * 5 + 5)
                pe.wait_ge(o_copied, it + PRIMED)
                for j in range(KEY_TILES):
                    last = nc.tensor.transpose(c.psum[:, 0, j * P:(j + 1) * P], k_pair[:, j * P:(j + 1) * P], c.ident[:])
                last.then_inc(rows_turned, 1)
                pe.wait_ge(so_copied, it * 2 + PRIMED)
                for j in range(KEY_TILES):
                    last = nc.tensor.transpose(c.psum[:, 1, j * P:(j + 1) * P], v_pair[:, j * P:(j + 1) * P], c.ident[:])
                last.then_inc(rows_turned, 1)
                nc.tensor.transpose(c.psum[0:DEC, 2, 0:P], k_pair[:, SEQ:T], c.ident[:])
                nc.tensor.transpose(c.psum[0:DEC, 2, P:2 * P], v_pair[:, SEQ:T], c.ident[:]).then_inc(rows_turned, 1)
                pe.wait_ge(past_k_landed, it * 16 + 16)
                for b in range(2):
                    for j in range(4):
                        last = nc.tensor.transpose(c.psum[:, 3 + b, j * P:(j + 1) * P], past_k[:, 4 * b + j, :], c.ident[:])
                    last.then_inc(past_turned, 1)
                for h in range(2):
                    if h == 0:
                        pe.wait_ge(k_rows_ready, it + 1)
                        pe.wait_ge(v_rows_ready, it + 1)
                        pe.wait_ge(new_rows_ready, it * 2 + 2)
                    else:
                        pe.wait_ge(past_kt_lo, it + 1)
                        pe.wait_ge(past_kt_hi, it + 1)
                    for j in (0, 1, 3, 2):
                        a = SCORE_AT[j]
                        last = nc.tensor.matmul(zs[h][:, a:a + SEQ - j * P], k_pair[:, j * P:(j + 1) * P], q_pad[:, h, j * P:SEQ],
                                                start=j != 3, stop=False, skip_group_check=True)
                        last = nc.tensor.matmul(zs[h][:, a:a + P], c.ident_bf[:], c.barred[:], start=False, stop=False, skip_group_check=True)
                    last.then_inc(scored[h], 1)
                for j in range(PAST_TILES + 1):
                    last = nc.tensor.matmul(zs[2][:, j * 2 * DEC:(j + 1) * 2 * DEC], past_kt[:, j * P:(j + 1) * P], q_pad[:, :, SEQ:T],
                                            start=j in (0, PAST_TILES), stop=False, skip_group_check=True)
                for h in range(2):
                    a = PAST_TILES * 2 * DEC + h * DEC
                    last = nc.tensor.matmul(zs[2][:, a:a + DEC], c.ident_bf[:], c.barred[:, 0:DEC], start=False, stop=False, skip_group_check=True)
                last.then_inc(scored[2], 1)
                for h in range(2):
                    pe.wait_ge(sp_ready[h], it + 1)
                    for j in (0, 1, 3, 2):
                        a, n = SCORE_AT[j], SEQ - j * P
                        last = nc.tensor.matmul(zs[h][:, a:a + n], c.later[:], sps[h][:, a:a + n],
                                                start=False, stop=j == KEY_TILES - 1, skip_group_check=True)
                        for i in range(j + 1, KEY_TILES):
                            b, m = SCORE_AT[i], SEQ - i * P
                            last = nc.tensor.matmul(zs[h][:, a + n - m:a + n], c.neg_ones[:], sps[h][:, b:b + m],
                                                    start=False, stop=i == KEY_TILES - 1, skip_group_check=True)
                    last.then_inc(summed[h], 1)
                pe.wait_ge(sp_ready[2], it + 1)
                nc.tensor.matmul(zs[2][:, 512:], c.later[:], sps[2][:, 512:], start=False, stop=True, skip_group_check=True)
                last = nc.tensor.matmul(zs[2][:, 0:512], c.later[:], sps[2][:, 0:512], start=False, stop=False, skip_group_check=True)
                for j in range(1, PAST_TILES + 1):
                    n = min(PAST_TILES, PAST_TILES + 1 - j) * 2 * DEC
                    last = nc.tensor.matmul(zs[2][:, 0:n], c.neg_ones[:], sps[2][:, j * 2 * DEC:j * 2 * DEC + n],
                                            start=False, stop=j == PAST_TILES, skip_group_check=True)
                last.then_inc(summed[2], 1)
                for h in range(2):
                    r = slice(h * HD, (h + 1) * HD)
                    pe.wait_ge(w_ready[h], it + 1)
                    for j in range(KEY_TILES):
                        a = SCORE_AT[j]
                        last = nc.tensor.matmul(c.psum[r, 0, j * P:SEQ], v_rows[:, j, r], es[h][:, a:a + SEQ - j * P],
                                                start=j == 0, stop=j == KEY_TILES - 1, skip_group_check=True)
                last.then_inc(o_done, 1)
                pe.wait_ge(w_ready[2], it + 1)
                pe.wait_ge(past_v_landed, it * 16 + 16)
                for j in range(PAST_TILES + 1):
                    last = nc.tensor.matmul(c.psum[:, 1, 0:2 * DEC], past_v[:, j, :], es[2][:, j * 2 * DEC:(j + 1) * 2 * DEC],
                                            start=j == 0, stop=j == PAST_TILES)
                last.then_inc(so_done, 1)

        @block.vector
        def _(dve):
            with dve.Fori(0, PAIRS) as it:
                dve.wait_ge(rows_stored, it * 64 + PRIMED)
                dve.wait_ge(rows_turned, it * 3 + 2)
                nc.vector.tensor_copy(v_rows, c.psum[:, 1, :].rearrange("p (j n) -> p j n", j=4)).then_inc(v_rows_ready, 1)
                dve.wait_ge(past_turned, it * 2 + 1 + PRIMED)
                nc.vector.tensor_copy(past_kt[:, 0:512], c.psum[:, 3, :]).then_inc(past_kt_lo, 1)
                for u in range(3):
                    dve.wait_ge(scored[u], it + 1 + PRIMED)
                    nc.vector.tensor_scalar(es[u], zs[u], EXP_CAP, None, ALU.min).then_inc(capped[u], 1)
                for u in range(3):
                    dve.wait_ge(log_taken[u], it + 1)
                    nc.vector.tensor_tensor(sps[u], zs[u], es[u], ALU.max).then_inc(sp_ready[u], 1)
                dve.wait_ge(o_done, it + 1)
                nc.vector.tensor_scalar(o[:, bass.ds(it, 1), 0:SEQ].rearrange("p o t -> p (o t)"), c.psum[:, 0, :], 1.0, None, ALU.mult).then_inc(o_copied, 1)

        @block.scalar
        def _(act):
            act.wait_ge(zeroed, 3)
            with act.Fori(0, PAIRS) as it:
                for u in range(3):
                    act.wait_ge(scored[u], it + PRIMED)
                for h in range(2):
                    r = slice(h * HD, (h + 1) * HD)
                    nc.scalar.copy(q_pad[r, h, :], q[r, bass.ds(it, 1), :].rearrange("p o t -> p (o t)")).then_inc(pair_staged, 1)
                act.wait_ge(rows_stored, it * 64 + PRIMED)
                act.wait_ge(rows_turned, it * 3 + 1)
                nc.scalar.copy(k_rows, c.psum[:, 0, :].rearrange("p (j n) -> p j n", j=4)).then_inc(k_rows_ready, 1)
                act.wait_ge(rows_turned, it * 3 + 3)
                nc.scalar.copy(k_rows_new[0:DEC, :], c.psum[0:DEC, 2, 0:P]).then_inc(new_rows_ready, 1)
                nc.scalar.copy(past_v[0:DEC, PAST_TILES, :], c.psum[0:DEC, 2, P:2 * P]).then_inc(new_rows_ready, 1)
                act.wait_ge(past_turned, it * 2 + 2 + PRIMED)
                nc.scalar.copy(past_kt[:, 512:PAST], c.psum[:, 4, :]).then_inc(past_kt_hi, 1)
                for u in range(3):
                    act.wait_ge(capped[u], it + 1)
                    nc.scalar.activation(es[u], es[u], ACT.Exp).then_inc(exp_taken[u], 1)
                    act.wait_ge(exp_taken[u], it + 1)
                    nc.scalar.activation(es[u], es[u], ACT.Ln, bias=1.0).then_inc(log_taken[u], 1)
                for u in range(3):
                    act.wait_ge(summed[u], it + 1)
                    nc.scalar.activation(es[u], zs[u], ACT.Exp).then_inc(w_ready[u], 1)
                act.wait_ge(so_done, it + 1 + PRIMED)
                for h in range(2):
                    r = slice(h * HD, (h + 1) * HD)
                    nc.scalar.copy(o[r, bass.ds(it, 1), SEQ:T].rearrange("p o t -> p (o t)"),
                                   c.psum[r, 1, h * DEC:(h + 1) * DEC]).then_inc(so_copied, 1)


def memory_rows(c, name, layer, kv, k_rows_all):
    nc = c.nc
    turned, copied, stored = c.sem(name + "_turned"), c.sem(name + "_copied"), c.sem(name + "_stored")
    steps = [(m, f) for f in range(0, 2 * KT, 4) for m in range(NMEM // P)]
    with c.stage() as block:
        @block.tensor
        def _(pe):
            for i, (m, f) in enumerate(steps):
                if i >= 4:
                    pe.wait_ge(copied, i - 3)
                for j in range(4):
                    last = nc.tensor.transpose(c.psum[:, i % 4, j * P:(j + 1) * P], kv[:, f + j, m * P:(m + 1) * P], c.ident[:])
                last.then_inc(turned, 1)

        @block.vector
        def _(dve):
            for i, (m, f) in enumerate(steps):
                dve.wait_ge(turned, i + 1)
                nc.vector.tensor_copy(k_rows_all[:, m, f * P:(f + 4) * P], c.psum[:, i % 4, :]).then_inc(copied, 1)

        @block.sync
        def _(sp):
            half = len(steps) // 2
            for i, out in enumerate(("prompt_mem_k", "prompt_mem_v")):
                sp.wait_ge(copied, half * (i + 1))
                sp.dma_start(c.outs[out][layer, 0].rearrange("(m p) h d -> p m (h d)", p=P),
                             k_rows_all[:, :, i * D:(i + 1) * D]).then_inc(stored, 16)
            sp.wait_ge(stored, 32)


def cross_attention(c, name, q, kv, kv_rows, s_kt, s_v, o, scratch):
    nc = c.nc
    MT = NMEM // P
    QT = SEQ // P
    at = [0]

    def part(*shape):
        n = int(np.prod(shape))
        ap = c.flat(scratch, n, at=at[0])
        at[0] += n
        return ap if len(shape) == 1 else ap.rearrange("p (a b) -> p a b", a=shape[0])
    qh, vh, svh = part(2, T), part(MT, 2 * P), part(MT, 2 * P)
    prob, prob_s = part(QT, NMEM), part(NMEM)
    prob_t, prob_ts = part(MT, SEQ), part(MT, DEC)
    neg_max, total, inverse = part(QT + 1), part(QT + 1), part(QT + 1)
    assert at[0] <= 2 * REGION

    s = {x: c.sem(f"{name}_{x}", primed=x in ("weighed_s", "o_copied")) for x in (
        "staged", "scored", "scored_s", "maxed", "exped", "inverted", "scaled", "turned", "turned_s",
        "copied", "copied_s", "weighed", "weighed_s", "o_copied")}
    zp = c.psum[:, 0:2, :].rearrange("p b (i n) -> p (b i) n", i=2)
    zsamp = c.psum[0:DEC, 2, 0:NMEM]

    with c.stage() as block:
        @block.gpsimd
        def _(pool):
            with pool.Fori(0, XH) as it:
                pool.wait_ge(s["weighed_s"], it + PRIMED)
                two = bass.ds(it * 2, 2)
                nc.gpsimd.tensor_copy(qh, q[:, two, :]).then_inc(s["staged"], 1)
                nc.gpsimd.tensor_copy(vh, kv_rows[:, :, bass.ds(it * 2 * P + D, 2 * P)]).then_inc(s["staged"], 1)
                nc.gpsimd.tensor_copy(svh, s_v[:, :, bass.ds(it * 2 * P, 2 * P)]).then_inc(s["staged"], 1)

        @block.tensor
        def _(pe):
            with pe.Fori(0, XH) as it:
                def keys(t, kk):
                    return t[:, bass.ds(it * 2 + kk, 1), :].rearrange("p o n -> p (o n)")
                pe.wait_ge(s["staged"], it * 3 + 3)
                for i in range(QT):
                    for kk in range(2):
                        last = nc.tensor.matmul(zp[:, i, :], qh[:, kk, i * P:(i + 1) * P], keys(kv, kk),
                                                start=kk == 0 and i % 2 == 0, stop=kk == 1, skip_group_check=True)
                last.then_inc(s["scored"], 1)
                pe.wait_ge(s["o_copied"], it * 4 + PRIMED)
                for kk in range(2):
                    last = nc.tensor.matmul(zsamp, qh[:, kk, SEQ:T], keys(s_kt, kk), start=kk == 0, stop=kk == 1)
                last.then_inc(s["scored_s"], 1)
                pe.wait_ge(s["scaled"], it * (QT + 1) + QT + 1)
                for m in range(MT):
                    for i in range(QT):
                        last = nc.tensor.transpose(c.psum[:, 3 + m, i * P:(i + 1) * P], prob[:, i, m * P:(m + 1) * P], c.ident[:])
                last.then_inc(s["turned"], 1)
                for m in range(MT):
                    last = nc.tensor.transpose(c.psum[:, 5, m * DEC:(m + 1) * DEC], prob_s[0:DEC, m * P:(m + 1) * P], c.ident[0:DEC, 0:DEC])
                last.then_inc(s["turned_s"], 1)
                pe.wait_ge(s["copied"], it * 2 + 2)
                for e in range(2):
                    for m in range(MT):
                        last = nc.tensor.matmul(c.psum[:, 6 + e, :], vh[:, m, e * P:(e + 1) * P], prob_t[:, m, :],
                                                start=m == 0, stop=m == MT - 1)
                    last.then_inc(s["weighed"], 1)
                pe.wait_ge(s["copied_s"], it + 1)
                for e in range(2):
                    for m in range(MT):
                        last = nc.tensor.matmul(c.psum[:, 2, e * DEC:(e + 1) * DEC], svh[:, m, e * P:(e + 1) * P], prob_ts[:, m, :],
                                                start=m == 0 and e == 0, stop=m == MT - 1, skip_group_check=True)
                last.then_inc(s["weighed_s"], 1)

        @block.vector
        def _(dve):
            with dve.Fori(0, XH) as it:
                dve.wait_ge(s["scored"], it + 1)
                nc.vector.tensor_reduce(neg_max[:, 0:QT], zp, AX_X, ALU.max, negate=True).then_inc(s["maxed"], 1)
                dve.wait_ge(s["scored_s"], it + 1)
                nc.vector.tensor_reduce(neg_max[0:DEC, QT:QT + 1], zsamp, AX_X, ALU.max, negate=True).then_inc(s["maxed"], 1)
                dve.wait_ge(s["exped"], it * (QT + 1) + QT + 1)
                nc.vector.reciprocal(inverse[:, 0:QT], total[:, 0:QT]).then_inc(s["inverted"], 1)
                nc.vector.reciprocal(inverse[0:DEC, QT:QT + 1], total[0:DEC, QT:QT + 1]).then_inc(s["inverted"], 1)
                dve.wait_ge(s["inverted"], it * 2 + 2)
                for i in range(QT):
                    nc.vector.tensor_scalar(prob[:, i, :], prob[:, i, :], inverse[:, i:i + 1], None, ALU.mult).then_inc(s["scaled"], 1)
                nc.vector.tensor_scalar(prob_s[0:DEC, :], prob_s[0:DEC, :], inverse[0:DEC, QT:QT + 1], None, ALU.mult).then_inc(s["scaled"], 1)
                dve.wait_ge(s["turned"], it + 1)
                nc.vector.tensor_copy(prob_t[:, 0, :], c.psum[:, 3, :]).then_inc(s["copied"], 1)
                dve.wait_ge(s["weighed"], it * 2 + 2)
                nc.vector.tensor_scalar(o[:, bass.ds(it * 2, 1), 0:SEQ].rearrange("p o t -> p (o t)"), c.psum[:, 6, :], 1.0, None, ALU.mult).then_inc(s["o_copied"], 1)
                dve.wait_ge(s["weighed_s"], it + 1 + PRIMED)
                nc.vector.tensor_scalar(o[:, bass.ds(it * 2, 2), SEQ:T], c.psum[:, 2, 0:2 * DEC].rearrange("p (e t) -> p e t", e=2), 1.0, None, ALU.mult).then_inc(s["o_copied"], 2)

        @block.scalar
        def _(act):
            with act.Fori(0, XH) as it:
                act.wait_ge(s["maxed"], it * 2 + 2)
                for i in range(QT):
                    nc.scalar.activation(prob[:, i, :], zp[:, i, :], ACT.Exp, bias=neg_max[:, i:i + 1],
                                         accum_out=total[:, i:i + 1]).then_inc(s["exped"], 1)
                nc.scalar.activation(prob_s[0:DEC, :], zsamp, ACT.Exp, bias=neg_max[0:DEC, QT:QT + 1],
                                     accum_out=total[0:DEC, QT:QT + 1]).then_inc(s["exped"], 1)
                act.wait_ge(s["turned"], it + 1)
                nc.scalar.copy(prob_t[:, 1, :], c.psum[:, 4, :]).then_inc(s["copied"], 1)
                act.wait_ge(s["turned_s"], it + 1)
                nc.scalar.copy(prob_ts, c.psum[:, 5, 0:MT * DEC].rearrange("p (m t) -> p m t", m=MT)).then_inc(s["copied_s"], 1)
                act.wait_ge(s["weighed"], it * 2 + 2)
                nc.scalar.copy(o[:, bass.ds(it * 2 + 1, 1), 0:SEQ].rearrange("p o t -> p (o t)"), c.psum[:, 7, :]).then_inc(s["o_copied"], 1)


def sample_memory(c, name, layer, rows, s_kt):
    nc = c.nc
    landed, turned, copied = c.sem(name + "_landed"), c.sem(name + "_turned"), c.sem(name + "_copied")
    with c.stage() as block:
        @block.scalar
        def _(act):
            for i, src in enumerate(("cache_mem_k", "cache_mem_v")):
                act.dma_start(rows[i], c.ins[src][layer, 0].rearrange("(m p) h d -> p m (h d)", p=P)).then_inc(landed, 16)

        @block.tensor
        def _(pe):
            pe.wait_ge(landed, 32)
            for i in range(KT // 2):
                for j in range(2):
                    for m in range(2):
                        f = 2 * i + j
                        last = nc.tensor.transpose(c.psum[:, i, j * NMEM + m * P:j * NMEM + (m + 1) * P],
                                                   rows[0][:, m, f * P:(f + 1) * P], c.ident[:])
                last.then_inc(turned, 1)

        @block.vector
        def _(dve):
            for i in range(KT // 2):
                dve.wait_ge(turned, i + 1)
                nc.vector.tensor_copy(s_kt[:, 2 * i:2 * i + 2, :], c.psum[:, i, :].rearrange("p (j n) -> p j n", j=2)).then_inc(copied, 1)
            dve.wait_ge(copied, KT // 2)


def gate_and_up(c, name, job, nxt, hidden, gated):
    nc, base = c.nc, c.rounds
    with c.stage() as block:
        @block.sync
        def _(sp):
            stream_weights(c, sp, job, nxt)

        @block.tensor
        def _(pe):
            multiply_units(c, pe, job)

        @block.scalar
        def _(act):
            with act.Fori(0, job.iters) as it:
                for i in range(2):
                    act.wait_ge(c.unit_done[2 * i], it + base + 1)
                    act.wait_ge(c.slot_emptied[2 * i + 1], it + c.emptied[2 * i + 1])
                    nc.scalar.activation(gated[:, i, :].rearrange("p (a b) -> p a b", a=2), c.psum[:, 4 * i:4 * i + 2, 0:HALF],
                                         ACT.Silu).then_inc(c.slot_emptied[2 * i], 1)

        @block.vector
        def _(dve):
            with dve.Fori(0, job.iters) as it:
                for i in range(2):
                    dve.wait_ge(c.slot_emptied[2 * i], it + c.emptied[2 * i] + 1)
                    dve.wait_ge(c.unit_done[2 * i + 1], it + base + 1)
                    nc.vector.tensor_tensor(halves(hidden[:, bass.ds(it * 2 + i, 1), :]), c.psum[:, 4 * i + 2:4 * i + 4, 0:HALF],
                                            gated[:, i, :].rearrange("p (a b) -> p a b", a=2), ALU.mult).then_inc(c.slot_emptied[2 * i + 1], 1)
    for q in range(RING):
        c.emptied[q] += job.iters
    c.rounds += job.iters


def token_shift(c, h, xx, mixes):
    nc = c.nc
    shift_rows = c.flat(9, 2 * P)[0:KT, :].rearrange("p (i n) -> p i n", i=2)
    shifted, mixed = c.sem("tokens_shifted"), c.sem("tokens_mixed")
    turned, copied, stored = c.sem("shift_turned"), c.sem("shift_copied"), c.sem("shift_stored")
    with c.stage() as block:
        @block.vector
        def _(dve):
            nc.vector.tensor_tensor(xx[:, 0:5, 1:T], h[:, 0:5, 0:T - 1], h[:, 0:5, 1:T], ALU.subtract).then_inc(shifted, 1)
            dve.wait_ge(shifted, 2)
            nc.vector.tensor_scalar(xx[:, :, 0:1], h[:, :, 0:1], -1.0, None, ALU.mult).then_inc(shifted, 1)
            nc.vector.tensor_tensor(xx[:, :, SEQ:SEQ + 1], c.vec["state_rwkv_shift"].rearrange("p (k o) -> p k o", o=1),
                                    h[:, :, SEQ:SEQ + 1], ALU.subtract).then_inc(shifted, 1)
            dve.wait_ge(shifted, 4)
            for m, out in mixes:
                mix_tokens(c, h, xx, m, out, mixed)
            dve.wait_ge(mixed, KT * len(mixes))

        @block.gpsimd
        def _(pool):
            nc.gpsimd.tensor_tensor(xx[:, 5:KT, 1:T], h[:, 5:KT, 0:T - 1], h[:, 5:KT, 1:T], ALU.subtract).then_inc(shifted, 1)

        @block.tensor
        def _(pe):
            for i, t in enumerate((SEQ - 1, T - 1)):
                last = nc.tensor.transpose(c.psum[0:KT, 0, i * P:(i + 1) * P], h[:, :, t], c.ident[:])
            last.then_inc(turned, 1)

        @block.scalar
        def _(act):
            act.wait_ge(turned, 1)
            nc.scalar.copy(shift_rows, c.psum[0:KT, 0, 0:2 * P].rearrange("p (i n) -> p i n", i=2)).then_inc(copied, 1)

        @block.sync
        def _(sp):
            sp.wait_ge(copied, 1)
            for i, out in enumerate(("prompt_rwkv_shift", "sample_rwkv_shift")):
                sp.dma_start(c.outs[out].rearrange("l b (k p) -> (l b k) p", p=P), shift_rows[:, i, :]).then_inc(stored, 16)
            sp.wait_ge(stored, 32)


def mix_tokens(c, h, xx, m, out, done):
    mu = c.vec["rw_mu"]
    for k in range(KT):
        c.nc.vector.scalar_tensor_tensor(out=out[:, k, :], in0=xx[:, k, :], scalar=mu[:, m * KT + k:m * KT + k + 1],
                                         in1=h[:, k, :], op0=ALU.mult, op1=ALU.add).then_inc(done, 1)


def key_norms(c, k, inv):
    nc = c.nc
    s = {x: c.sem("key_" + x, primed=x in ("summed", "bounded")) for x in ("squared", "summed", "bounded", "rooted", "inverted")}
    sq = c.ring_words()[:, 0:T]
    pv = c.psum[:, 0:2, 0:HALF]
    with c.stage() as block:
        @block.scalar
        def _(act):
            with act.Fori(0, PAIRS) as it:
                act.wait_ge(s["summed"], it + PRIMED)
                nc.scalar.activation(sq, k[:, bass.ds(it, 1), :].rearrange("p o t -> p (o t)"), ACT.Square,
                                     scale=c.vec["rw_k_k"][:, bass.ds(it, 1)]).then_inc(s["squared"], 1)
            act.wait_ge(s["bounded"], PAIRS + PRIMED)
            for p in range(PAIRS):
                nc.scalar.activation(inv[:, p, :], inv[:, p, :], ACT.Sqrt).then_inc(s["rooted"], 1)

        @block.tensor
        def _(pe):
            with pe.Fori(0, PAIRS) as it:
                pe.wait_ge(s["squared"], it + 1)
                pe.wait_ge(s["bounded"], it + PRIMED)
                for b in range(2):
                    last = nc.tensor.matmul(c.psum[:, b, 0:HALF], c.head_ones[:], sq[:, b * HALF:(b + 1) * HALF], start=True, stop=True)
                last.then_inc(s["summed"], 1)

        @block.vector
        def _(dve):
            with dve.Fori(0, PAIRS) as it:
                dve.wait_ge(s["summed"], it + 1 + PRIMED)
                nc.vector.tensor_scalar(halves(inv[:, bass.ds(it, 1), :]), pv, 1e-24, None, ALU.max).then_inc(s["bounded"], 1)
            for p in range(PAIRS):
                dve.wait_ge(s["rooted"], p + 1)
                nc.vector.reciprocal(inv[:, p, :], inv[:, p, :]).then_inc(s["inverted"], 1)
            dve.wait_ge(s["inverted"], PAIRS)


def decay_factors(c, r, k, v, sw, a, inv, a_out, b_out, scratch):
    nc = c.nc
    c.chunk_decay = c.tile("chunk_decay", [P, PAIRS, SEQ // L + 1])
    c.one_minus_ka = c.tile("one_minus_ka", [P, KT])
    goes_on, logw, cum, cum_prev, e_cum, e_prev = (c.flat(scratch, T, at=(2 + i) * T) for i in range(6))
    kk, kka, kmul, kmod, rk, e_neg = (c.ring_words()[:, i * T:(i + 1) * T] for i in range(6))
    s = {x: c.sem("decay_" + x, primed=x in ("done_v", "done_p")) for x in ("ready", "log", "cum", "prev", "e_cum", "e_prev", "e_neg", "kk", "kka",
                                          "kmul", "kmod", "rk", "bonus_sum", "done_v", "done_p")}

    def tile(t, it):
        return t[:, bass.ds(it, 1), :].rearrange("p o t -> p (o t)")

    def col(name, it):
        return c.vec[name][:, bass.ds(it, 1)]
    DONE_V, DONE_P = 4, 3
    with c.stage() as block:
        @block.scalar
        def _(act):
            with act.Fori(0, PAIRS) as it:
                act.wait_ge(s["done_v"], it * DONE_V + PRIMED)
                act.wait_ge(s["done_p"], it * DONE_P + PRIMED)
                nc.scalar.activation(logw, tile(sw, it), ACT.Copy, scale=-float(np.exp(-0.5))).then_inc(s["log"], 1)
                act.wait_ge(s["cum"], it + 1)
                nc.scalar.activation(e_neg, cum, ACT.Exp, scale=-1.0).then_inc(s["e_neg"], 1)
                nc.scalar.activation(e_cum, cum, ACT.Exp).then_inc(s["e_cum"], 1)
                act.wait_ge(s["prev"], it + 1)
                nc.scalar.activation(e_prev, cum_prev, ACT.Exp).then_inc(s["e_prev"], 1)
                act.wait_ge(s["e_cum"], it + 1)
                ends = e_cum[:, 0:SEQ].rearrange("p (n l) -> p n l", l=L)[:, :, L - 1]
                nc.scalar.copy(c.chunk_decay[:, bass.ds(it, 1), 0:SEQ // L].rearrange("p o n -> p (o n)"), ends).then_inc(s["done_v"], 1)
                nc.scalar.copy(c.chunk_decay[:, bass.ds(it, 1), SEQ // L:].rearrange("p o n -> p (o n)"), e_cum[:, T - 1:T]).then_inc(s["done_v"], 1)

        @block.gpsimd
        def _(pool):
            nc.gpsimd.memset(goes_on, 1.0).then_inc(s["ready"], 1)
            pool.wait_ge(s["ready"], 1)
            nc.gpsimd.memset(goes_on.rearrange("p (n l) -> p n l", l=DEC)[:, 0::2, 0], 0.0).then_inc(s["ready"], 1)
            with pool.Fori(0, PAIRS) as it:
                pool.wait_ge(s["log"], it + 1)
                pool.wait_ge(s["cum"], it + 1)
                nc.gpsimd.tensor_tensor(cum_prev, cum, logw, ALU.subtract).then_inc(s["prev"], 1)
                pool.wait_ge(s["kk"], it + 1)
                nc.gpsimd.tensor_tensor(kka, kk, tile(a, it), ALU.mult).then_inc(s["kka"], 1)
                pool.wait_ge(s["kka"], it + 1)
                pool.wait_ge(s["e_neg"], it + 1)
                nc.gpsimd.tensor_tensor(tile(b_out, it), kka, e_neg, ALU.mult).then_inc(s["done_p"], 1)
                pool.wait_ge(s["kmod"], it + 1)
                nc.gpsimd.tensor_tensor(tile(k, it), kmod, e_neg, ALU.mult).then_inc(s["done_p"], 1)
                pool.wait_ge(s["rk"], it + 1)
                pool.wait_ge(s["e_cum"], it + 1)
                nc.gpsimd.tensor_tensor(tile(r, it), tile(r, it), e_cum, ALU.mult).then_inc(s["done_p"], 1)

        @block.tensor
        def _(pe):
            with pe.Fori(0, PAIRS) as it:
                pe.wait_ge(s["rk"], it + 1)
                pe.wait_ge(s["done_v"], it * DONE_V + PRIMED)
                for b in range(2):
                    last = nc.tensor.matmul(c.psum[:, b, 0:HALF], c.head_ones[:], rk[:, b * HALF:(b + 1) * HALF], start=True, stop=True)
                last.then_inc(s["bonus_sum"], 1)

        @block.vector
        def _(dve):
            dve.wait_ge(s["ready"], 2)
            nc.vector.tensor_scalar(c.one_minus_ka[:], c.vec["rw_k_a"], -1.0, 1.0, ALU.mult, ALU.add).then_inc(s["ready"], 1)
            dve.wait_ge(s["ready"], 3)
            with dve.Fori(0, PAIRS) as it:
                dve.wait_ge(s["done_v"], it * DONE_V + PRIMED)
                dve.wait_ge(s["done_p"], it * DONE_P + PRIMED)
                nc.vector.scalar_tensor_tensor(out=kk, in0=tile(k, it), scalar=col("rw_k_k", it), in1=tile(inv, it),
                                               op0=ALU.mult, op1=ALU.mult).then_inc(s["kk"], 1)
                nc.vector.tensor_scalar(kmul, tile(a, it), col("rw_k_a", it), c.one_minus_ka[:, bass.ds(it, 1)],
                                        ALU.mult, ALU.add).then_inc(s["kmul"], 1)
                dve.wait_ge(s["log"], it + 1)
                nc.vector.tensor_tensor_scan(cum, goes_on, logw, 0.0, ALU.mult, ALU.add).then_inc(s["cum"], 1)
                dve.wait_ge(s["kmul"], it + 1)
                nc.vector.tensor_tensor(kmod, tile(k, it), kmul, ALU.mult).then_inc(s["kmod"], 1)
                dve.wait_ge(s["kmod"], it + 1)
                nc.vector.scalar_tensor_tensor(out=rk, in0=tile(r, it), scalar=col("rw_r_k", it), in1=kmod,
                                               op0=ALU.mult, op1=ALU.mult).then_inc(s["rk"], 1)
                dve.wait_ge(s["e_prev"], it + 1)
                dve.wait_ge(s["kk"], it + 1)
                nc.vector.scalar_tensor_tensor(out=tile(a_out, it), in0=kk, scalar=-1.0, in1=e_prev,
                                               op0=ALU.mult, op1=ALU.mult).then_inc(s["done_v"], 1)
                dve.wait_ge(s["bonus_sum"], it + 1)
                nc.vector.tensor_tensor(halves(inv[:, bass.ds(it, 1), :]), c.psum[:, 0:2, 0:HALF], halves(v[:, bass.ds(it, 1), :]),
                                        ALU.mult).then_inc(s["done_v"], 1)


class Quad:

    def __init__(self, spaces, tail):
        n = 4 * P
        buf = [w[:, i * n:(i + 1) * n].rearrange("p (j n) -> p j n", j=4)
               for w in spaces for i in range(w.shape[-1] // n)]
        (self.A, self.B, self.K, self.V, self.m16t, self.m16, self.to32, self.to64, self.q, self.ak,
         self.rbk, self.A_rows, self.B_rows, self.K_rows, self.V_rows, self.mv) = buf[0:16]
        self.R = tail.rearrange("p (j n) -> p j n", j=4)
        self.m2, self.m2t, self.m4, self.m4t, self.m8 = self.A, self.B, self.K, self.V, self.ak
        self.x, self.turned = self.m16, self.m16t
        self.Pa, self.U0, self.phi, self.Rh = self.A, self.B, self.K, self.mv[:, :, 0:L]


def wkv(c, quads, states, finals, A, B, R, K, V, y, sample):
    nc = c.nc
    n_it = 1 if sample else PAIRS
    names = ("zeroed ready_v ready_s ready_p ab_done am_done ak_done rbk_done am_copied m16t_ready m16_ready joins_ready "
             "ak_ready rbk_ready q0_ready rowsA_done rowsB_done rowsK_done rowsV_done rowsA rowsB rowsK rowsV m2_done m2_ready m2t_done m2t_ready "
             "mv_done mv_ready q_done q_ready m4_done m4_ready m4t_done m4t_ready m8_done m8_ready x_done x_ready "
             "turned_done turned_ready pa_done pa_ready u_done u_ready rh_done rh_ready phi_done phi_ready "
             "s_done s_ready y_done y_ready").split()
    s = [{x: c.sem(f"wkv{q}_{x}", primed=x in ("y_done", "s_ready", "y_ready")) for x in names} for q in range(2)]
    rows64 = [slice(0, HD), slice(HD, P)]

    def bank(q, b):
        return c.psum[:, 4 * q + b, :].rearrange("p (j n) -> p j n", j=4)

    def tokens(t, it, q, rows):
        if sample:
            return t[rows, 4 * q:4 * q + 4, SEQ:T]
        return t[rows, bass.ds(it, 1), q * 4 * L:(q + 1) * 4 * L].rearrange("p o (j n) -> p (o j) n", j=4)
    W = DEC if sample else L

    def loop(eng, body):
        if sample:
            body(0)
        else:
            with eng.Fori(0, n_it) as it:
                body(it)

    with c.stage() as block:
        @block.gpsimd
        def _(pool):
            for q in range(2):
                for t in (quads[q].A, quads[q].B, quads[q].K, quads[q].V, quads[q].R):
                    nc.gpsimd.memset(t, 0.0).then_inc(s[q]["zeroed"], 1)
            if not sample:
                nc.gpsimd.memset(states[:, 0, :], 0.0).then_inc(s[0]["zeroed"], 1)
            pool.wait_ge(s[0]["zeroed"], 5 if sample else 6)
            pool.wait_ge(s[1]["zeroed"], 5)

            def body(it):
                for q in range(2):
                    z = quads[q]
                    pool.wait_ge(s[q]["y_done"], it + PRIMED)
                    nc.gpsimd.tensor_copy(z.R[:, :, 0:W], tokens(R, it, q, slice(0, P))).then_inc(s[q]["ready_p"], 1)
                for q in range(2):
                    z = quads[q]
                    pool.wait_ge(s[q]["m16t_ready"], it + 1)
                    nc.gpsimd.tensor_tensor(z.q, z.m16t, c.ident[:].rearrange("p (o n) -> p o n", o=1).broadcast_to([P, 4, P]), ALU.add).then_inc(s[q]["q0_ready"], 1)
                for q in range(2):
                    z = quads[q]
                    pool.wait_ge(s[q]["am_copied"], it + 1)
                    nc.gpsimd.tensor_tensor(z.to64, z.to32, c.to64_lo[:].rearrange("p (o n) -> p o n", o=1).broadcast_to([P, 4, P]), ALU.mult).then_inc(s[q]["joins_ready"], 1)
                    pool.wait_ge(s[q]["joins_ready"], it * 2 + 1)
                    nc.gpsimd.tensor_tensor(z.to32, z.to32, c.to32_lo[:].rearrange("p (o n) -> p o n", o=1).broadcast_to([P, 4, P]), ALU.mult).then_inc(s[q]["joins_ready"], 1)
            loop(pool, body)

        @block.vector
        def _(dve):
            def spread(m, n=P):
                return m[:].rearrange("p (o n) -> p o n", o=1).broadcast_to([P, 4, n])

            def body(it):
                for q in range(2):
                    z, e = quads[q], s[q]
                    dve.wait_ge(e["zeroed"], 5)
                    dve.wait_ge(e["y_done"], it + PRIMED)
                    for src, dst in ((A, z.A), (B, z.B)):
                        for h, r in enumerate(rows64):
                            nc.vector.tensor_scalar(dst[r, :, h * L:h * L + W], tokens(src, it, q, r), 1.0, None, ALU.mult).then_inc(e["ready_v"], 1)
                for q in range(2):
                    z, e = quads[q], s[q]
                    dve.wait_ge(e["ab_done"], it + 1)
                    nc.vector.tensor_tensor(z.m16t, bank(q, 0), spread(c.in16_up), ALU.mult).then_inc(e["m16t_ready"], 1)
                    dve.wait_ge(e["am_done"], it + 1)
                    dve.wait_ge(e["am_copied"], it + 1)
                    nc.vector.tensor_tensor(z.m16, bank(q, 1), spread(c.in16_lo), ALU.mult).then_inc(e["m16_ready"], 1)
                    dve.wait_ge(e["ak_done"], it + 1)
                    nc.vector.tensor_tensor(z.ak, bank(q, 2), spread(c.strict_up), ALU.mult).then_inc(e["ak_ready"], 1)
                    dve.wait_ge(e["rbk_done"], it + 1)
                    nc.vector.tensor_tensor(z.rbk.rearrange("p j (u n) -> p (j u) n", u=2), bank(q, 3).rearrange("p j (u n) -> p (j u) n", u=2),
                                            c.incl_up[:].rearrange("p (o n) -> p o n", o=1).broadcast_to([P, 8, L]), ALU.mult).then_inc(e["rbk_ready"], 1)
                for q in range(2):
                    z, e = quads[q], s[q]
                    dve.wait_ge(e["rowsK_done"], it + 1)
                    nc.vector.tensor_copy(z.K_rows, bank(q, 2)).then_inc(e["rowsK"], 1)
                for q in range(2):
                    z, e = quads[q], s[q]
                    dve.wait_ge(e["m2_done"], it + 1)
                    nc.vector.tensor_copy(z.m2, bank(q, 0)).then_inc(e["m2_ready"], 1)

                def add_q(step):
                    for q in range(2):
                        z, e = quads[q], s[q]
                        dve.wait_ge(e["q0_ready"], it + 1)
                        dve.wait_ge(e["q_done"], it * 5 + step)
                        nc.vector.tensor_tensor(z.q, bank(q, 3), z.q, ALU.add).then_inc(e["q_ready"], 1)
                add_q(1)
                for q in range(2):
                    z, e = quads[q], s[q]
                    dve.wait_ge(e["m4t_done"], it + 1)
                    nc.vector.tensor_copy(z.m4t, bank(q, 1)).then_inc(e["m4t_ready"], 1)
                add_q(2)
                add_q(3)
                for join in range(2):
                    for q in range(2):
                        z, e = quads[q], s[q]
                        dve.wait_ge(e["turned_done"], it * 2 + join + 1)
                        nc.vector.tensor_copy(z.turned, bank(q, 1)).then_inc(e["turned_ready"], 1)
                    add_q(4 + join)
                for q in range(2):
                    z, e = quads[q], s[q]
                    dve.wait_ge(e["u_done"], it + 1)
                    nc.vector.tensor_copy(z.U0, bank(q, 1)).then_inc(e["u_ready"], 1)
                for q in range(2):
                    z, e = quads[q], s[q]
                    dve.wait_ge(e["phi_done"], it + 1)
                    nc.vector.tensor_tensor(z.phi, bank(q, 3), spread(c.ident), ALU.add).then_inc(e["phi_ready"], 1)
                    dve.wait_ge(e["rh_done"], it + 1)
                    nc.vector.tensor_tensor(z.Rh, bank(q, 2)[:, :, 0:L], z.R, ALU.add).then_inc(e["rh_ready"], 1)
                for q in range(2):
                    z, e = quads[q], s[q]
                    dve.wait_ge(e["y_done"], it + 1 + PRIMED)
                    out = tokens(y, it, q, slice(0, P))
                    nc.vector.tensor_scalar(out, bank(q, 1)[:, :, 0:W], 1.0, None, ALU.mult).then_inc(e["y_ready"], 1)
            loop(dve, body)

        @block.scalar
        def _(act):
            def body(it):
                for q in range(2):
                    z, e = quads[q], s[q]
                    act.wait_ge(e["zeroed"], 5)
                    act.wait_ge(e["y_done"], it + PRIMED)
                    for src, dst in ((K, z.K), (V, z.V)):
                        for h, r in enumerate(rows64):
                            nc.scalar.copy(dst[r, :, h * L:h * L + W], tokens(src, it, q, r)).then_inc(e["ready_s"], 1)
                for q in range(2):
                    z, e = quads[q], s[q]
                    act.wait_ge(e["am_done"], it + 1)
                    nc.scalar.copy(z.to32, bank(q, 1)).then_inc(e["am_copied"], 1)
                for q in range(2):
                    z, e = quads[q], s[q]
                    act.wait_ge(e["rowsA_done"], it + 1)
                    nc.scalar.copy(z.A_rows, bank(q, 0)).then_inc(e["rowsA"], 1)
                    act.wait_ge(e["rowsB_done"], it + 1)
                    nc.scalar.copy(z.B_rows, bank(q, 1)).then_inc(e["rowsB"], 1)
                    act.wait_ge(e["rowsV_done"], it + 1)
                    nc.scalar.copy(z.V_rows, bank(q, 3)).then_inc(e["rowsV"], 1)
                for q in range(2):
                    z, e = quads[q], s[q]
                    act.wait_ge(e["mv_done"], it + 1)
                    nc.scalar.copy(z.mv, bank(q, 2)).then_inc(e["mv_ready"], 1)
                    act.wait_ge(e["m2t_done"], it + 1)
                    nc.scalar.copy(z.m2t, bank(q, 1)).then_inc(e["m2t_ready"], 1)
                for q in range(2):
                    z, e = quads[q], s[q]
                    act.wait_ge(e["m4_done"], it + 1)
                    nc.scalar.copy(z.m4, bank(q, 0)).then_inc(e["m4_ready"], 1)
                for q in range(2):
                    z, e = quads[q], s[q]
                    act.wait_ge(e["m8_done"], it + 1)
                    nc.scalar.copy(z.m8, bank(q, 0)).then_inc(e["m8_ready"], 1)
                for join in range(2):
                    for q in range(2):
                        z, e = quads[q], s[q]
                        act.wait_ge(e["x_done"], it * 2 + join + 1)
                        nc.scalar.copy(z.x, bank(q, 0)).then_inc(e["x_ready"], 1)
                for q in range(2):
                    z, e = quads[q], s[q]
                    act.wait_ge(e["pa_done"], it + 1)
                    nc.scalar.copy(z.Pa, bank(q, 0)).then_inc(e["pa_ready"], 1)
                for q in range(2):
                    e = s[q]
                    for j in range(4):
                        act.wait_ge(e["s_done"], it * 4 + j + 1)
                        unit = 4 * q + j
                        if sample:
                            out, decay = finals[:, unit, :], c.chunk_decay[:, unit, SEQ // L:]
                        else:
                            out = states[:, unit + 1, :] if unit < 7 else finals[:, bass.ds(it, 1), :].rearrange("p o n -> p (o n)")
                            decay = c.chunk_decay[:, bass.ds(it, 1), unit:unit + 1].rearrange("p a b -> p (a b)")
                        nc.scalar.activation(out, bank(q, 0)[:, j, :], ACT.Copy, scale=decay).then_inc(e["s_ready"], 1)
            loop(act, body)

        @block.tensor
        def _(pe):
            mm, tr = nc.tensor.matmul, nc.tensor.transpose

            def four(dst, lhs, rhs):
                for j in range(4):
                    last = mm(dst[:, j, :], lhs[:, j, :], rhs[:, j, :], start=j == 0, stop=True, skip_group_check=True)
                return last

            def turn(dst, src):
                for j in range(4):
                    last = tr(dst[:, j, :], src[:, j, :], c.ident[:])
                return last

            def body(it):
                for q in range(2):
                    z, e = quads[q], s[q]
                    pe.wait_ge(e["ready_v"], it * 4 + 4)
                    pe.wait_ge(e["s_ready"], it * 4 + PRIMED)
                    pe.wait_ge(e["y_ready"], it + PRIMED)
                    four(bank(q, 0), z.B, z.A).then_inc(e["ab_done"], 1)
                    four(bank(q, 1), z.A, z.B).then_inc(e["am_done"], 1)
                    pe.wait_ge(e["ready_s"], it * 4 + 4)
                    pe.wait_ge(e["ready_p"], it + 1)
                    four(bank(q, 2), z.K, z.A).then_inc(e["ak_done"], 1)
                    for j in range(4):
                        mm(bank(q, 3)[:, j, 0:L], z.B[:, j, :], z.R[:, j, :], start=j == 0, stop=True, skip_group_check=True)
                        last = mm(bank(q, 3)[:, j, L:P], z.K[:, j, :], z.R[:, j, :], start=False, stop=True, skip_group_check=True)
                    last.then_inc(e["rbk_done"], 1)
                for q in range(2):
                    z, e = quads[q], s[q]
                    pe.wait_ge(e["m16t_ready"], it + 1)
                    turn(bank(q, 0), z.A).then_inc(e["rowsA_done"], 1)
                    pe.wait_ge(e["m16_ready"], it + 1)
                    turn(bank(q, 1), z.B).then_inc(e["rowsB_done"], 1)
                    pe.wait_ge(e["ak_ready"], it + 1)
                    turn(bank(q, 2), z.K).then_inc(e["rowsK_done"], 1)
                    pe.wait_ge(e["rbk_ready"], it + 1)
                    turn(bank(q, 3), z.V).then_inc(e["rowsV_done"], 1)
                for q in range(2):
                    z, e = quads[q], s[q]
                    pe.wait_ge(e["rowsA"], it + 1)
                    four(bank(q, 0), z.m16t, z.m16).then_inc(e["m2_done"], 1)
                    pe.wait_ge(e["rowsB"], it + 1)
                    four(bank(q, 1), z.m16, z.m16t).then_inc(e["m2t_done"], 1)
                    pe.wait_ge(e["rowsV"], it + 1)
                    pe.wait_ge(e["rowsK"], it + 1)
                    four(bank(q, 2), z.ak, z.V_rows).then_inc(e["mv_done"], 1)
                for q in range(2):
                    z, e = quads[q], s[q]
                    pe.wait_ge(e["m2_ready"], it + 1)
                    pe.wait_ge(e["q0_ready"], it + 1)
                    four(bank(q, 3), z.m2, z.q).then_inc(e["q_done"], 1)
                    pe.wait_ge(e["m2t_ready"], it + 1)
                    four(bank(q, 0), z.m2t, z.m2).then_inc(e["m4_done"], 1)
                    four(bank(q, 1), z.m2, z.m2t).then_inc(e["m4t_done"], 1)
                for q in range(2):
                    z, e = quads[q], s[q]
                    pe.wait_ge(e["m4_ready"], it + 1)
                    pe.wait_ge(e["q_ready"], it * 5 + 1)
                    four(bank(q, 3), z.m4, z.q).then_inc(e["q_done"], 1)
                    pe.wait_ge(e["m4t_ready"], it + 1)
                    pe.wait_ge(e["mv_ready"], it + 1)
                    four(bank(q, 0), z.m4t, z.m4).then_inc(e["m8_done"], 1)
                for q in range(2):
                    z, e = quads[q], s[q]
                    pe.wait_ge(e["m8_ready"], it + 1)
                    pe.wait_ge(e["q_ready"], it * 5 + 2)
                    four(bank(q, 3), z.m8, z.q).then_inc(e["q_done"], 1)
                for join in range(2):
                    for q in range(2):
                        z, e = quads[q], s[q]
                        pe.wait_ge(e["q_ready"], it * 5 + 3 + join)
                        pe.wait_ge(e["joins_ready"], it * 2 + 2)
                        turn(bank(q, 1), z.q).then_inc(e["turned_done"], 1)
                        four(bank(q, 0), (z.to32, z.to64)[join], z.q).then_inc(e["x_done"], 1)
                    for q in range(2):
                        z, e = quads[q], s[q]
                        pe.wait_ge(e["x_ready"], it * 2 + join + 1)
                        pe.wait_ge(e["turned_ready"], it * 2 + join + 1)
                        four(bank(q, 3), z.turned, z.x).then_inc(e["q_done"], 1)
                for q in range(2):
                    z, e = quads[q], s[q]
                    pe.wait_ge(e["q_ready"], it * 5 + 5)
                    four(bank(q, 0), z.q, z.A_rows).then_inc(e["pa_done"], 1)
                    pe.wait_ge(e["mv_ready"], it + 1)
                    four(bank(q, 1), z.q, z.mv).then_inc(e["u_done"], 1)
                for q in range(2):
                    z, e = quads[q], s[q]
                    pe.wait_ge(e["pa_ready"], it + 1)
                    four(bank(q, 3), z.Pa, z.B_rows).then_inc(e["phi_done"], 1)
                    for j in range(4):
                        last = mm(bank(q, 2)[:, j, 0:L], z.Pa[:, j, :], z.rbk[:, j, 0:L], start=j == 0, stop=True, skip_group_check=True)
                    last.then_inc(e["rh_done"], 1)
                for q in range(2):
                    z, e = quads[q], s[q]
                    pe.wait_ge(e["u_ready"], it + 1)
                    for j in range(4):
                        mm(bank(q, 0)[:, j, :], z.B_rows[:, j, :], z.U0[:, j, :], start=j == 0, stop=False, skip_group_check=True)
                        mm(bank(q, 0)[:, j, :], z.K_rows[:, j, :], z.V_rows[:, j, :], start=False, stop=False, skip_group_check=True)
                for q in range(2):
                    z, e = quads[q], s[q]
                    pe.wait_ge(e["phi_ready"], it + 1)
                    for j in range(4):
                        state = states[:, 4 * q + j, :]
                        if j:
                            pe.wait_ge(e["s_ready"], it * 4 + j + PRIMED)
                        elif q and not sample:
                            pe.wait_ge(s[0]["s_ready"], it * 4 + 4 + PRIMED)
                        mm(bank(q, 0)[:, j, :], z.phi[:, j, :], state, start=False, stop=True, skip_group_check=True).then_inc(e["s_done"], 1)
                for q in range(2):
                    z, e = quads[q], s[q]
                    pe.wait_ge(e["rh_ready"], it + 1)
                    for j in range(4):
                        state = states[:, 4 * q + j, :]
                        mm(bank(q, 1)[:, j, 0:L], state, z.Rh[:, j, :], start=j == 0, stop=False, skip_group_check=True)
                        mm(bank(q, 1)[:, j, 0:L], z.U0[:, j, :], z.rbk[:, j, 0:L], start=False, stop=False, skip_group_check=True)
                        last = mm(bank(q, 1)[:, j, 0:L], z.V_rows[:, j, :], z.rbk[:, j, L:P], start=False, stop=True, skip_group_check=True)
                    last.then_inc(e["y_done"], 1)
            pe.wait_ge(s[0]["zeroed"], 5 if sample else 6)
            loop(pe, body)


def load_states(c, states, stage):
    nc = c.nc
    zeroed, landed, turned, copied = (c.sem("state_" + x) for x in ("zeroed", "landed", "turned", "copied"))
    with c.stage() as block:
        @block.gpsimd
        def _(pool):
            nc.gpsimd.memset(stage, 0.0).then_inc(zeroed, 1)

        @block.sync
        def _(sp):
            sp.wait_ge(zeroed, 1)
            heads = c.ins["state_rwkv_wkv"][0, 0].rearrange("(p h) i j -> h i p j", h=2)
            for h in range(2):
                sp.dma_start(stage[h * HD:(h + 1) * HD, :, h * HD:(h + 1) * HD], heads[h]).then_inc(landed, 16)

        @block.tensor
        def _(pe):
            pe.wait_ge(landed, 32)
            for b in range(2):
                for j in range(4):
                    last = nc.tensor.transpose(c.psum[:, b, j * P:(j + 1) * P], stage[:, 4 * b + j, :], c.ident[:])
                last.then_inc(turned, 1)

        @block.vector
        def _(dve):
            for b in range(2):
                dve.wait_ge(turned, b + 1)
                nc.vector.tensor_copy(states[:, 4 * b:4 * b + 4, :], c.psum[:, b, :].rearrange("p (j n) -> p j n", j=4)).then_inc(copied, 1)
            dve.wait_ge(copied, 2)


def store_states(c, finals, stage, out):
    nc = c.nc
    turned, copied, stored = (c.sem("final_" + x) for x in ("turned", "copied", "stored"))
    with c.stage() as block:
        @block.tensor
        def _(pe):
            for b in range(2):
                for j in range(4):
                    last = nc.tensor.transpose(c.psum[:, b, j * P:(j + 1) * P], finals[:, 4 * b + j, :], c.ident[:])
                last.then_inc(turned, 1)

        @block.vector
        def _(dve):
            for b in range(2):
                dve.wait_ge(turned, b + 1)
                nc.vector.tensor_copy(stage[:, 4 * b:4 * b + 4, :], c.psum[:, b, :].rearrange("p (j n) -> p j n", j=4)).then_inc(copied, 1)

        @block.sync
        def _(sp):
            sp.wait_ge(copied, 2)
            heads = out[0, 0].rearrange("(p h) i j -> h i p j", h=2)
            for h in range(2):
                sp.dma_start(heads[h], stage[h * HD:(h + 1) * HD, :, h * HD:(h + 1) * HD]).then_inc(stored, 16)
            sp.wait_ge(stored, 32)


def group_norm(c, y, bonus, gate, out, scratch):
    nc = c.nc
    d, d2, var, root, inv, n1, n2 = (c.flat(scratch, T, at=i * T) for i in range(7))
    s = {x: c.sem("gn_" + x, primed=x == "d") for x in ("mean", "d", "d2", "var_sum", "var", "root", "inv", "n1", "n2", "n3", "out")}
    means, sums = c.psum[:, 0:2, 0:HALF], c.psum[:, 2:4, 0:HALF]

    def tile(t, it):
        return t[:, bass.ds(it, 1), :].rearrange("p o t -> p (o t)")

    def two(ap):
        return ap.rearrange("p (a b) -> p a b", a=2)
    with c.stage() as block:
        @block.tensor
        def _(pe):
            with pe.Fori(0, PAIRS) as it:
                pe.wait_ge(s["d"], it + PRIMED)
                for b in range(2):
                    last = nc.tensor.matmul(c.psum[:, b, 0:HALF], c.head_ones[:], tile(y, it)[:, b * HALF:(b + 1) * HALF], start=True, stop=True)
                last.then_inc(s["mean"], 1)
                pe.wait_ge(s["d2"], it + 1)
                for b in range(2):
                    last = nc.tensor.matmul(c.psum[:, 2 + b, 0:HALF], c.head_ones[:], d2[:, b * HALF:(b + 1) * HALF], start=True, stop=True)
                last.then_inc(s["var_sum"], 1)

        @block.scalar
        def _(act):
            with act.Fori(0, PAIRS) as it:
                act.wait_ge(s["d"], it + 1 + PRIMED)
                nc.scalar.activation(d2, d, ACT.Square).then_inc(s["d2"], 1)
                act.wait_ge(s["var"], it + 1)
                nc.scalar.activation(root, var, ACT.Sqrt).then_inc(s["root"], 1)

        @block.vector
        def _(dve):
            with dve.Fori(0, PAIRS) as it:
                dve.wait_ge(s["mean"], it + 1)
                nc.vector.scalar_tensor_tensor(out=two(d), in0=means, scalar=-1.0 / HD, in1=halves(y[:, bass.ds(it, 1), :]),
                                               op0=ALU.mult, op1=ALU.add).then_inc(s["d"], 1)
                dve.wait_ge(s["var_sum"], it + 1)
                nc.vector.tensor_scalar(two(var), sums, 1.0 / HD, GN_EPS, ALU.mult, ALU.add).then_inc(s["var"], 1)
                dve.wait_ge(s["root"], it + 1)
                nc.vector.reciprocal(inv, root).then_inc(s["inv"], 1)
                dve.wait_ge(s["inv"], it + 1)
                nc.vector.scalar_tensor_tensor(out=n1, in0=d, scalar=c.vec["rw_lnx_w"][:, bass.ds(it, 1)], in1=inv,
                                               op0=ALU.mult, op1=ALU.mult).then_inc(s["n1"], 1)
                dve.wait_ge(s["n1"], it + 1)
                nc.vector.scalar_tensor_tensor(out=n2, in0=n1, scalar=c.vec["rw_lnx_b"][:, bass.ds(it, 1)], in1=tile(bonus, it),
                                               op0=ALU.add, op1=ALU.add).then_inc(s["n2"], 1)
                dve.wait_ge(s["n2"], it + 1)
                nc.vector.tensor_tensor(tile(out, it), n2, tile(gate, it), ALU.mult).then_inc(s["out"], 1)


def store_rows(c, name, x, stage, groups):
    nc = c.nc
    turned, copied, stored = c.sem(name + "_turned"), c.sem(name + "_copied"), c.sem(name + "_stored")
    steps = [(g, k) for g in range(len(groups)) for k in range(0, KT, 4)]
    with c.stage() as block:
        @block.tensor
        def _(pe):
            for i, (g, k) in enumerate(steps):
                t0, n, _ = groups[g]
                if i >= 4:
                    pe.wait_ge(copied, i - 3)
                for j in range(4):
                    last = nc.tensor.transpose(c.psum[0:n, i % 4, j * P:(j + 1) * P], x[:, k + j, t0:t0 + n], c.ident[:])
                last.then_inc(turned, 1)

        @block.vector
        def _(dve):
            for i, (g, k) in enumerate(steps):
                n = groups[g][1]
                dve.wait_ge(turned, i + 1)
                nc.vector.tensor_copy(stage[0:n, g, k * P:(k + 4) * P], c.psum[0:n, i % 4, :]).then_inc(copied, 1)

        @block.sync
        def _(sp):
            for g, (_, n, out) in enumerate(groups):
                sp.wait_ge(copied, 2 * g + 2)
                sp.dma_start(out, stage[0:n, g, :]).then_inc(stored, 16)
            sp.wait_ge(stored, 16 * len(groups))


def build(nc, ins, outs):
    with ExitStack() as ctx:
        c = Core(nc, ctx, ins, outs)
        x, h = c.region(0), c.region(1)
        xm = c.region(7, t=NMEM)
        mn = c.region(8, t=NMEM)
        qkv = [c.region(2), c.region(3), c.region(4)]
        hidden = c.region(2, k=FT)
        kv = c.region(3, k=2 * KT, t=NMEM)
        kv_rows = c.region(4, k=2, t=2 * D)
        s_rows = [c.region(5, k=2, t=D), c.region(5, k=2, t=D, at=2 * D)]
        s_kt = c.region(6, t=NMEM)
        gated = c.region(9, k=2)

        def third(i):
            return copy_to(c, qkv[i], HD ** -0.5 if i == 0 else 1.0)

        w_qkv = ins["sb_w_qkv"][0]
        stages = []

        def square_job(w, moving, out=None, scale=1.0):
            emits = add_to(c, x), {}
            if out is not None:
                emits = copy_to(c, out, scale)
            return Job(KT, KT, columns(w), lambda s: moving), emits

        def kv_job(layer):
            job = Job(2 * KT, KT, columns(ins["xa_w_kv"][layer]), lambda s: mn, tokens=NMEM)
            return job, copy_to(c, kv)

        def up_job(layer):
            w = ins["ffn_w_gate_up"][layer].rearrange("(k p) m -> p k m", p=P)
            return Job(2 * FT, KT, lambda it, s: w[:, :, bass.ds(it * (2 * P) + (s // 2) * P + (s % 2) * FF, P)], lambda s: h)

        def down_job(layer):
            w = ins["ffn_w_down"][layer].rearrange("(k p) m -> p k m", p=P)
            ch = FT // 2
            return Job(2 * KT, ch, lambda it, s: w[:, (s % 2) * ch:(s % 2 + 1) * ch, bass.ds(it * (2 * P) + (s // 2) * P, P)],
                       lambda s: hidden[:, (s % 2) * ch:(s % 2 + 1) * ch, :], slot=lambda s: s // 2,
                       opens=lambda s: s % 2 == 0, closes=lambda s: s % 2 == 1)

        q_job = [square_job(w_qkv[:, i * D:(i + 1) * D], h, qkv[i], HD ** -0.5 if i == 0 else 1.0) for i in range(3)]
        sbo_job = square_job(ins["sb_w_o"][0], qkv[0])
        layer_jobs = []
        for layer in range(DEPTH):
            layer_jobs.append(dict(
                kv=kv_job(layer), xq=square_job(ins["xa_w_q"][layer], h, qkv[0], (D // XH) ** -0.5),
                xo=square_job(ins["xa_w_o"][layer], h), up=up_job(layer), down=down_job(layer)))

        constants(c)
        load_vectors(c)
        load_turned(c, "x", [
            (ins["x_prompt"][0], c.region(2, k=4, t=D), x[:, :, 0:SEQ]),
            (ins["x_sample"][0], c.region(3, k=1, t=D), x[:, :, SEQ:T])], D)
        with c.stage() as block:
            @block.sync
            def _(sp):
                for s in range(RING):
                    load_unit(c, sp, q_job[0][0], 0, s)

        def memory_attention(layer, nxt):
            jobs = layer_jobs[layer]
            n = f"xa{layer}"
            rms(c, n + "_norm", x, h, c.vec["norm_xattn"][:, layer * KT:])
            load_turned(c, n + "_mem", [(ins["mem_prompt"][0], c.region(6, k=2, t=D), xm)], D)
            project(c, jobs["xq"][0], jobs["kv"][0], *jobs["xq"][1])
            rms(c, n + "_mem_norm", xm, mn, c.vec["norm_mem"][:, layer * KT:], tokens=NMEM)
            project(c, jobs["kv"][0], jobs["xo"][0], *jobs["kv"][1])
            memory_rows(c, n + "_rows", layer, kv, kv_rows)
            sample_memory(c, n + "_sample", layer, s_rows, s_kt)
            cross_attention(c, n, qkv[0], kv, kv_rows, s_kt, s_rows[1], h, 7)
            project(c, jobs["xo"][0], jobs["up"], *jobs["xo"][1])
            rms(c, n + "_ffn_norm", x, h, c.vec["norm_ffn"][:, layer * KT:])
            gate_and_up(c, n, jobs["up"], jobs["down"], hidden, gated)
            project(c, jobs["down"], nxt, add_to(c, x, units=(1, 3), per=2), {})

        def lora_in_job():
            src = [ins["rw_w1"][0], ins["rw_a1"][0], ins["rw_g1"][0][:, 0:GK], ins["rw_g1"][0][:, GK:GATE]]
            src = [w.rearrange("(k p) m -> p k m", p=P) for w in src]
            mixed = [c.region(3), c.region(4), c.region(5), c.region(5)]
            outs_ = [tanh_w[0:LORA, :], a_low[0:LORA, :], gate_low[0:GK, 0, :], gate_low[0:GK, 1, :]]
            funcs = [ACT.Tanh, ACT.Copy, ACT.Sigmoid, ACT.Sigmoid]

            def emit(s):
                return lambda it, ps: nc.scalar.activation(outs_[s].rearrange("p (a b) -> p a b", a=2), ps, funcs[s])
            return (Job(RING, KT, lambda it, s: src[s], lambda s: mixed[s], m=lambda s: (LORA, LORA, GK, GK)[s]),
                    ({}, {s: emit(s) for s in range(RING)}))

        def lora_out_job(name, low, out, bias):
            def emit(s):
                def run(it, ps):
                    dst = halves(out[:, bass.ds(it * RING + s, 1), :])
                    if bias is None:
                        return nc.scalar.copy(dst, ps)
                    return nc.scalar.activation(dst, ps, ACT.Sigmoid, bias=c.vec[bias][:, bass.ds(it * RING + s, 1)])
                return run
            kt = low.shape[1]
            return (Job(KT, kt, columns(ins[name][0], kp=low.shape[0]), lambda s: low, kp=low.shape[0]),
                    ({}, {s: emit(s) for s in range(RING)}))

        gate_low = c.flat(9, 2 * T).rearrange("p (k t) -> p k t", k=2)
        tanh_w, a_low = c.flat(9, T, at=2 * T), c.flat(9, T, at=3 * T)

        def time_mix_job(w, moving, out):
            return (Job(KT, KT, columns(ins[w][0]), lambda s: moving), copy_to(c, out, vector=(), scalar=range(RING)))

        rms(c, "sb_norm", x, h, c.vec["norm_mix"])
        for i in range(3):
            nxt = q_job[i + 1][0] if i < 2 else sbo_job[0]
            project(c, q_job[i][0], nxt, *q_job[i][1])
        stick_breaking(c, *qkv, h, 5)
        o_job = Job(KT, KT, columns(ins["sb_w_o"][0]), lambda s: h)
        project(c, o_job, layer_jobs[0]["xq"][0], add_to(c, x), {})
        lora_in = lora_in_job()
        memory_attention(0, lora_in[0])
        r_out, k_out, v_out = c.region(3), c.region(4), c.region(5)
        mixes = [c.region(6), c.region(7)]
        time_mix = [time_mix_job("rw_w_r", mixes[0], r_out), time_mix_job("rw_w_k", mixes[1], k_out),
                    time_mix_job("rw_w_v", mixes[0], v_out)]
        lora_w = lora_out_job("rw_w2", tanh_w[0:LORA, :].rearrange("p (o t) -> p o t", o=1), c.region(6), "rw_w0")
        lora_a = lora_out_job("rw_a2", a_low[0:LORA, :].rearrange("p (o t) -> p o t", o=1), c.region(7), "rw_a0")
        lora_g = lora_out_job("rw_g2", gate_low[0:GK], c.region(6), None)
        xx = c.region(2)
        rms(c, "rw_norm", x, h, c.vec["norm_mix"][:, KT:])
        token_shift(c, h, xx, [(1, c.region(3)), (4, c.region(4)), (5, c.region(5))])

        def mix_ahead(m, out):
            def run(dve):
                done = c.sem(f"mixed{m}")
                mix_tokens(c, h, xx, m, out, done)
                dve.wait_ge(done, KT)
            return run
        project(c, lora_in[0], time_mix[0][0], *lora_in[1], before=mix_ahead(0, mixes[0]))
        project(c, time_mix[0][0], time_mix[1][0], *time_mix[0][1], before=mix_ahead(2, mixes[1]))
        project(c, time_mix[1][0], time_mix[2][0], *time_mix[1][1], before=mix_ahead(3, mixes[0]))
        project(c, time_mix[2][0], lora_w[0], *time_mix[2][1])
        project(c, lora_w[0], lora_a[0], *lora_w[1])
        project(c, lora_a[0], None, *lora_a[1])
        key_norms(c, k_out, c.region(8))
        A, B, bonus = c.region(1), c.region(2), c.region(8)
        decay_factors(c, r_out, k_out, v_out, c.region(6), c.region(7), bonus, A, B, 9)
        states, finals = (c.ring_words()[:, i * KT * P:(i + 1) * KT * P].rearrange("p (j n) -> p j n", j=KT) for i in range(2))
        n = 16 * 4 * P
        more = [c.flat(9, 6 * 4 * P, at=2 * T), c.ring_words()[:, 2 * KT * P:], c.tile("more_words", [P, 3 * 4 * P])[:]]
        quads = [Quad([c.flat(6, n)], c.flat(6, 4 * L, at=n)), Quad(more, c.flat(6, 4 * L, at=n + 4 * L))]
        turning = c.region(6, t=P)
        for sample in (False, True):
            if sample:
                load_states(c, states, turning)
            wkv(c, quads, states, finals, A, B, r_out, k_out, v_out, A, sample)
            store_states(c, finals, turning, outs["sample_rwkv_wkv" if sample else "prompt_rwkv_wkv"])
        with c.stage() as block:
            @block.sync
            def _(sp):
                for s in range(RING):
                    load_unit(c, sp, lora_g[0], 0, s)
        o_job = Job(KT, KT, columns(ins["rw_w_o"][0]), lambda s: r_out)
        project(c, lora_g[0], o_job, *lora_g[1])
        group_norm(c, A, bonus, c.region(6), r_out, 9)
        project(c, o_job, layer_jobs[1]["xq"][0], add_to(c, x), {})
        memory_attention(1, None)
        rms(c, "final_norm", x, h, c.vec["norm_final"])
        rows = outs["y_prompt"][0].rearrange("(g p) d -> g p d", p=P)
        store_rows(c, "y", h, c.region(2, k=5, t=D), [(g * P, P, rows[g]) for g in range(SEQ // P)] + [(SEQ, DEC, outs["y_sample"][0])])


_INS = ["x_prompt", "x_sample", "mem_prompt", "cache_sb_k", "cache_sb_v", "state_rwkv_wkv",
        "state_rwkv_shift", "cache_mem_k", "cache_mem_v", "norm_mix", "norm_xattn", "norm_ffn", "norm_mem",
        "norm_final", "sb_w_qkv", "sb_w_o", "rw_mu", "rw_w_r", "rw_w_k", "rw_w_v", "rw_w_o", "rw_w0",
        "rw_w1", "rw_w2", "rw_a0", "rw_a1", "rw_a2", "rw_g1", "rw_g2", "rw_k_k", "rw_k_a", "rw_r_k",
        "rw_lnx_w", "rw_lnx_b", "xa_w_q", "xa_w_kv", "xa_w_o", "ffn_w_gate_up", "ffn_w_down"]
_OUTS = [("y_prompt", (1, 512, 1024)), ("y_sample", (1, 32, 1024)), ("prompt_sb_k", (1, 1, 512, 16, 64)),
         ("prompt_sb_v", (1, 1, 512, 16, 64)), ("prompt_rwkv_wkv", (1, 1, 16, 64, 64)),
         ("prompt_rwkv_shift", (1, 1, 1024)), ("prompt_mem_k", (2, 1, 256, 4, 256)),
         ("prompt_mem_v", (2, 1, 256, 4, 256)), ("sample_sb_k", (1, 1, 32, 16, 64)),
         ("sample_sb_v", (1, 1, 32, 16, 64)), ("sample_rwkv_wkv", (1, 1, 16, 64, 64)),
         ("sample_rwkv_shift", (1, 1, 1024))]


def kernel(**inputs):
    import numpy as _np
    import concourse.bacc as _bacc
    from concourse import mybir as _mybir
    from concourse.bass_utils import run_bass_kernel_spmd as _run

    nc = _bacc.Bacc("TRN2", target_bir_lowering=False, num_devices=1)
    arrays, ins, outs = {}, {}, {}
    for name in _INS:
        a = _np.ascontiguousarray(inputs[name])
        arrays[f"in_{name}_dram"] = a
        ins[name] = nc.dram_tensor(f"in_{name}_dram", a.shape, _mybir.dt.from_np(a.dtype), kind="ExternalInput").ap()
    for name, shape in _OUTS:
        outs[name] = nc.dram_tensor(f"out_{name}_dram", shape, _mybir.dt.float32, kind="ExternalOutput").ap()
    build(nc, ins, outs)
    r = _run(nc, [arrays], core_ids=[0])
    return tuple(r.results[0][f"out_{name}_dram"] for name, _ in _OUTS)
```

```python
from contextlib import ExitStack, contextmanager

import numpy as np
import concourse.bass as bass
from concourse import mybir

F32 = mybir.dt.float32
F32R = mybir.dt.float32r
I32 = mybir.dt.int32
BF16 = mybir.dt.bfloat16
ALU = mybir.AluOpType
ACT = mybir.ActivationFunctionType
AX_X = mybir.AxisListType.X

P = 128
D = 1024
KT = D // P
SEQ = 512
DEC = 32
T = SEQ + DEC
HALF = T // 2
PAST = 1024
NMEM = 256
HD = 64
PAIRS = D // P
XH = 4
FF = 2816
FT = FF // P
DEPTH = 2
EPS = 1e-6
GN_EPS = 64e-5
L = 64
REGION = KT * T
RING = 4
UNIT_KT = 8
LORA = 64
GATE = 160
GK = GATE // 2
AHEAD = 2
SEMS_KEPT = 40
PRIMED = 1

ROWS_A = [("norm_mix", 16), ("norm_xattn", 16), ("norm_ffn", 16), ("norm_mem", 16), ("norm_final", 8),
          ("rw_w0", 8), ("rw_a0", 8), ("rw_k_k", 8), ("rw_k_a", 8), ("rw_r_k", 8), ("rw_lnx_w", 8), ("rw_lnx_b", 8)]
ROWS_B = [("rw_mu", 48), ("state_rwkv_shift", 8)]


class Job:

    def __init__(self, n, kt, src, moving=None, parts=None, kp=P, m=lambda u: P, slot=lambda u: u,
                 opens=lambda u: True, closes=lambda u: True, tokens=T, per=RING):
        self.n, self.src, self.moving, self.parts, self.kp, self.m = n, src, moving, parts, kp, m
        self.kt = kt if callable(kt) else lambda u: kt
        self.slot, self.opens, self.closes, self.tokens, self.per = slot, opens, closes, tokens, per
        self.iters = n // per
        self.rounds = per // RING


class Parts:

    def __init__(self, c, high, low, k=KT, t=T, high_at=0):
        self.high = c.region(high, k, t, high_at, F32R)
        self.full, self.low = c.region(low, k, t), c.region(low, k, t, dtype=F32R)


class Core:

    def __init__(self, nc, ctx, ins, outs):
        self.nc, self.ctx, self.ins, self.outs = nc, ctx, ins, outs
        self.base = self.base_of(nc)
        ctx.enter_context(nc.sbuf_tensor("arena", [P, 10 * REGION], F32))
        self.views = {}
        self.ring, self.ring_r = self.aliased("weight_ring", [P, RING, UNIT_KT, P])
        self.high, self.high_r = self.aliased("weights_high", [P, 2, UNIT_KT, P])
        self.psum = ctx.enter_context(nc.psum_tensor("psum", [P, 8, 512], F32))
        self.stages = 0
        self.stage_sems = []
        self.weights_landed = [nc.alloc_semaphore(f"weights_landed{s}") for s in range(RING)]
        self.weights_high = [nc.alloc_semaphore(f"weights_high{s}") for s in range(RING)]
        self.weights_split = [nc.alloc_semaphore(f"weights_split{s}") for s in range(RING)]
        self.splits = 0
        self.unit_done = [nc.alloc_semaphore(f"unit_done{s}") for s in range(RING)]
        self.slot_emptied = [nc.alloc_semaphore(f"slot_emptied{s}") for s in range(RING)]
        self.rounds = 0
        for sem in self.slot_emptied:
            nc.sync.sem_inc(sem, PRIMED)
        self.emptied = [PRIMED] * RING
        self.jobs = []

    @staticmethod
    def base_of(nc):
        return -(-nc.sbuf_base // 32) * 32

    def aliased(self, name, shape):
        offset = self.base_of(self.nc)
        plain = self.ctx.enter_context(self.nc.sbuf_tensor(name, shape, F32))
        return plain, self.nc.alloc_sbuf_tensor_at(name + "_r", shape, F32R, offset=offset)

    def sem(self, name, primed=False):
        self.stage_sems.append(self.nc.alloc_semaphore(f"{name}_{self.stages}"))
        if primed:
            self.nc.sync.sem_inc(self.stage_sems[-1], PRIMED)
        return self.stage_sems[-1]

    @contextmanager
    def stage(self):
        with self.nc.Block() as block:
            yield block
        if len(self.stage_sems) > SEMS_KEPT:
            self.nc.clear_and_free_semaphores(self.stage_sems)
            self.nc.all_engine_barrier()
            self.stage_sems = []
        self.stages += 1

    def tile(self, name, shape, dtype=F32):
        return self.ctx.enter_context(self.nc.sbuf_tensor(name, shape, dtype))

    def ring_words(self):
        return self.ring[:].rearrange("p s k n -> p (s k n)")

    def region(self, r, k=KT, t=T, at=0, dtype=F32):
        return self.flat(r, k * t, at, dtype).rearrange("p (k t) -> p k t", k=k)

    def flat(self, r, n, at=0, dtype=F32):
        a = r * REGION + at
        if (a, n, dtype) not in self.views:
            name = f"words_{a}_{n}" + ("_r" if dtype == F32R else "")
            self.views[a, n, dtype] = self.nc.alloc_sbuf_tensor_at(name, [P, n], dtype, offset=self.base + 4 * a, align_bytes=4)
        return self.views[a, n, dtype][:]


def take_high(c, high, full):
    return c.nc.vector.tensor_scalar(high, full, 1.0, None, ALU.mult)


def take_low(c, low, full, high):
    return c.nc.vector.tensor_tensor(low, full, high.bitcast(F32), ALU.subtract)


def split_stage(c, name, x):
    nc = c.nc
    high, low = c.sem(name + "_high"), c.sem(name + "_low")
    BY_POOL = (2, 5)
    with c.stage() as block:
        @block.scalar
        def _(act):
            for k in range(KT):
                nc.scalar.activation(x.high[:, k, :], x.full[:, k, :], ACT.Copy).then_inc(high, 1)

        @block.vector
        def _(dve):
            for k in range(KT):
                if k not in BY_POOL:
                    dve.wait_ge(high, k + 1)
                    take_low(c, x.low[:, k, :], x.full[:, k, :], x.high[:, k, :]).then_inc(low, 1)
            dve.wait_ge(low, KT)

        @block.gpsimd
        def _(pool):
            for k in BY_POOL:
                pool.wait_ge(high, k + 1)
                nc.gpsimd.tensor_tensor(x.low[:, k, :], x.full[:, k, :], x.high[:, k, :].bitcast(F32), ALU.subtract).then_inc(low, 1)


def load_unit(c, sp, job, it, u):
    s = u % RING
    sp.dma_start(c.ring[0:job.kp, s, 0:job.kt(u), 0:job.m(u)], job.src(it, u)).then_inc(c.weights_landed[s], 16)


def stream_weights(c, sp, job, nxt):
    base = c.rounds
    for u in range(RING, job.per):
        sp.wait_ge(c.unit_done[u % RING], base + u // RING)
        load_unit(c, sp, job, 0, u)
    if job.iters > 1:
        with sp.Fori(1, job.iters) as it:
            for u in range(job.per):
                sp.wait_ge(c.unit_done[u % RING], it * job.rounds + (base + u // RING))
                load_unit(c, sp, job, it, u)
    if nxt is not None:
        for u in range(RING):
            sp.wait_ge(c.unit_done[u], base + job.iters * job.rounds)
            load_unit(c, sp, nxt, 0, u)


def multiply_units(c, pe, job):
    nc, base, splits = c.nc, c.rounds, c.splits
    w = job.tokens // 2 if job.tokens > 512 else job.tokens
    units = range(job.per)
    closes = [sum(job.slot(u) == q and job.closes(u) for u in units) for q in range(RING)]
    with pe.Fori(0, job.iters) as it:
        for u in units:
            s, q = u % RING, job.slot(u)
            if job.parts:
                pe.wait_ge(c.weights_split[s], it * job.rounds + (splits + u // RING + 1))
            else:
                pe.wait_ge(c.weights_landed[s], it * (16 * job.rounds) + 16 * (base + u // RING + 1))
            if job.opens(u):
                before = sum(job.slot(v) == q and job.closes(v) for v in range(u))
                pe.wait_ge(c.slot_emptied[q], it * closes[q] + (c.emptied[q] + before))
            if job.parts:
                high, low = c.high_r[:, s % 2], c.ring_r[:, s]
                x_high, x_low = job.parts(u)
                passes = [(high, x_high), (high, x_low), (low, x_high)]
            else:
                passes = [(c.ring[0:job.kp, s, :, 0:job.m(u)], job.moving(u))]
            n = job.kt(u)
            for k in range(n):
                for h in range(job.tokens // w):
                    for i, (weights, x) in enumerate(passes):
                        last = nc.tensor.matmul(
                            c.psum[0:job.m(u), 2 * q + h, 0:w], weights[:, k, :], x[:, k, h * w:(h + 1) * w],
                            start=job.opens(u) and k == 0 and i == 0,
                            stop=job.closes(u) and k == n - 1 and i == len(passes) - 1)
            last.then_inc(c.unit_done[s], 1)


def split_unit(c, dve, job, it, u):
    s, n = u % RING, job.kt(u)
    full, low, high = c.ring[:, s, 0:n, :], c.ring_r[:, s, 0:n, :], c.high_r[:, s % 2, 0:n, :]
    dve.wait_ge(c.weights_landed[s], it * (16 * job.rounds) + 16 * (c.rounds + u // RING + 1))
    other = (s + 2) % RING
    done = it * job.rounds + (c.rounds + (u - 2 - other) // RING + 1)
    if not isinstance(done, int) or done > 0:
        dve.wait_ge(c.unit_done[other], done)
    split = it * job.rounds + (c.splits + u // RING + 1)
    take_high(c, high, full).then_inc(c.weights_high[s], 1)
    dve.wait_ge(c.weights_high[s], split)
    take_low(c, low, full, high).then_inc(c.weights_split[s], 1)


def split_and_empty(c, dve, job, emits, beside=None):
    per = job.per
    for u in range(per):
        split_unit(c, dve, job, 0, u)
        if beside is not None:
            beside(0, u)
        if u >= AHEAD and u - AHEAD in emits:
            emits[u - AHEAD](0)
    if job.iters > 1:
        with dve.Fori(1, job.iters) as it:
            for u in range(per):
                split_unit(c, dve, job, it, u)
                if beside is not None:
                    beside(it, u)
                v = u - AHEAD
                if v % per in emits:
                    emits[v % per](it if v >= 0 else it - 1)
    for u in range(per - AHEAD, per):
        if u in emits:
            emits[u](job.iters - 1)


def project(c, job, nxt, by_vector, by_scalar, beside=None):
    nc, base = c.nc, c.rounds
    wide = job.tokens > 512

    def view(u):
        q = job.slot(u)
        if wide:
            return c.psum[0:job.m(u), 2 * q:2 * q + 2, 0:HALF]
        return c.psum[0:job.m(u), 2 * q, 0:job.tokens]

    def emptying(eng, emit, u):
        def run(it):
            eng.wait_ge(c.unit_done[u % RING], it * job.rounds + (base + u // RING + 1))
            emit(it, view(u)).then_inc(c.slot_emptied[job.slot(u)], 1)
        return run

    with c.stage() as block:
        @block.sync
        def _(sp):
            stream_weights(c, sp, job, nxt)

        @block.tensor
        def _(pe):
            multiply_units(c, pe, job)

        @block.vector
        def _(dve):
            if job.parts:
                split_and_empty(c, dve, job, {u: emptying(dve, e, u) for u, e in by_vector.items()}, beside)
            elif by_vector:
                with dve.Fori(0, job.iters) as it:
                    for u in sorted(by_vector):
                        emptying(dve, by_vector[u], u)(it)
            if beside is not None and not job.parts:
                for t in range(KT):
                    beside(0, t)

        @block.scalar
        def _(act):
            if by_scalar:
                with act.Fori(0, job.iters) as it:
                    for u in sorted(by_scalar):
                        emptying(act, by_scalar[u], u)(it)
    finish(c, job, list(by_vector) + list(by_scalar))


def finish(c, job, closing):
    for u in closing:
        c.emptied[job.slot(u)] += job.iters
    c.rounds += job.iters * job.rounds
    if job.parts:
        c.splits += job.iters * job.rounds


def halves(ap):
    return ap.rearrange("p o (a b) -> p (o a) b", a=2)


def copy_to(c, dst, scale=1.0, first=0, vector=(), scalar=(0, 1, 2, 3)):
    nc = c.nc

    def emit(s, eng):
        def run(it, ps):
            out = dst[:, bass.ds(it * RING + (first + s), 1), :]
            out = halves(out) if dst.shape[-1] == T else out.rearrange("p o t -> p (o t)")
            if eng == "v":
                return nc.vector.tensor_scalar(out, ps, scale, None, ALU.mult)
            return nc.scalar.activation(out, ps, ACT.Copy, scale=scale)
        return run
    return {s: emit(s, "v") for s in vector}, {s: emit(s, "s") for s in scalar}


def add_to(c, x, units=(0, 1, 2, 3)):
    nc = c.nc

    def emit(i):
        def run(it, ps):
            out = halves(x[:, bass.ds(it * len(units) + i, 1), :])
            return nc.vector.tensor_tensor(out, ps, out, ALU.add)
        return run
    return {u: emit(i) for i, u in enumerate(units)}


def columns(w, kp=P):
    v = w.rearrange("(k p) m -> p k m", p=kp)
    return lambda it, s: v[:, :, bass.ds(it * (RING * P) + s * P, P)]


def constants(c):
    nc = c.nc
    c.ident = c.tile("ident", [P, P])
    c.ones = c.tile("ones", [P, P])
    c.head_ones = c.tile("head_ones", [P, P])
    c.later = c.tile("later", [P, P])
    c.later_r, c.neg_ones_r = c.tile("later_r", [P, P], F32R), c.tile("neg_ones_r", [P, P], F32R)
    c.in16_up = c.tile("in16_up", [P, P])
    c.in16_lo = c.tile("in16_lo", [P, P])
    c.to32_lo = c.tile("to32_lo", [P, P])
    c.to64_lo = c.tile("to64_lo", [P, P])
    c.strict_up = c.tile("strict_up", [P, P])
    c.incl_up = c.tile("incl_up", [P, L])
    c.ident_bf = c.tile("ident_bf", [P, P], BF16)
    c.barred = c.tile("barred", [P, P], BF16)
    sel = c.sem("constant_selected")
    cast = c.sem("constant_cast")
    n = [0]

    with c.stage() as block:
        @block.gpsimd
        def _(pool):
            def step(ins):
                ins.then_inc(sel, 1)
                n[0] += 1
                pool.wait_ge(sel, n[0])

            def keep(ap, pattern, op, fill, base, mult):
                step(nc.gpsimd.affine_select(out=ap, in_=ap, pattern=pattern, compare_op=op, fill=fill,
                                             base=base, channel_multiplier=mult))

            def same_block(t, w):
                v = t[:].rearrange("p (b i) -> p b i", i=w)
                keep(v, [[-w, P // w], [0, w]], ALU.is_ge, 0.0, 0, 1)
                keep(v, [[w, P // w], [0, w]], ALU.is_ge, 0.0, w - 1, -1)

            for t, v in ((c.ident, 1.0), (c.ones, 1.0), (c.head_ones, 1.0), (c.later, -1.0),
                         (c.in16_up, 1.0), (c.in16_lo, 1.0), (c.to32_lo, 1.0), (c.to64_lo, 1.0),
                         (c.strict_up, 1.0), (c.incl_up, 1.0)):
                step(nc.gpsimd.memset(t[:], v))
            keep(c.ident[:], [[-1, P]], ALU.is_equal, 0.0, 0, 1)
            same_block(c.head_ones, HD)
            keep(c.later[:], [[-1, P]], ALU.is_ge, 0.0, 0, 1)
            keep(c.in16_up[:], [[1, P]], ALU.is_gt, 0.0, 0, -1)
            same_block(c.in16_up, 16)
            keep(c.in16_lo[:], [[-1, P]], ALU.is_gt, 0.0, 0, 1)
            same_block(c.in16_lo, 16)
            for t, w in ((c.to32_lo, 32), (c.to64_lo, 64)):
                v = t[:].rearrange("p (b h i) -> p b h i", h=2, i=w // 2)
                keep(v, [[0, P // w], [-1, 2], [0, w // 2]], ALU.is_ge, 0.0, 0, 0)
                same_block(t, w)
                keep(v, [[-w, P // w], [0, 2], [0, w // 2]], ALU.is_ge, 0.0, -(w // 2), 1)
            keep(c.strict_up[:], [[1, P]], ALU.is_gt, 0.0, 0, -1)
            same_block(c.strict_up, L)
            keep(c.incl_up[0:L, :], [[1, L]], ALU.is_ge, 0.0, 0, -1)
            keep(c.incl_up[L:P, :], [[1, L]], ALU.is_ge, 0.0, 0, -1)

        @block.vector
        def _(dve):
            dve.wait_ge(sel, n[0])
            nc.vector.tensor_copy(c.ident_bf[:], c.ident[:]).then_inc(cast, 1)
            nc.vector.tensor_copy(c.later_r[:], c.later[:]).then_inc(cast, 1)
            nc.vector.tensor_scalar(c.neg_ones_r[:], c.ones[:], -1.0, None, ALU.mult).then_inc(cast, 1)
            nc.vector.tensor_scalar(c.barred[:], c.later[:], float(2 ** 100), None, ALU.mult).then_inc(cast, 1)
            dve.wait_ge(cast, 4)


def load_vectors(c):
    nc = c.nc
    stack = [c.flat(5, P), c.flat(5, P, at=P)[0:56, :]]
    c.columns = c.tile("vector_columns", [P, P + 56])
    landed, turned, copied = c.sem("vectors_landed"), c.sem("vectors_turned"), c.sem("vectors_copied")
    c.vec = {}
    n = 0
    with c.stage() as block:
        @block.scalar
        def _(act):
            nonlocal n
            for t, rows, base in ((stack[0], ROWS_A, 0), (stack[1], ROWS_B, P)):
                at = 0
                for name, k in rows:
                    src = c.ins[name]
                    dims = " ".join(f"d{i}" for i in range(len(src.shape)))
                    src = src.rearrange(f"{dims} -> ({dims})").rearrange("(k p) -> k p", p=P)
                    act.dma_start(t[at:at + k, :], src).then_inc(landed, 16)
                    c.vec[name] = c.columns[:, base + at:base + at + k]
                    at += k
                    n += 1

        @block.tensor
        def _(pe):
            pe.wait_ge(landed, 16 * n)
            nc.tensor.transpose(c.psum[:, 0, 0:P], stack[0], c.ident[:])
            nc.tensor.transpose(c.psum[:, 0, P:P + 56], stack[1], c.ident[0:56, 0:56]).then_inc(turned, 1)

        @block.vector
        def _(dve):
            dve.wait_ge(turned, 1)
            nc.vector.tensor_copy(c.columns[:], c.psum[:, 0, 0:P + 56]).then_inc(copied, 1)
            dve.wait_ge(copied, 1)


def load_turned(c, name, groups, width):
    nc = c.nc
    landed, turned, copied = c.sem(name + "_landed"), c.sem(name + "_turned"), c.sem(name + "_copied")
    steps = []
    for src, stage, dst in groups:
        n = src.shape[0]
        for m in range(max(1, n // P)):
            for k in range(0, KT, 4):
                steps.append((stage[0:min(n, P), m, :], min(n, P), m, k, dst))
    with c.stage() as block:
        @block.scalar
        def _(act):
            for src, stage, dst in groups:
                n = src.shape[0]
                p = min(n, P)
                act.dma_start(stage[0:p, 0:max(1, n // P), :], src.rearrange("(m p) d -> p m d", p=p)).then_inc(landed, 16)

        @block.tensor
        def _(pe):
            pe.wait_ge(landed, 16 * len(groups))
            for i, (st, p, m, k, dst) in enumerate(steps):
                if i >= 4:
                    pe.wait_ge(copied, i - 3)
                for j in range(4):
                    last = nc.tensor.transpose(c.psum[:, i % 4, j * P:j * P + p], st[:, (k + j) * P:(k + j + 1) * P],
                                               c.ident[0:p, 0:p])
                last.then_inc(turned, 1)

        @block.vector
        def _(dve):
            for i, (st, p, m, k, dst) in enumerate(steps):
                dve.wait_ge(turned, i + 1)
                nc.vector.tensor_copy(dst[:, k:k + 4, m * P:m * P + p],
                                      c.psum[:, i % 4, :].rearrange("p (j t) -> p j t", j=4)[:, :, 0:p]).then_inc(copied, 1)
            dve.wait_ge(copied, len(steps))


def rms(c, name, x, h, gain, tokens=T, parts=None):
    h = parts.full if parts else h
    nc = c.nc
    w = tokens // 2 if tokens > 512 else tokens
    nb = tokens // w
    sq, inv, root = c.flat(9, 4 * tokens), c.flat(9, tokens, at=4 * T), c.flat(9, tokens, at=5 * T)
    sq = sq.rearrange("p (k t) -> p k t", k=4)
    BY_VECTOR = (3, 7)
    BY_POOL = (1, 3, 5)
    squared = [c.sem(f"{name}_squared{k}") for k in range(KT)]
    meaned, rooted, inverted, scaled = (c.sem(name + x) for x in ("_meaned", "_rooted", "_inverted", "_scaled"))
    used, high, low = (c.sem(name + x) for x in ("_square_used", "_high", "_low"))
    view = c.psum[:, 0:nb, 0:w]

    def shape(ap):
        return ap.rearrange("p (a b) -> p a b", a=nb)

    nc.scalar.preload_act_table_set("sqrt_and_others")
    with c.stage() as block:
        @block.scalar
        def _(act):
            for k in range(KT):
                if k in BY_VECTOR:
                    continue
                if k >= 4:
                    act.wait_ge(used, k - 3)
                nc.scalar.activation(sq[:, k % 4, :], x[:, k, :], ACT.Square).then_inc(squared[k], 1)
            act.wait_ge(meaned, 1)
            nc.scalar.activation(root, root, ACT.Sqrt).then_inc(rooted, 1)
            if parts:
                for k in range(KT):
                    act.wait_ge(scaled, k + 1)
                    nc.scalar.activation(parts.high[:, k, :], parts.full[:, k, :], ACT.Copy).then_inc(high, 1)

        @block.tensor
        def _(pe):
            for k in range(KT):
                pe.wait_ge(squared[k], 1)
                for b in range(nb):
                    last = nc.tensor.matmul(c.psum[:, b, 0:w], c.ones[:], sq[:, k % 4, b * w:(b + 1) * w],
                                            start=k == 0, stop=k == KT - 1)
                last.then_inc(used, 1)

        @block.vector
        def _(dve):
            for k in BY_VECTOR:
                if k >= 4:
                    dve.wait_ge(used, k - 3)
                nc.vector.tensor_tensor(sq[:, k % 4, :], x[:, k, :], x[:, k, :], ALU.mult).then_inc(squared[k], 1)
            dve.wait_ge(used, KT)
            nc.vector.tensor_scalar(shape(root), view, 1.0 / D, EPS, ALU.mult, ALU.add).then_inc(meaned, 1)
            dve.wait_ge(rooted, 1)
            nc.vector.reciprocal(inv, root).then_inc(inverted, 1)
            dve.wait_ge(inverted, 1)

            def low_part(k):
                if parts and k >= 0 and k not in BY_POOL:
                    dve.wait_ge(high, k + 1)
                    take_low(c, parts.low[:, k, :], parts.full[:, k, :], parts.high[:, k, :]).then_inc(low, 1)
            for k in range(KT):
                nc.vector.scalar_tensor_tensor(out=h[:, k, :], in0=x[:, k, :], scalar=gain[:, k:k + 1], in1=inv,
                                               op0=ALU.mult, op1=ALU.mult).then_inc(scaled, 1)
                low_part(k - 2)
            low_part(KT - 2)
            low_part(KT - 1)
            dve.wait_ge(scaled, KT)
            if parts:
                dve.wait_ge(low, KT)

        @block.gpsimd
        def _(pool):
            if parts:
                for k in BY_POOL:
                    pool.wait_ge(high, k + 1)
                    nc.gpsimd.tensor_tensor(parts.low[:, k, :], parts.full[:, k, :], parts.high[:, k, :].bitcast(F32), ALU.subtract).then_inc(low, 1)


SCORE_AT = {0: 0, 1: 512, 3: 896, 2: 1024}
SCORES = 1280
KEY_TILES = SEQ // P
PAST_TILES = PAST // P
EXP_CAP = 30.0
SAMPLE_SCORES = (PAST_TILES + 1) * 2 * DEC


def stick_breaking(c, q, k, v, o, scratch):
    nc, ins, outs = c.nc, c.ins, c.outs
    at = [0]

    def part(*shape, dtype=F32):
        n = int(np.prod(shape))
        ap = c.flat(scratch, n, at=at[0], dtype=dtype)
        at[0] += n
        return ap if len(shape) == 1 else ap.rearrange("p (a b) -> p a b", a=shape[0])

    k_pair, v_pair = part(T), part(T)
    q_pad = part(2, T)
    k_rows, v_rows, k_rows_new = part(KEY_TILES, P), part(KEY_TILES, P), part(P)
    past_k = part(PAST_TILES, P)
    past_v = part(PAST_TILES + 1, P)
    past_kt = part((PAST_TILES + 1) * P)
    es = [part(SCORES), part(SCORES), part(SAMPLE_SCORES)]
    sizes, sps, lows, highs = (SCORES, SCORES, SAMPLE_SCORES), [], [], []
    for n in sizes:
        lows.append(c.flat(scratch, n, at=at[0], dtype=F32R))
        sps.append(part(n))
        highs.append(part(n, dtype=F32R))
    flat_psum = c.psum[:].rearrange("p b n -> p (b n)")
    zs = [flat_psum[:, 0:SCORES], flat_psum[:, 3 * 512:3 * 512 + SCORES], flat_psum[:, 6 * 512:6 * 512 + SAMPLE_SCORES]]

    queries_staged = c.sem("queries_staged")
    zeroed, pair_staged = c.sem("pads_zeroed"), c.sem("pair_staged")
    past_k_landed, past_v_landed = c.sem("past_k_landed"), c.sem("past_v_landed")
    rows_turned, past_turned = c.sem("rows_turned"), c.sem("past_turned", primed=True)
    k_rows_ready, v_rows_ready, new_rows_ready = c.sem("k_rows_ready"), c.sem("v_rows_ready"), c.sem("new_rows_ready")
    past_kt_lo, past_kt_hi = c.sem("past_kt_lo"), c.sem("past_kt_hi")
    rows_stored = c.sem("rows_stored", primed=True)
    scored = [c.sem(f"scored{u}", primed=True) for u in range(3)]
    capped = [c.sem(f"scores_capped{u}") for u in range(3)]
    exp_taken = [c.sem(f"exp_taken{u}") for u in range(3)]
    log_taken = [c.sem(f"log_taken{u}") for u in range(3)]
    sp_ready = [c.sem(f"softplus_ready{u}") for u in range(3)]
    sp_high = [c.sem(f"softplus_high{u}") for u in range(3)]
    sp_split = [c.sem(f"softplus_split{u}") for u in range(3)]
    summed = [c.sem(f"sums_added{u}") for u in range(3)]
    w_ready = [c.sem(f"weights_ready{u}") for u in range(3)]
    o_done, o_copied = c.sem("o_done"), c.sem("o_copied", primed=True)
    so_done, so_copied = c.sem("sample_o_done", primed=True), c.sem("sample_o_copied", primed=True)

    def rows(ap, w):
        return ap.rearrange("l b (m p) h d -> (l b m) p (h d)", p=w)

    nc.scalar.preload_act_table_set("natural_log_exp_and_others")
    with c.stage() as block:
        @block.sync
        def _(sp):
            with sp.Fori(0, PAIRS) as it:
                cols = bass.ds(it * P, P)
                sp.wait_ge(past_turned, it * 2 + PRIMED)
                sp.dma_start(past_k, rows(ins["cache_sb_k"], P).rearrange("m p n -> p m n")[:, :, cols]).then_inc(past_k_landed, 16)
                sp.wait_ge(so_done, it + PRIMED)
                sp.dma_start(past_v[:, 0:PAST_TILES, :], rows(ins["cache_sb_v"], P).rearrange("m p n -> p m n")[:, :, cols]).then_inc(past_v_landed, 16)
                sp.wait_ge(k_rows_ready, it + 1)
                sp.dma_start(rows(outs["prompt_sb_k"], P).rearrange("m p n -> p m n")[:, :, cols], k_rows).then_inc(rows_stored, 16)
                sp.wait_ge(v_rows_ready, it + 1)
                sp.dma_start(rows(outs["prompt_sb_v"], P).rearrange("m p n -> p m n")[:, :, cols], v_rows).then_inc(rows_stored, 16)
                sp.wait_ge(new_rows_ready, it * 2 + 2)
                sp.dma_start(rows(outs["sample_sb_k"], DEC).rearrange("m p n -> p m n")[:, :, cols], k_rows_new[0:DEC, :].rearrange("p (o n) -> p o n", o=1)).then_inc(rows_stored, 16)
                sp.dma_start(rows(outs["sample_sb_v"], DEC).rearrange("m p n -> p m n")[:, :, cols], past_v[0:DEC, PAST_TILES:PAST_TILES + 1, :]).then_inc(rows_stored, 16)
            sp.wait_ge(rows_stored, PAIRS * 64 + PRIMED)

        @block.gpsimd
        def _(pool):
            nc.gpsimd.memset(q_pad, 0.0).then_inc(zeroed, 1)
            nc.gpsimd.memset(past_kt[:, PAST:], 0.0).then_inc(zeroed, 1)
            nc.gpsimd.memset(past_v[:, PAST_TILES, :], 0.0).then_inc(zeroed, 1)
            pool.wait_ge(zeroed, 3)
            with pool.Fori(0, PAIRS) as it:
                for u in range(3):
                    pool.wait_ge(scored[u], it + PRIMED)
                pair = lambda x: x[:, bass.ds(it, 1), :].rearrange("p o t -> p (o t)")
                nc.gpsimd.tensor_copy(k_pair, pair(k)).then_inc(pair_staged, 1)
                nc.gpsimd.tensor_copy(v_pair, pair(v)).then_inc(pair_staged, 1)
                nc.gpsimd.tensor_copy(past_kt[:, PAST:PAST + DEC], k[:, bass.ds(it, 1), SEQ:T].rearrange("p o t -> p (o t)")).then_inc(pair_staged, 1)

        @block.tensor
        def _(pe):
            with pe.Fori(0, PAIRS) as it:
                pe.wait_ge(pair_staged, it * 3 + 3)
                pe.wait_ge(o_copied, it + PRIMED)
                for j in range(KEY_TILES):
                    last = nc.tensor.transpose(c.psum[:, 0, j * P:(j + 1) * P], k_pair[:, j * P:(j + 1) * P], c.ident[:])
                last.then_inc(rows_turned, 1)
                pe.wait_ge(so_copied, it * 2 + PRIMED)
                for j in range(KEY_TILES):
                    last = nc.tensor.transpose(c.psum[:, 1, j * P:(j + 1) * P], v_pair[:, j * P:(j + 1) * P], c.ident[:])
                last.then_inc(rows_turned, 1)
                nc.tensor.transpose(c.psum[0:DEC, 2, 0:P], k_pair[:, SEQ:T], c.ident[:])
                nc.tensor.transpose(c.psum[0:DEC, 2, P:2 * P], v_pair[:, SEQ:T], c.ident[:]).then_inc(rows_turned, 1)
                pe.wait_ge(past_k_landed, it * 16 + 16)
                for b in range(2):
                    for j in range(4):
                        last = nc.tensor.transpose(c.psum[:, 3 + b, j * P:(j + 1) * P], past_k[:, 4 * b + j, :], c.ident[:])
                    last.then_inc(past_turned, 1)
                pe.wait_ge(queries_staged, it * 2 + 2)
                for h in range(2):
                    if h == 0:
                        pe.wait_ge(k_rows_ready, it + 1)
                        pe.wait_ge(v_rows_ready, it + 1)
                        pe.wait_ge(new_rows_ready, it * 2 + 2)
                    else:
                        pe.wait_ge(past_kt_lo, it + 1)
                        pe.wait_ge(past_kt_hi, it + 1)
                    for j in (0, 1, 3, 2):
                        a = SCORE_AT[j]
                        last = nc.tensor.matmul(zs[h][:, a:a + SEQ - j * P], k_pair[:, j * P:(j + 1) * P], q_pad[:, h, j * P:SEQ],
                                                start=j != 3, stop=False, skip_group_check=True)
                        last = nc.tensor.matmul(zs[h][:, a:a + P], c.ident_bf[:], c.barred[:], start=False, stop=False, skip_group_check=True)
                    last.then_inc(scored[h], 1)
                for j in range(PAST_TILES + 1):
                    last = nc.tensor.matmul(zs[2][:, j * 2 * DEC:(j + 1) * 2 * DEC], past_kt[:, j * P:(j + 1) * P], q_pad[:, :, SEQ:T],
                                            start=j in (0, PAST_TILES), stop=False, skip_group_check=True)
                for h in range(2):
                    a = PAST_TILES * 2 * DEC + h * DEC
                    last = nc.tensor.matmul(zs[2][:, a:a + DEC], c.ident_bf[:], c.barred[:, 0:DEC], start=False, stop=False, skip_group_check=True)
                last.then_inc(scored[2], 1)
                for h in range(2):
                    pe.wait_ge(sp_split[h], it + 1)
                    for j in (0, 1, 3, 2):
                        a, n = SCORE_AT[j], SEQ - j * P
                        for x in (highs[h], lows[h]):
                            last = nc.tensor.matmul(zs[h][:, a:a + n], c.later_r[:], x[:, a:a + n], start=False,
                                                    stop=j == KEY_TILES - 1 and x is lows[h], skip_group_check=True)
                            for i in range(j + 1, KEY_TILES):
                                b, m = SCORE_AT[i], SEQ - i * P
                                last = nc.tensor.matmul(zs[h][:, a + n - m:a + n], c.neg_ones_r[:], x[:, b:b + m], start=False,
                                                        stop=i == KEY_TILES - 1 and x is lows[h], skip_group_check=True)
                    last.then_inc(summed[h], 1)
                pe.wait_ge(sp_split[2], it + 1)
                for x in (highs[2], lows[2]):
                    nc.tensor.matmul(zs[2][:, 512:], c.later_r[:], x[:, 512:], start=False, stop=x is lows[2], skip_group_check=True)
                    nc.tensor.matmul(zs[2][:, 0:512], c.later_r[:], x[:, 0:512], start=False, stop=False, skip_group_check=True)
                    for j in range(1, PAST_TILES + 1):
                        n = min(PAST_TILES, PAST_TILES + 1 - j) * 2 * DEC
                        last = nc.tensor.matmul(zs[2][:, 0:n], c.neg_ones_r[:], x[:, j * 2 * DEC:j * 2 * DEC + n], start=False,
                                                stop=j == PAST_TILES and x is lows[2], skip_group_check=True)
                last.then_inc(summed[2], 1)
                for h in range(2):
                    r = slice(h * HD, (h + 1) * HD)
                    pe.wait_ge(w_ready[h], it + 1)
                    for j in range(KEY_TILES):
                        a = SCORE_AT[j]
                        last = nc.tensor.matmul(c.psum[r, 0, j * P:SEQ], v_rows[:, j, r], es[h][:, a:a + SEQ - j * P],
                                                start=j == 0, stop=j == KEY_TILES - 1, skip_group_check=True)
                last.then_inc(o_done, 1)
                pe.wait_ge(w_ready[2], it + 1)
                pe.wait_ge(past_v_landed, it * 16 + 16)
                for j in range(PAST_TILES + 1):
                    last = nc.tensor.matmul(c.psum[:, 1, 0:2 * DEC], past_v[:, j, :], es[2][:, j * 2 * DEC:(j + 1) * 2 * DEC],
                                            start=j == 0, stop=j == PAST_TILES)
                last.then_inc(so_done, 1)

        @block.vector
        def _(dve):
            with dve.Fori(0, PAIRS) as it:
                dve.wait_ge(rows_stored, it * 64 + PRIMED)
                dve.wait_ge(rows_turned, it * 3 + 2)
                nc.vector.tensor_copy(v_rows, c.psum[:, 1, :].rearrange("p (j n) -> p j n", j=4)).then_inc(v_rows_ready, 1)
                dve.wait_ge(past_turned, it * 2 + 1 + PRIMED)
                nc.vector.tensor_copy(past_kt[:, 0:512], c.psum[:, 3, :]).then_inc(past_kt_lo, 1)
                def cap(u):
                    dve.wait_ge(scored[u], it + 1 + PRIMED)
                    nc.vector.tensor_scalar(es[u], zs[u], EXP_CAP, None, ALU.min).then_inc(capped[u], 1)

                def softplus(u):
                    dve.wait_ge(log_taken[u], it + 1)
                    nc.vector.tensor_tensor(sps[u], zs[u], es[u], ALU.max).then_inc(sp_ready[u], 1)

                def low_part(u):
                    dve.wait_ge(sp_high[u], it + 1)
                    take_low(c, lows[u], sps[u], highs[u]).then_inc(sp_split[u], 1)
                for step, u in ((cap, 0), (cap, 1), (softplus, 0), (cap, 2), (low_part, 0), (softplus, 1),
                                (low_part, 1), (softplus, 2), (low_part, 2)):
                    step(u)
                dve.wait_ge(o_done, it + 1)
                nc.vector.tensor_scalar(o[:, bass.ds(it, 1), 0:SEQ].rearrange("p o t -> p (o t)"), c.psum[:, 0, :], 1.0, None, ALU.mult).then_inc(o_copied, 1)

        @block.scalar
        def _(act):
            act.wait_ge(zeroed, 3)
            with act.Fori(0, PAIRS) as it:
                for u in range(3):
                    act.wait_ge(scored[u], it + PRIMED)
                for h in range(2):
                    r = slice(h * HD, (h + 1) * HD)
                    nc.scalar.copy(q_pad[r, h, :], q[r, bass.ds(it, 1), :].rearrange("p o t -> p (o t)")).then_inc(queries_staged, 1)
                act.wait_ge(rows_stored, it * 64 + PRIMED)
                act.wait_ge(rows_turned, it * 3 + 1)
                nc.scalar.copy(k_rows, c.psum[:, 0, :].rearrange("p (j n) -> p j n", j=4)).then_inc(k_rows_ready, 1)
                act.wait_ge(rows_turned, it * 3 + 3)
                nc.scalar.copy(k_rows_new[0:DEC, :], c.psum[0:DEC, 2, 0:P]).then_inc(new_rows_ready, 1)
                nc.scalar.copy(past_v[0:DEC, PAST_TILES, :], c.psum[0:DEC, 2, P:2 * P]).then_inc(new_rows_ready, 1)
                act.wait_ge(past_turned, it * 2 + 2 + PRIMED)
                nc.scalar.copy(past_kt[:, 512:PAST], c.psum[:, 4, :]).then_inc(past_kt_hi, 1)
                def exp(u):
                    act.wait_ge(capped[u], it + 1)
                    nc.scalar.activation(es[u], es[u], ACT.Exp).then_inc(exp_taken[u], 1)

                def log(u):
                    act.wait_ge(exp_taken[u], it + 1)
                    nc.scalar.activation(es[u], es[u], ACT.Ln, bias=1.0).then_inc(log_taken[u], 1)

                def high_part(u):
                    act.wait_ge(sp_ready[u], it + 1)
                    nc.scalar.activation(highs[u], sps[u], ACT.Copy).then_inc(sp_high[u], 1)
                for step, u in ((exp, 0), (log, 0), (exp, 1), (high_part, 0), (log, 1), (exp, 2), (high_part, 1),
                                (log, 2), (high_part, 2)):
                    step(u)
                for u in range(3):
                    act.wait_ge(summed[u], it + 1)
                    nc.scalar.activation(es[u], zs[u], ACT.Exp).then_inc(w_ready[u], 1)
                act.wait_ge(so_done, it + 1 + PRIMED)
                for h in range(2):
                    r = slice(h * HD, (h + 1) * HD)
                    nc.scalar.copy(o[r, bass.ds(it, 1), SEQ:T].rearrange("p o t -> p (o t)"),
                                   c.psum[r, 1, h * DEC:(h + 1) * DEC]).then_inc(so_copied, 1)


def memory_rows(c, name, layer, kv, k_rows_all):
    nc = c.nc
    turned, copied, stored = c.sem(name + "_turned"), c.sem(name + "_copied"), c.sem(name + "_stored")
    steps = [(m, f) for f in range(0, 2 * KT, 4) for m in range(NMEM // P)]
    with c.stage() as block:
        @block.tensor
        def _(pe):
            for i, (m, f) in enumerate(steps):
                if i >= 4:
                    pe.wait_ge(copied, i - 3)
                for j in range(4):
                    last = nc.tensor.transpose(c.psum[:, i % 4, j * P:(j + 1) * P], kv[:, f + j, m * P:(m + 1) * P], c.ident[:])
                last.then_inc(turned, 1)

        @block.vector
        def _(dve):
            for i, (m, f) in enumerate(steps):
                dve.wait_ge(turned, i + 1)
                nc.vector.tensor_copy(k_rows_all[:, m, f * P:(f + 4) * P], c.psum[:, i % 4, :]).then_inc(copied, 1)

        @block.sync
        def _(sp):
            half = len(steps) // 2
            for i, out in enumerate(("prompt_mem_k", "prompt_mem_v")):
                sp.wait_ge(copied, half * (i + 1))
                sp.dma_start(c.outs[out][layer, 0].rearrange("(m p) h d -> p m (h d)", p=P),
                             k_rows_all[:, :, i * D:(i + 1) * D]).then_inc(stored, 16)
            sp.wait_ge(stored, 32)


def cross_attention(c, name, q, kv, kv_rows, s_kt, s_v, o, scratch):
    nc = c.nc
    MT = NMEM // P
    QT = SEQ // P
    at = [0]

    def part(*shape):
        n = int(np.prod(shape))
        ap = c.flat(scratch, n, at=at[0])
        at[0] += n
        return ap if len(shape) == 1 else ap.rearrange("p (a b) -> p a b", a=shape[0])

    class Head:

        def __init__(self, g):
            self.q, self.v, self.s_v = part(2, T), part(MT, 2 * P), part(MT, 2 * P)
            self.prob, self.prob_s = part(QT, NMEM), part(NMEM)[0:DEC, :]
            self.prob_t, self.prob_ts = part(MT, SEQ), part(MT, DEC)
            self.neg_max, self.total, self.inverse = part(QT + 1), part(QT + 1), part(QT + 1)
            bank = [c.psum[:, 4 * g + b, :] for b in range(4)]
            self.z = c.psum[:, 4 * g:4 * g + 2, :].rearrange("p b (i n) -> p (b i) n", i=2)
            self.wide = bank[0:2]
            self.z_s = bank[2][0:DEC, 0:NMEM]
            self.turned_s, self.o_s = bank[3][:, 0:MT * DEC], bank[3][:, MT * DEC:MT * DEC + 2 * DEC]
            self.sems = {}
            for x in ("q_staged", "v_staged", "s_v_staged", "scored", "maxed", "maxed_s", "exped", "exped_s", "inverted",
                      "scaled", "turned", "copied", "turned_s", "copied_s"):
                self.sems[x] = c.sem(f"{name}_{x}{g}")
            for x in ("scored_s", "weighed", "weighed_s", "o_copied", "o_s_copied"):
                self.sems[x] = c.sem(f"{name}_{x}{g}", primed=True)

    heads = [Head(g) for g in range(2)]
    assert at[0] <= 3 * REGION

    def s(x, g):
        return heads[g].sems[x]

    with c.stage() as block:
        @block.gpsimd
        def _(pool):
            with pool.Fori(0, XH // 2) as it:
                for g, hd in enumerate(heads):
                    pool.wait_ge(s("scored_s", g), it + PRIMED)
                    nc.gpsimd.tensor_copy(hd.q, q[:, bass.ds(it * 4 + 2 * g, 2), :]).then_inc(s("q_staged", g), 1)
                for g, hd in enumerate(heads):
                    pool.wait_ge(s("weighed", g), it * 2 + PRIMED)
                    nc.gpsimd.tensor_copy(hd.v, kv_rows[:, :, bass.ds(it * 4 * P + (D + 2 * g * P), 2 * P)]).then_inc(s("v_staged", g), 1)
                    pool.wait_ge(s("weighed_s", g), it + PRIMED)
                    nc.gpsimd.tensor_copy(hd.s_v, s_v[:, :, bass.ds(it * 4 * P + 2 * g * P, 2 * P)]).then_inc(s("s_v_staged", g), 1)

        @block.tensor
        def _(pe):
            with pe.Fori(0, XH // 2) as it:
                def keys(t, g, kk):
                    return t[:, bass.ds(it * 4 + (2 * g + kk), 1), :].rearrange("p o n -> p (o n)")
                for g, hd in enumerate(heads):
                    pe.wait_ge(s("q_staged", g), it + 1)
                    pe.wait_ge(s("o_copied", g), it * 2 + PRIMED)
                    for i in range(QT):
                        for kk in range(2):
                            last = nc.tensor.matmul(hd.z[:, i, :], hd.q[:, kk, i * P:(i + 1) * P], keys(kv, g, kk),
                                                    start=kk == 0 and i % 2 == 0, stop=kk == 1, skip_group_check=True)
                    last.then_inc(s("scored", g), 1)
                    for kk in range(2):
                        last = nc.tensor.matmul(hd.z_s, hd.q[:, kk, SEQ:T], keys(s_kt, g, kk), start=kk == 0, stop=kk == 1)
                    last.then_inc(s("scored_s", g), 1)
                for g, hd in enumerate(heads):
                    pe.wait_ge(s("o_s_copied", g), it + PRIMED)
                    pe.wait_ge(s("scaled", g), it * (QT + 1) + QT + 1)
                    for m in range(MT):
                        for i in range(QT):
                            last = nc.tensor.transpose(hd.wide[m][:, i * P:(i + 1) * P], hd.prob[:, i, m * P:(m + 1) * P], c.ident[:])
                        last.then_inc(s("turned", g), 1)
                    for m in range(MT):
                        last = nc.tensor.transpose(hd.turned_s[:, m * DEC:(m + 1) * DEC], hd.prob_s[:, m * P:(m + 1) * P], c.ident[0:DEC, 0:DEC])
                    last.then_inc(s("turned_s", g), 1)
                for g, hd in enumerate(heads):
                    pe.wait_ge(s("copied", g), it * 2 + 2)
                    pe.wait_ge(s("v_staged", g), it + 1)
                    for e in range(2):
                        for m in range(MT):
                            last = nc.tensor.matmul(hd.wide[e], hd.v[:, m, e * P:(e + 1) * P], hd.prob_t[:, m, :],
                                                    start=m == 0, stop=m == MT - 1)
                        last.then_inc(s("weighed", g), 1)
                    pe.wait_ge(s("copied_s", g), it + 1)
                    pe.wait_ge(s("s_v_staged", g), it + 1)
                    for e in range(2):
                        for m in range(MT):
                            last = nc.tensor.matmul(hd.o_s[:, e * DEC:(e + 1) * DEC], hd.s_v[:, m, e * P:(e + 1) * P], hd.prob_ts[:, m, :],
                                                    start=m == 0 and e == 0, stop=m == MT - 1, skip_group_check=True)
                    last.then_inc(s("weighed_s", g), 1)

        @block.vector
        def _(dve):
            with dve.Fori(0, XH // 2) as it:
                for g, hd in enumerate(heads):
                    dve.wait_ge(s("scored", g), it + 1)
                    nc.vector.tensor_reduce(hd.neg_max[:, 0:QT], hd.z, AX_X, ALU.max, negate=True).then_inc(s("maxed", g), 1)
                    dve.wait_ge(s("scored_s", g), it + 1 + PRIMED)
                    nc.vector.tensor_reduce(hd.neg_max[0:DEC, QT:QT + 1], hd.z_s, AX_X, ALU.max, negate=True).then_inc(s("maxed_s", g), 1)
                for g, hd in enumerate(heads):
                    dve.wait_ge(s("exped", g), it * QT + QT)
                    nc.vector.reciprocal(hd.inverse[:, 0:QT], hd.total[:, 0:QT]).then_inc(s("inverted", g), 1)
                    dve.wait_ge(s("exped_s", g), it + 1)
                    nc.vector.reciprocal(hd.inverse[0:DEC, QT:QT + 1], hd.total[0:DEC, QT:QT + 1]).then_inc(s("inverted", g), 1)
                    dve.wait_ge(s("inverted", g), it * 2 + 2)
                    for i in range(QT):
                        nc.vector.tensor_scalar(hd.prob[:, i, :], hd.prob[:, i, :], hd.inverse[:, i:i + 1], None, ALU.mult).then_inc(s("scaled", g), 1)
                    nc.vector.tensor_scalar(hd.prob_s, hd.prob_s, hd.inverse[0:DEC, QT:QT + 1], None, ALU.mult).then_inc(s("scaled", g), 1)
                for g, hd in enumerate(heads):
                    dve.wait_ge(s("turned", g), it * 2 + 1)
                    nc.vector.tensor_copy(hd.prob_t[:, 0, :], hd.wide[0]).then_inc(s("copied", g), 1)
                for g, hd in enumerate(heads):
                    dve.wait_ge(s("weighed", g), it * 2 + 1 + PRIMED)
                    nc.vector.tensor_scalar(o[:, bass.ds(it * 4 + 2 * g, 1), 0:SEQ].rearrange("p o t -> p (o t)"), hd.wide[0],
                                            1.0, None, ALU.mult).then_inc(s("o_copied", g), 1)
                    dve.wait_ge(s("weighed_s", g), it + 1 + PRIMED)
                    nc.vector.tensor_scalar(o[:, bass.ds(it * 4 + 2 * g, 2), SEQ:T], hd.o_s.rearrange("p (e t) -> p e t", e=2),
                                            1.0, None, ALU.mult).then_inc(s("o_s_copied", g), 1)

        @block.scalar
        def _(act):
            with act.Fori(0, XH // 2) as it:
                for g, hd in enumerate(heads):
                    act.wait_ge(s("maxed", g), it + 1)
                    for i in range(QT):
                        nc.scalar.activation(hd.prob[:, i, :], hd.z[:, i, :], ACT.Exp, bias=hd.neg_max[:, i:i + 1],
                                             accum_out=hd.total[:, i:i + 1]).then_inc(s("exped", g), 1)
                    act.wait_ge(s("maxed_s", g), it + 1)
                    nc.scalar.activation(hd.prob_s, hd.z_s, ACT.Exp, bias=hd.neg_max[0:DEC, QT:QT + 1],
                                         accum_out=hd.total[0:DEC, QT:QT + 1]).then_inc(s("exped_s", g), 1)
                for g, hd in enumerate(heads):
                    act.wait_ge(s("turned", g), it * 2 + 2)
                    nc.scalar.copy(hd.prob_t[:, 1, :], hd.wide[1]).then_inc(s("copied", g), 1)
                    act.wait_ge(s("turned_s", g), it + 1)
                    nc.scalar.copy(hd.prob_ts, hd.turned_s.rearrange("p (m t) -> p m t", m=MT)).then_inc(s("copied_s", g), 1)
                for g, hd in enumerate(heads):
                    act.wait_ge(s("weighed", g), it * 2 + 2 + PRIMED)
                    nc.scalar.copy(o[:, bass.ds(it * 4 + (2 * g + 1), 1), 0:SEQ].rearrange("p o t -> p (o t)"), hd.wide[1]).then_inc(s("o_copied", g), 1)


def sample_memory(c, name, layer, rows, s_kt):
    nc = c.nc
    landed, turned, copied = c.sem(name + "_landed"), c.sem(name + "_turned"), c.sem(name + "_copied")
    with c.stage() as block:
        @block.scalar
        def _(act):
            for i, src in enumerate(("cache_mem_k", "cache_mem_v")):
                act.dma_start(rows[i], c.ins[src][layer, 0].rearrange("(m p) h d -> p m (h d)", p=P)).then_inc(landed, 16)

        @block.tensor
        def _(pe):
            pe.wait_ge(landed, 32)
            for i in range(KT // 2):
                for j in range(2):
                    for m in range(2):
                        f = 2 * i + j
                        last = nc.tensor.transpose(c.psum[:, i, j * NMEM + m * P:j * NMEM + (m + 1) * P],
                                                   rows[0][:, m, f * P:(f + 1) * P], c.ident[:])
                last.then_inc(turned, 1)

        @block.vector
        def _(dve):
            for i in range(KT // 2):
                dve.wait_ge(turned, i + 1)
                nc.vector.tensor_copy(s_kt[:, 2 * i:2 * i + 2, :], c.psum[:, i, :].rearrange("p (j n) -> p j n", j=2)).then_inc(copied, 1)
            dve.wait_ge(copied, KT // 2)


def gate_and_up(c, name, job, nxt, hidden, gated):
    nc, base = c.nc, c.rounds
    cut, lowered = c.sem(name + "_hidden_high"), c.sem(name + "_hidden_low")

    def two(ap):
        return ap.rearrange("p (a b) -> p a b", a=2)

    def emptying(i):
        def run(it):
            full, high, low = (t[:, bass.ds(it * 2 + i, 1), :] for t in (hidden.full, hidden.high, hidden.low))
            nc.vector.wait_ge(c.slot_emptied[2 * i], it + (c.emptied[2 * i] + 1))
            nc.vector.wait_ge(c.unit_done[2 * i + 1], it + (base + 1))
            nc.vector.tensor_tensor(halves(full), c.psum[:, 4 * i + 2:4 * i + 4, 0:HALF], two(gated[:, i, :]),
                                    ALU.mult).then_inc(c.slot_emptied[2 * i + 1], 1)
            nc.vector.wait_ge(c.slot_emptied[2 * i + 1], it + (c.emptied[2 * i + 1] + 1))
            take_high(c, high, full).then_inc(cut, 1)
            nc.vector.wait_ge(cut, it * 2 + (i + 1))
            take_low(c, low, full, high).then_inc(lowered, 1)
        return run

    with c.stage() as block:
        @block.sync
        def _(sp):
            stream_weights(c, sp, job, nxt)

        @block.tensor
        def _(pe):
            multiply_units(c, pe, job)

        @block.scalar
        def _(act):
            with act.Fori(0, job.iters) as it:
                for i in range(2):
                    act.wait_ge(c.unit_done[2 * i], it + base + 1)
                    act.wait_ge(c.slot_emptied[2 * i + 1], it + c.emptied[2 * i + 1])
                    nc.scalar.activation(two(gated[:, i, :]), c.psum[:, 4 * i:4 * i + 2, 0:HALF],
                                         ACT.Silu).then_inc(c.slot_emptied[2 * i], 1)

        @block.vector
        def _(dve):
            split_and_empty(c, dve, job, {2 * i + 1: emptying(i) for i in range(2)})
            dve.wait_ge(lowered, job.iters * 2)
    finish(c, job, range(RING))


def token_shift(c, h, xx, mixes):
    nc = c.nc
    shift_rows = c.flat(9, 2 * P)[0:KT, :].rearrange("p (i n) -> p i n", i=2)
    shifted, mixed = c.sem("tokens_shifted"), c.sem("tokens_mixed")
    turned, copied, stored = c.sem("shift_turned"), c.sem("shift_copied"), c.sem("shift_stored")
    with c.stage() as block:
        @block.vector
        def _(dve):
            nc.vector.tensor_tensor(xx[:, 0:5, 1:T], h[:, 0:5, 0:T - 1], h[:, 0:5, 1:T], ALU.subtract).then_inc(shifted, 1)
            dve.wait_ge(shifted, 2)
            nc.vector.tensor_scalar(xx[:, :, 0:1], h[:, :, 0:1], -1.0, None, ALU.mult).then_inc(shifted, 1)
            nc.vector.tensor_tensor(xx[:, :, SEQ:SEQ + 1], c.vec["state_rwkv_shift"].rearrange("p (k o) -> p k o", o=1),
                                    h[:, :, SEQ:SEQ + 1], ALU.subtract).then_inc(shifted, 1)
            dve.wait_ge(shifted, 4)
            for m, out in mixes:
                mix_tokens(c, h, xx, m, out, mixed)
            dve.wait_ge(mixed, KT * len(mixes))

        @block.gpsimd
        def _(pool):
            nc.gpsimd.tensor_tensor(xx[:, 5:KT, 1:T], h[:, 5:KT, 0:T - 1], h[:, 5:KT, 1:T], ALU.subtract).then_inc(shifted, 1)

        @block.tensor
        def _(pe):
            for i, t in enumerate((SEQ - 1, T - 1)):
                last = nc.tensor.transpose(c.psum[0:KT, 0, i * P:(i + 1) * P], h[:, :, t], c.ident[:])
            last.then_inc(turned, 1)

        @block.scalar
        def _(act):
            act.wait_ge(turned, 1)
            nc.scalar.copy(shift_rows, c.psum[0:KT, 0, 0:2 * P].rearrange("p (i n) -> p i n", i=2)).then_inc(copied, 1)

        @block.sync
        def _(sp):
            sp.wait_ge(copied, 1)
            for i, out in enumerate(("prompt_rwkv_shift", "sample_rwkv_shift")):
                sp.dma_start(c.outs[out].rearrange("l b (k p) -> (l b k) p", p=P), shift_rows[:, i, :]).then_inc(stored, 16)
            sp.wait_ge(stored, 32)


def mix_tokens(c, h, xx, m, out, done):
    mu = c.vec["rw_mu"]
    for k in range(KT):
        c.nc.vector.scalar_tensor_tensor(out=out[:, k, :], in0=xx[:, k, :], scalar=mu[:, m * KT + k:m * KT + k + 1],
                                         in1=h[:, k, :], op0=ALU.mult, op1=ALU.add).then_inc(done, 1)


def key_norms(c, k, inv):
    nc = c.nc
    s = {x: c.sem("key_" + x, primed=x in ("summed", "bounded")) for x in ("squared", "summed", "bounded", "rooted", "inverted")}
    sq = c.ring_words()[:, 0:T]
    pv = c.psum[:, 0:2, 0:HALF]
    with c.stage() as block:
        @block.scalar
        def _(act):
            with act.Fori(0, PAIRS) as it:
                act.wait_ge(s["summed"], it + PRIMED)
                nc.scalar.activation(sq, k[:, bass.ds(it, 1), :].rearrange("p o t -> p (o t)"), ACT.Square,
                                     scale=c.vec["rw_k_k"][:, bass.ds(it, 1)]).then_inc(s["squared"], 1)
            act.wait_ge(s["bounded"], PAIRS + PRIMED)
            for p in range(PAIRS):
                nc.scalar.activation(inv[:, p, :], inv[:, p, :], ACT.Sqrt).then_inc(s["rooted"], 1)

        @block.tensor
        def _(pe):
            with pe.Fori(0, PAIRS) as it:
                pe.wait_ge(s["squared"], it + 1)
                pe.wait_ge(s["bounded"], it + PRIMED)
                for b in range(2):
                    last = nc.tensor.matmul(c.psum[:, b, 0:HALF], c.head_ones[:], sq[:, b * HALF:(b + 1) * HALF], start=True, stop=True)
                last.then_inc(s["summed"], 1)

        @block.vector
        def _(dve):
            with dve.Fori(0, PAIRS) as it:
                dve.wait_ge(s["summed"], it + 1 + PRIMED)
                nc.vector.tensor_scalar(halves(inv[:, bass.ds(it, 1), :]), pv, 1e-24, None, ALU.max).then_inc(s["bounded"], 1)
            for p in range(PAIRS):
                dve.wait_ge(s["rooted"], p + 1)
                nc.vector.reciprocal(inv[:, p, :], inv[:, p, :]).then_inc(s["inverted"], 1)
            dve.wait_ge(s["inverted"], PAIRS)


def decay_factors(c, r, k, v, sw, a, inv, a_out, b_out, scratch):
    nc = c.nc
    c.chunk_decay = c.tile("chunk_decay", [P, PAIRS, SEQ // L + 1])
    c.one_minus_ka = c.tile("one_minus_ka", [P, KT])
    goes_on, logw, cum, cum_prev, e_cum, e_prev = (c.flat(scratch, T, at=(2 + i) * T) for i in range(6))
    kk, kka, kmul, kmod, rk, e_neg = (c.ring_words()[:, i * T:(i + 1) * T] for i in range(6))
    s = {x: c.sem("decay_" + x, primed=x in ("done_v", "done_p")) for x in ("ready", "log", "cum", "prev", "e_cum", "e_prev", "e_neg", "kk", "kka",
                                          "kmul", "kmod", "rk", "bonus_sum", "done_v", "done_p")}

    def tile(t, it):
        return t[:, bass.ds(it, 1), :].rearrange("p o t -> p (o t)")

    def col(name, it):
        return c.vec[name][:, bass.ds(it, 1)]
    DONE_V, DONE_P = 4, 3
    with c.stage() as block:
        @block.scalar
        def _(act):
            with act.Fori(0, PAIRS) as it:
                act.wait_ge(s["done_v"], it * DONE_V + PRIMED)
                act.wait_ge(s["done_p"], it * DONE_P + PRIMED)
                nc.scalar.activation(logw, tile(sw, it), ACT.Copy, scale=-float(np.exp(-0.5))).then_inc(s["log"], 1)
                act.wait_ge(s["cum"], it + 1)
                nc.scalar.activation(e_neg, cum, ACT.Exp, scale=-1.0).then_inc(s["e_neg"], 1)
                nc.scalar.activation(e_cum, cum, ACT.Exp).then_inc(s["e_cum"], 1)
                act.wait_ge(s["prev"], it + 1)
                nc.scalar.activation(e_prev, cum_prev, ACT.Exp).then_inc(s["e_prev"], 1)
                act.wait_ge(s["e_cum"], it + 1)
                ends = e_cum[:, 0:SEQ].rearrange("p (n l) -> p n l", l=L)[:, :, L - 1]
                nc.scalar.copy(c.chunk_decay[:, bass.ds(it, 1), 0:SEQ // L].rearrange("p o n -> p (o n)"), ends).then_inc(s["done_v"], 1)
                nc.scalar.copy(c.chunk_decay[:, bass.ds(it, 1), SEQ // L:].rearrange("p o n -> p (o n)"), e_cum[:, T - 1:T]).then_inc(s["done_v"], 1)

        @block.gpsimd
        def _(pool):
            nc.gpsimd.memset(goes_on, 1.0).then_inc(s["ready"], 1)
            pool.wait_ge(s["ready"], 1)
            nc.gpsimd.memset(goes_on.rearrange("p (n l) -> p n l", l=DEC)[:, 0::2, 0], 0.0).then_inc(s["ready"], 1)
            with pool.Fori(0, PAIRS) as it:
                pool.wait_ge(s["log"], it + 1)
                pool.wait_ge(s["cum"], it + 1)
                nc.gpsimd.tensor_tensor(cum_prev, cum, logw, ALU.subtract).then_inc(s["prev"], 1)
                pool.wait_ge(s["kk"], it + 1)
                nc.gpsimd.tensor_tensor(kka, kk, tile(a, it), ALU.mult).then_inc(s["kka"], 1)
                pool.wait_ge(s["kka"], it + 1)
                pool.wait_ge(s["e_neg"], it + 1)
                nc.gpsimd.tensor_tensor(tile(b_out, it), kka, e_neg, ALU.mult).then_inc(s["done_p"], 1)
                pool.wait_ge(s["kmod"], it + 1)
                nc.gpsimd.tensor_tensor(tile(k, it), kmod, e_neg, ALU.mult).then_inc(s["done_p"], 1)
                pool.wait_ge(s["rk"], it + 1)
                pool.wait_ge(s["e_cum"], it + 1)
                nc.gpsimd.tensor_tensor(tile(r, it), tile(r, it), e_cum, ALU.mult).then_inc(s["done_p"], 1)

        @block.tensor
        def _(pe):
            with pe.Fori(0, PAIRS) as it:
                pe.wait_ge(s["rk"], it + 1)
                pe.wait_ge(s["done_v"], it * DONE_V + PRIMED)
                for b in range(2):
                    last = nc.tensor.matmul(c.psum[:, b, 0:HALF], c.head_ones[:], rk[:, b * HALF:(b + 1) * HALF], start=True, stop=True)
                last.then_inc(s["bonus_sum"], 1)

        @block.vector
        def _(dve):
            dve.wait_ge(s["ready"], 2)
            nc.vector.tensor_scalar(c.one_minus_ka[:], c.vec["rw_k_a"], -1.0, 1.0, ALU.mult, ALU.add).then_inc(s["ready"], 1)
            dve.wait_ge(s["ready"], 3)
            with dve.Fori(0, PAIRS) as it:
                dve.wait_ge(s["done_v"], it * DONE_V + PRIMED)
                dve.wait_ge(s["done_p"], it * DONE_P + PRIMED)
                nc.vector.scalar_tensor_tensor(out=kk, in0=tile(k, it), scalar=col("rw_k_k", it), in1=tile(inv, it),
                                               op0=ALU.mult, op1=ALU.mult).then_inc(s["kk"], 1)
                nc.vector.tensor_scalar(kmul, tile(a, it), col("rw_k_a", it), c.one_minus_ka[:, bass.ds(it, 1)],
                                        ALU.mult, ALU.add).then_inc(s["kmul"], 1)
                dve.wait_ge(s["log"], it + 1)
                nc.vector.tensor_tensor_scan(cum, goes_on, logw, 0.0, ALU.mult, ALU.add).then_inc(s["cum"], 1)
                dve.wait_ge(s["kmul"], it + 1)
                nc.vector.tensor_tensor(kmod, tile(k, it), kmul, ALU.mult).then_inc(s["kmod"], 1)
                dve.wait_ge(s["kmod"], it + 1)
                nc.vector.scalar_tensor_tensor(out=rk, in0=tile(r, it), scalar=col("rw_r_k", it), in1=kmod,
                                               op0=ALU.mult, op1=ALU.mult).then_inc(s["rk"], 1)
                dve.wait_ge(s["e_prev"], it + 1)
                dve.wait_ge(s["kk"], it + 1)
                nc.vector.scalar_tensor_tensor(out=tile(a_out, it), in0=kk, scalar=-1.0, in1=e_prev,
                                               op0=ALU.mult, op1=ALU.mult).then_inc(s["done_v"], 1)
                dve.wait_ge(s["bonus_sum"], it + 1)
                nc.vector.tensor_tensor(halves(inv[:, bass.ds(it, 1), :]), c.psum[:, 0:2, 0:HALF], halves(v[:, bass.ds(it, 1), :]),
                                        ALU.mult).then_inc(s["done_v"], 1)


class Quad:

    def __init__(self, spaces, tail):
        n = 4 * P
        buf = [w[:, i * n:(i + 1) * n].rearrange("p (j n) -> p j n", j=4)
               for w in spaces for i in range(w.shape[-1] // n)]
        (self.A, self.B, self.K, self.V, self.m16t, self.m16, self.to32, self.to64, self.q, self.ak,
         self.rbk, self.A_rows, self.B_rows, self.K_rows, self.V_rows, self.mv) = buf[0:16]
        self.R = tail.rearrange("p (j n) -> p j n", j=4)
        self.m2, self.m2t, self.m4, self.m4t, self.m8 = self.A, self.B, self.K, self.V, self.ak
        self.x, self.turned = self.m16, self.m16t
        self.Pa, self.U0, self.phi, self.Rh = self.A, self.B, self.K, self.mv[:, :, 0:L]


def wkv(c, quads, states, finals, A, B, R, K, V, y, sample):
    nc = c.nc
    n_it = 1 if sample else PAIRS
    names = ("zeroed ready_v ready_s ready_p ab_done am_done ak_done rbk_done am_copied m16t_ready m16_ready joins_ready "
             "ak_ready rbk_ready q0_ready rowsA_done rowsB_done rowsK_done rowsV_done rowsA rowsB rowsK rowsV m2_done m2_ready m2t_done m2t_ready "
             "mv_done mv_ready q_done q_ready m4_done m4_ready m4t_done m4t_ready m8_done m8_ready x_done x_ready "
             "turned_done turned_ready pa_done pa_ready u_done u_ready rh_done rh_ready phi_done phi_ready "
             "s_done s_ready y_done y_ready").split()
    s = [{x: c.sem(f"wkv{q}_{x}", primed=x in ("y_done", "s_ready", "y_ready")) for x in names} for q in range(2)]
    rows64 = [slice(0, HD), slice(HD, P)]

    def bank(q, b):
        return c.psum[:, 4 * q + b, :].rearrange("p (j n) -> p j n", j=4)

    def tokens(t, it, q, rows):
        if sample:
            return t[rows, 4 * q:4 * q + 4, SEQ:T]
        return t[rows, bass.ds(it, 1), q * 4 * L:(q + 1) * 4 * L].rearrange("p o (j n) -> p (o j) n", j=4)
    W = DEC if sample else L

    def loop(eng, body):
        if sample:
            body(0)
        else:
            with eng.Fori(0, n_it) as it:
                body(it)

    with c.stage() as block:
        @block.gpsimd
        def _(pool):
            for q in range(2):
                for t in (quads[q].A, quads[q].B, quads[q].K, quads[q].V, quads[q].R):
                    nc.gpsimd.memset(t, 0.0).then_inc(s[q]["zeroed"], 1)
            if not sample:
                nc.gpsimd.memset(states[:, 0, :], 0.0).then_inc(s[0]["zeroed"], 1)
            pool.wait_ge(s[0]["zeroed"], 5 if sample else 6)
            pool.wait_ge(s[1]["zeroed"], 5)

            def body(it):
                for q in range(2):
                    z = quads[q]
                    pool.wait_ge(s[q]["y_done"], it + PRIMED)
                    nc.gpsimd.tensor_copy(z.R[:, :, 0:W], tokens(R, it, q, slice(0, P))).then_inc(s[q]["ready_p"], 1)
                for q in range(2):
                    z = quads[q]
                    pool.wait_ge(s[q]["m16t_ready"], it + 1)
                    nc.gpsimd.tensor_tensor(z.q, z.m16t, c.ident[:].rearrange("p (o n) -> p o n", o=1).broadcast_to([P, 4, P]), ALU.add).then_inc(s[q]["q0_ready"], 1)
                for q in range(2):
                    z = quads[q]
                    pool.wait_ge(s[q]["am_copied"], it + 1)
                    nc.gpsimd.tensor_tensor(z.to64, z.to32, c.to64_lo[:].rearrange("p (o n) -> p o n", o=1).broadcast_to([P, 4, P]), ALU.mult).then_inc(s[q]["joins_ready"], 1)
                    pool.wait_ge(s[q]["joins_ready"], it * 2 + 1)
                    nc.gpsimd.tensor_tensor(z.to32, z.to32, c.to32_lo[:].rearrange("p (o n) -> p o n", o=1).broadcast_to([P, 4, P]), ALU.mult).then_inc(s[q]["joins_ready"], 1)
            loop(pool, body)

        @block.vector
        def _(dve):
            def spread(m, n=P):
                return m[:].rearrange("p (o n) -> p o n", o=1).broadcast_to([P, 4, n])

            def body(it):
                for q in range(2):
                    z, e = quads[q], s[q]
                    dve.wait_ge(e["zeroed"], 5)
                    dve.wait_ge(e["y_done"], it + PRIMED)
                    for src, dst in ((A, z.A), (B, z.B)):
                        for h, r in enumerate(rows64):
                            nc.vector.tensor_scalar(dst[r, :, h * L:h * L + W], tokens(src, it, q, r), 1.0, None, ALU.mult).then_inc(e["ready_v"], 1)
                for q in range(2):
                    z, e = quads[q], s[q]
                    dve.wait_ge(e["ab_done"], it + 1)
                    nc.vector.tensor_tensor(z.m16t, bank(q, 0), spread(c.in16_up), ALU.mult).then_inc(e["m16t_ready"], 1)
                    dve.wait_ge(e["am_done"], it + 1)
                    dve.wait_ge(e["am_copied"], it + 1)
                    nc.vector.tensor_tensor(z.m16, bank(q, 1), spread(c.in16_lo), ALU.mult).then_inc(e["m16_ready"], 1)
                    dve.wait_ge(e["ak_done"], it + 1)
                    nc.vector.tensor_tensor(z.ak, bank(q, 2), spread(c.strict_up), ALU.mult).then_inc(e["ak_ready"], 1)
                    dve.wait_ge(e["rbk_done"], it + 1)
                    nc.vector.tensor_tensor(z.rbk.rearrange("p j (u n) -> p (j u) n", u=2), bank(q, 3).rearrange("p j (u n) -> p (j u) n", u=2),
                                            c.incl_up[:].rearrange("p (o n) -> p o n", o=1).broadcast_to([P, 8, L]), ALU.mult).then_inc(e["rbk_ready"], 1)
                for q in range(2):
                    z, e = quads[q], s[q]
                    dve.wait_ge(e["rowsK_done"], it + 1)
                    nc.vector.tensor_copy(z.K_rows, bank(q, 2)).then_inc(e["rowsK"], 1)
                for q in range(2):
                    z, e = quads[q], s[q]
                    dve.wait_ge(e["m2_done"], it + 1)
                    nc.vector.tensor_copy(z.m2, bank(q, 0)).then_inc(e["m2_ready"], 1)

                def add_q(step):
                    for q in range(2):
                        z, e = quads[q], s[q]
                        dve.wait_ge(e["q0_ready"], it + 1)
                        dve.wait_ge(e["q_done"], it * 5 + step)
                        nc.vector.tensor_tensor(z.q, bank(q, 3), z.q, ALU.add).then_inc(e["q_ready"], 1)
                add_q(1)
                for q in range(2):
                    z, e = quads[q], s[q]
                    dve.wait_ge(e["m4t_done"], it + 1)
                    nc.vector.tensor_copy(z.m4t, bank(q, 1)).then_inc(e["m4t_ready"], 1)
                add_q(2)
                add_q(3)
                for join in range(2):
                    for q in range(2):
                        z, e = quads[q], s[q]
                        dve.wait_ge(e["turned_done"], it * 2 + join + 1)
                        nc.vector.tensor_copy(z.turned, bank(q, 1)).then_inc(e["turned_ready"], 1)
                    add_q(4 + join)
                for q in range(2):
                    z, e = quads[q], s[q]
                    dve.wait_ge(e["u_done"], it + 1)
                    nc.vector.tensor_copy(z.U0, bank(q, 1)).then_inc(e["u_ready"], 1)
                for q in range(2):
                    z, e = quads[q], s[q]
                    dve.wait_ge(e["phi_done"], it + 1)
                    nc.vector.tensor_tensor(z.phi, bank(q, 3), spread(c.ident), ALU.add).then_inc(e["phi_ready"], 1)
                    dve.wait_ge(e["rh_done"], it + 1)
                    nc.vector.tensor_tensor(z.Rh, bank(q, 2)[:, :, 0:L], z.R, ALU.add).then_inc(e["rh_ready"], 1)
                for q in range(2):
                    z, e = quads[q], s[q]
                    dve.wait_ge(e["y_done"], it + 1 + PRIMED)
                    out = tokens(y, it, q, slice(0, P))
                    nc.vector.tensor_scalar(out, bank(q, 1)[:, :, 0:W], 1.0, None, ALU.mult).then_inc(e["y_ready"], 1)
            loop(dve, body)

        @block.scalar
        def _(act):
            def body(it):
                for q in range(2):
                    z, e = quads[q], s[q]
                    act.wait_ge(e["zeroed"], 5)
                    act.wait_ge(e["y_done"], it + PRIMED)
                    for src, dst in ((K, z.K), (V, z.V)):
                        for h, r in enumerate(rows64):
                            nc.scalar.copy(dst[r, :, h * L:h * L + W], tokens(src, it, q, r)).then_inc(e["ready_s"], 1)
                for q in range(2):
                    z, e = quads[q], s[q]
                    act.wait_ge(e["am_done"], it + 1)
                    nc.scalar.copy(z.to32, bank(q, 1)).then_inc(e["am_copied"], 1)
                for q in range(2):
                    z, e = quads[q], s[q]
                    act.wait_ge(e["rowsA_done"], it + 1)
                    nc.scalar.copy(z.A_rows, bank(q, 0)).then_inc(e["rowsA"], 1)
                    act.wait_ge(e["rowsB_done"], it + 1)
                    nc.scalar.copy(z.B_rows, bank(q, 1)).then_inc(e["rowsB"], 1)
                    act.wait_ge(e["rowsV_done"], it + 1)
                    nc.scalar.copy(z.V_rows, bank(q, 3)).then_inc(e["rowsV"], 1)
                for q in range(2):
                    z, e = quads[q], s[q]
                    act.wait_ge(e["mv_done"], it + 1)
                    nc.scalar.copy(z.mv, bank(q, 2)).then_inc(e["mv_ready"], 1)
                    act.wait_ge(e["m2t_done"], it + 1)
                    nc.scalar.copy(z.m2t, bank(q, 1)).then_inc(e["m2t_ready"], 1)
                for q in range(2):
                    z, e = quads[q], s[q]
                    act.wait_ge(e["m4_done"], it + 1)
                    nc.scalar.copy(z.m4, bank(q, 0)).then_inc(e["m4_ready"], 1)
                for q in range(2):
                    z, e = quads[q], s[q]
                    act.wait_ge(e["m8_done"], it + 1)
                    nc.scalar.copy(z.m8, bank(q, 0)).then_inc(e["m8_ready"], 1)
                for join in range(2):
                    for q in range(2):
                        z, e = quads[q], s[q]
                        act.wait_ge(e["x_done"], it * 2 + join + 1)
                        nc.scalar.copy(z.x, bank(q, 0)).then_inc(e["x_ready"], 1)
                for q in range(2):
                    z, e = quads[q], s[q]
                    act.wait_ge(e["pa_done"], it + 1)
                    nc.scalar.copy(z.Pa, bank(q, 0)).then_inc(e["pa_ready"], 1)
                for q in range(2):
                    e = s[q]
                    for j in range(4):
                        act.wait_ge(e["s_done"], it * 4 + j + 1)
                        unit = 4 * q + j
                        if sample:
                            out, decay = finals[:, unit, :], c.chunk_decay[:, unit, SEQ // L:]
                        else:
                            out = states[:, unit + 1, :] if unit < 7 else finals[:, bass.ds(it, 1), :].rearrange("p o n -> p (o n)")
                            decay = c.chunk_decay[:, bass.ds(it, 1), unit:unit + 1].rearrange("p a b -> p (a b)")
                        nc.scalar.activation(out, bank(q, 0)[:, j, :], ACT.Copy, scale=decay).then_inc(e["s_ready"], 1)
            loop(act, body)

        @block.tensor
        def _(pe):
            mm, tr = nc.tensor.matmul, nc.tensor.transpose

            def four(dst, lhs, rhs):
                for j in range(4):
                    last = mm(dst[:, j, :], lhs[:, j, :], rhs[:, j, :], start=j == 0, stop=True, skip_group_check=True)
                return last

            def turn(dst, src):
                for j in range(4):
                    last = tr(dst[:, j, :], src[:, j, :], c.ident[:])
                return last

            def body(it):
                for q in range(2):
                    z, e = quads[q], s[q]
                    pe.wait_ge(e["ready_v"], it * 4 + 4)
                    pe.wait_ge(e["s_ready"], it * 4 + PRIMED)
                    pe.wait_ge(e["y_ready"], it + PRIMED)
                    four(bank(q, 0), z.B, z.A).then_inc(e["ab_done"], 1)
                    four(bank(q, 1), z.A, z.B).then_inc(e["am_done"], 1)
                    pe.wait_ge(e["ready_s"], it * 4 + 4)
                    pe.wait_ge(e["ready_p"], it + 1)
                    four(bank(q, 2), z.K, z.A).then_inc(e["ak_done"], 1)
                    for j in range(4):
                        mm(bank(q, 3)[:, j, 0:L], z.B[:, j, :], z.R[:, j, :], start=j == 0, stop=True, skip_group_check=True)
                        last = mm(bank(q, 3)[:, j, L:P], z.K[:, j, :], z.R[:, j, :], start=False, stop=True, skip_group_check=True)
                    last.then_inc(e["rbk_done"], 1)
                for q in range(2):
                    z, e = quads[q], s[q]
                    pe.wait_ge(e["m16t_ready"], it + 1)
                    turn(bank(q, 0), z.A).then_inc(e["rowsA_done"], 1)
                    pe.wait_ge(e["m16_ready"], it + 1)
                    turn(bank(q, 1), z.B).then_inc(e["rowsB_done"], 1)
                    pe.wait_ge(e["ak_ready"], it + 1)
                    turn(bank(q, 2), z.K).then_inc(e["rowsK_done"], 1)
                    pe.wait_ge(e["rbk_ready"], it + 1)
                    turn(bank(q, 3), z.V).then_inc(e["rowsV_done"], 1)
                for q in range(2):
                    z, e = quads[q], s[q]
                    pe.wait_ge(e["rowsA"], it + 1)
                    four(bank(q, 0), z.m16t, z.m16).then_inc(e["m2_done"], 1)
                    pe.wait_ge(e["rowsB"], it + 1)
                    four(bank(q, 1), z.m16, z.m16t).then_inc(e["m2t_done"], 1)
                    pe.wait_ge(e["rowsV"], it + 1)
                    pe.wait_ge(e["rowsK"], it + 1)
                    four(bank(q, 2), z.ak, z.V_rows).then_inc(e["mv_done"], 1)
                for q in range(2):
                    z, e = quads[q], s[q]
                    pe.wait_ge(e["m2_ready"], it + 1)
                    pe.wait_ge(e["q0_ready"], it + 1)
                    four(bank(q, 3), z.m2, z.q).then_inc(e["q_done"], 1)
                    pe.wait_ge(e["m2t_ready"], it + 1)
                    four(bank(q, 0), z.m2t, z.m2).then_inc(e["m4_done"], 1)
                    four(bank(q, 1), z.m2, z.m2t).then_inc(e["m4t_done"], 1)
                for q in range(2):
                    z, e = quads[q], s[q]
                    pe.wait_ge(e["m4_ready"], it + 1)
                    pe.wait_ge(e["q_ready"], it * 5 + 1)
                    four(bank(q, 3), z.m4, z.q).then_inc(e["q_done"], 1)
                    pe.wait_ge(e["m4t_ready"], it + 1)
                    pe.wait_ge(e["mv_ready"], it + 1)
                    four(bank(q, 0), z.m4t, z.m4).then_inc(e["m8_done"], 1)
                for q in range(2):
                    z, e = quads[q], s[q]
                    pe.wait_ge(e["m8_ready"], it + 1)
                    pe.wait_ge(e["q_ready"], it * 5 + 2)
                    four(bank(q, 3), z.m8, z.q).then_inc(e["q_done"], 1)
                for join in range(2):
                    for q in range(2):
                        z, e = quads[q], s[q]
                        pe.wait_ge(e["q_ready"], it * 5 + 3 + join)
                        pe.wait_ge(e["joins_ready"], it * 2 + 2)
                        turn(bank(q, 1), z.q).then_inc(e["turned_done"], 1)
                        four(bank(q, 0), (z.to32, z.to64)[join], z.q).then_inc(e["x_done"], 1)
                    for q in range(2):
                        z, e = quads[q], s[q]
                        pe.wait_ge(e["x_ready"], it * 2 + join + 1)
                        pe.wait_ge(e["turned_ready"], it * 2 + join + 1)
                        four(bank(q, 3), z.turned, z.x).then_inc(e["q_done"], 1)
                for q in range(2):
                    z, e = quads[q], s[q]
                    pe.wait_ge(e["q_ready"], it * 5 + 5)
                    four(bank(q, 0), z.q, z.A_rows).then_inc(e["pa_done"], 1)
                    pe.wait_ge(e["mv_ready"], it + 1)
                    four(bank(q, 1), z.q, z.mv).then_inc(e["u_done"], 1)
                for q in range(2):
                    z, e = quads[q], s[q]
                    pe.wait_ge(e["pa_ready"], it + 1)
                    four(bank(q, 3), z.Pa, z.B_rows).then_inc(e["phi_done"], 1)
                    for j in range(4):
                        last = mm(bank(q, 2)[:, j, 0:L], z.Pa[:, j, :], z.rbk[:, j, 0:L], start=j == 0, stop=True, skip_group_check=True)
                    last.then_inc(e["rh_done"], 1)
                for q in range(2):
                    z, e = quads[q], s[q]
                    pe.wait_ge(e["u_ready"], it + 1)
                    for j in range(4):
                        mm(bank(q, 0)[:, j, :], z.B_rows[:, j, :], z.U0[:, j, :], start=j == 0, stop=False, skip_group_check=True)
                        mm(bank(q, 0)[:, j, :], z.K_rows[:, j, :], z.V_rows[:, j, :], start=False, stop=False, skip_group_check=True)
                for q in range(2):
                    z, e = quads[q], s[q]
                    pe.wait_ge(e["phi_ready"], it + 1)
                    pe.wait_ge(e["rh_ready"], it + 1)
                    for j in range(4):
                        state = states[:, 4 * q + j, :]
                        if j:
                            pe.wait_ge(e["s_ready"], it * 4 + j + PRIMED)
                        elif q and not sample:
                            pe.wait_ge(s[0]["s_ready"], it * 4 + 4 + PRIMED)
                        mm(bank(q, 0)[:, j, :], z.phi[:, j, :], state, start=False, stop=True, skip_group_check=True).then_inc(e["s_done"], 1)
                        mm(bank(q, 1)[:, j, 0:L], z.U0[:, j, :], z.rbk[:, j, 0:L], start=j == 0, stop=False, skip_group_check=True)
                        mm(bank(q, 1)[:, j, 0:L], z.V_rows[:, j, :], z.rbk[:, j, L:P], start=False, stop=False, skip_group_check=True)
                        last = mm(bank(q, 1)[:, j, 0:L], state, z.Rh[:, j, :], start=False, stop=True, skip_group_check=True)
                    last.then_inc(e["y_done"], 1)
            pe.wait_ge(s[0]["zeroed"], 5 if sample else 6)
            loop(pe, body)


def load_states(c, states, stage):
    nc = c.nc
    zeroed, landed, turned, copied = (c.sem("state_" + x) for x in ("zeroed", "landed", "turned", "copied"))
    with c.stage() as block:
        @block.gpsimd
        def _(pool):
            nc.gpsimd.memset(stage, 0.0).then_inc(zeroed, 1)

        @block.sync
        def _(sp):
            sp.wait_ge(zeroed, 1)
            heads = c.ins["state_rwkv_wkv"][0, 0].rearrange("(p h) i j -> h i p j", h=2)
            for h in range(2):
                sp.dma_start(stage[h * HD:(h + 1) * HD, :, h * HD:(h + 1) * HD], heads[h]).then_inc(landed, 16)

        @block.tensor
        def _(pe):
            pe.wait_ge(landed, 32)
            for b in range(2):
                for j in range(4):
                    last = nc.tensor.transpose(c.psum[:, b, j * P:(j + 1) * P], stage[:, 4 * b + j, :], c.ident[:])
                last.then_inc(turned, 1)

        @block.vector
        def _(dve):
            for b in range(2):
                dve.wait_ge(turned, b + 1)
                nc.vector.tensor_copy(states[:, 4 * b:4 * b + 4, :], c.psum[:, b, :].rearrange("p (j n) -> p j n", j=4)).then_inc(copied, 1)
            dve.wait_ge(copied, 2)


def store_states(c, finals, stage, out):
    nc = c.nc
    turned, copied, stored = (c.sem("final_" + x) for x in ("turned", "copied", "stored"))
    with c.stage() as block:
        @block.tensor
        def _(pe):
            for b in range(2):
                for j in range(4):
                    last = nc.tensor.transpose(c.psum[:, b, j * P:(j + 1) * P], finals[:, 4 * b + j, :], c.ident[:])
                last.then_inc(turned, 1)

        @block.vector
        def _(dve):
            for b in range(2):
                dve.wait_ge(turned, b + 1)
                nc.vector.tensor_copy(stage[:, 4 * b:4 * b + 4, :], c.psum[:, b, :].rearrange("p (j n) -> p j n", j=4)).then_inc(copied, 1)

        @block.sync
        def _(sp):
            sp.wait_ge(copied, 2)
            heads = out[0, 0].rearrange("(p h) i j -> h i p j", h=2)
            for h in range(2):
                sp.dma_start(heads[h], stage[h * HD:(h + 1) * HD, :, h * HD:(h + 1) * HD]).then_inc(stored, 16)
            sp.wait_ge(stored, 32)


def group_norm(c, y, bonus, gate, out, scratch):
    nc = c.nc
    sq, dev = (c.region(r) for r in scratch)
    s = {x: c.sem("gn_" + x, primed=x in ("d", "var")) for x in (
        "mean", "d", "d2", "var_sum", "var", "root", "inv", "n1", "n2", "n3", "full", "high", "low")}

    def tile(t, it, g):
        return t[:, bass.ds(it * 2 + g, 1), :].rearrange("p o t -> p (o t)")

    def banks(g, first):
        return c.psum[:, first + 2 * g:first + 2 * g + 2, 0:HALF]

    def over(eng, source, done, step):
        with eng.Fori(0, PAIRS // 2) as it:
            for g in range(2):
                eng.wait_ge(s[source], it * 2 + (g + 1) + (PRIMED if source in ("d", "var") else 0))
                step(it, g).then_inc(s[done], 1)

    def head_sums(pe, t, it, g, first):
        for b in range(2):
            last = nc.tensor.matmul(c.psum[:, first + 2 * g + b, 0:HALF], c.head_ones[:], tile(t, it, g)[:, b * HALF:(b + 1) * HALF],
                                    start=True, stop=True)
        return last

    nc.scalar.preload_act_table_set("sqrt_and_others")
    with c.stage() as block:
        @block.tensor
        def _(pe):
            with pe.Fori(0, PAIRS // 2) as it:
                pe.wait_ge(s["d"], it * 2 + PRIMED)
                for g in range(2):
                    head_sums(pe, y, it, g, 0).then_inc(s["mean"], 1)
            with pe.Fori(0, PAIRS // 2) as it:
                pe.wait_ge(s["var"], it * 2 + PRIMED)
                for g in range(2):
                    pe.wait_ge(s["d2"], it * 2 + g + 1)
                    head_sums(pe, sq, it, g, 4).then_inc(s["var_sum"], 1)

        @block.vector
        def _(dve):
            over(dve, "mean", "d", lambda it, g: nc.vector.scalar_tensor_tensor(
                out=halves(y[:, bass.ds(it * 2 + g, 1), :]), in0=banks(g, 0), scalar=-1.0 / HD,
                in1=halves(y[:, bass.ds(it * 2 + g, 1), :]), op0=ALU.mult, op1=ALU.add))
            over(dve, "var_sum", "var", lambda it, g: nc.vector.tensor_scalar(
                halves(dev[:, bass.ds(it * 2 + g, 1), :]), banks(g, 4), 1.0 / HD, GN_EPS, ALU.mult, ALU.add))
            with dve.Fori(0, PAIRS // 2) as it:
                for g in range(2):
                    dve.wait_ge(s["root"], it * 2 + (g + 1))
                    nc.vector.reciprocal(tile(sq, it, g), tile(dev, it, g)).then_inc(s["inv"], 1)
                    dve.wait_ge(s["inv"], it * 2 + (g + 1))
                    nc.vector.tensor_tensor(tile(y, it, g), tile(y, it, g), tile(sq, it, g), ALU.mult).then_inc(s["n1"], 1)
            over(dve, "high", "low", lambda it, g: take_low(c, tile(out.low, it, g), tile(out.full, it, g), tile(out.high, it, g)))

        @block.scalar
        def _(act):
            over(act, "d", "d2", lambda it, g: nc.scalar.activation(tile(sq, it, g), tile(y, it, g), ACT.Square))
            over(act, "var", "root", lambda it, g: nc.scalar.activation(tile(dev, it, g), tile(dev, it, g), ACT.Sqrt))
            over(act, "n1", "n2", lambda it, g: nc.scalar.activation(
                tile(y, it, g), tile(y, it, g), ACT.Identity, bias=c.vec["rw_lnx_b"][:, bass.ds(it * 2 + g, 1)],
                scale=c.vec["rw_lnx_w"][:, bass.ds(it * 2 + g, 1)]))
            over(act, "full", "high", lambda it, g: nc.scalar.activation(tile(out.high, it, g), tile(out.full, it, g), ACT.Copy))

        @block.gpsimd
        def _(pool):
            with pool.Fori(0, PAIRS // 2) as it:
                for g in range(2):
                    pool.wait_ge(s["n2"], it * 2 + (g + 1))
                    nc.gpsimd.tensor_tensor(tile(y, it, g), tile(y, it, g), tile(bonus, it, g), ALU.add).then_inc(s["n3"], 1)
                    pool.wait_ge(s["n3"], it * 2 + (g + 1))
                    nc.gpsimd.tensor_tensor(tile(out.full, it, g), tile(y, it, g), tile(gate, it, g), ALU.mult).then_inc(s["full"], 1)


def store_rows(c, name, x, stage, groups):
    nc = c.nc
    turned, copied, stored = c.sem(name + "_turned"), c.sem(name + "_copied"), c.sem(name + "_stored")
    steps = [(g, k) for g in range(len(groups)) for k in range(0, KT, 4)]
    with c.stage() as block:
        @block.tensor
        def _(pe):
            for i, (g, k) in enumerate(steps):
                t0, n, _ = groups[g]
                if i >= 4:
                    pe.wait_ge(copied, i - 3)
                for j in range(4):
                    last = nc.tensor.transpose(c.psum[0:n, i % 4, j * P:(j + 1) * P], x[:, k + j, t0:t0 + n], c.ident[:])
                last.then_inc(turned, 1)

        @block.vector
        def _(dve):
            for i, (g, k) in enumerate(steps):
                n = groups[g][1]
                dve.wait_ge(turned, i + 1)
                nc.vector.tensor_copy(stage[0:n, g, k * P:(k + 4) * P], c.psum[0:n, i % 4, :]).then_inc(copied, 1)

        @block.sync
        def _(sp):
            for g, (_, n, out) in enumerate(groups):
                sp.wait_ge(copied, 2 * g + 2)
                sp.dma_start(out, stage[0:n, g, :]).then_inc(stored, 16)
            sp.wait_ge(stored, 16 * len(groups))


def build(nc, ins, outs):
    with ExitStack() as ctx:
        c = Core(nc, ctx, ins, outs)
        x, h = c.region(0), c.region(1)
        h_parts, o_parts = Parts(c, 8, 1), Parts(c, 5, 1)
        xm = c.region(7, t=NMEM)
        mem_parts = Parts(c, 8, 8, t=NMEM, high_at=KT * NMEM)
        qkv = [c.region(2), c.region(3), c.region(4)]
        hidden = Parts(c, 5, 2, k=FT)
        kv = c.region(3, k=2 * KT, t=NMEM)
        kv_rows = c.region(4, k=2, t=2 * D)
        s_rows = [c.region(5, k=2, t=D), c.region(5, k=2, t=D, at=2 * D)]
        s_kt = c.region(6, t=NMEM)
        gated = c.region(9, k=2)

        w_qkv = ins["sb_w_qkv"][0]

        def square_job(w, parts, out=None, scale=1.0):
            emits = add_to(c, x), {}
            if out is not None:
                emits = copy_to(c, out, scale)
            return Job(KT, KT, columns(w), parts=lambda u: (parts.high, parts.low)), emits

        def kv_job(layer):
            job = Job(2 * KT, KT, columns(ins["xa_w_kv"][layer]), parts=lambda u: (mem_parts.high, mem_parts.low), tokens=NMEM)
            return job, copy_to(c, kv)

        def up_job(layer):
            w = ins["ffn_w_gate_up"][layer].rearrange("(k p) m -> p k m", p=P)
            return Job(2 * FT, KT, lambda it, u: w[:, :, bass.ds(it * (2 * P) + (u // 2) * P + (u % 2) * FF, P)],
                       parts=lambda u: (h_parts.high, h_parts.low))

        def down_job(layer):
            w = ins["ffn_w_down"][layer].rearrange("(k p) m -> p k m", p=P)
            cuts = [0, 8, 15, FT]

            def part(u):
                return tuple(t[:, cuts[u % 3]:cuts[u % 3 + 1], :] for t in (hidden.high, hidden.low))
            return Job(3 * KT, lambda u: cuts[u % 3 + 1] - cuts[u % 3],
                       lambda it, u: w[:, cuts[u % 3]:cuts[u % 3 + 1], bass.ds(it * (4 * P) + (u // 3) * P, P)],
                       parts=part, slot=lambda u: u // 3, opens=lambda u: u % 3 == 0,
                       closes=lambda u: u % 3 == 2, per=3 * RING)

        q_job = [square_job(w_qkv[:, i * D:(i + 1) * D], h_parts, qkv[i], HD ** -0.5 if i == 0 else 1.0) for i in range(3)]
        sbo_job = square_job(ins["sb_w_o"][0], o_parts)
        layer_jobs = []
        for layer in range(DEPTH):
            layer_jobs.append(dict(
                kv=kv_job(layer), xq=square_job(ins["xa_w_q"][layer], h_parts, qkv[0], (D // XH) ** -0.5),
                xo=square_job(ins["xa_w_o"][layer], o_parts), up=up_job(layer), down=down_job(layer)))

        constants(c)
        load_vectors(c)
        load_turned(c, "x", [
            (ins["x_prompt"][0], c.region(2, k=4, t=D), x[:, :, 0:SEQ]),
            (ins["x_sample"][0], c.region(3, k=1, t=D), x[:, :, SEQ:T])], D)
        with c.stage() as block:
            @block.sync
            def _(sp):
                for s in range(RING):
                    load_unit(c, sp, q_job[0][0], 0, s)

        def memory_attention(layer, nxt):
            jobs = layer_jobs[layer]
            n = f"xa{layer}"
            rms(c, n + "_norm", x, h, c.vec["norm_xattn"][:, layer * KT:], parts=h_parts)
            load_turned(c, n + "_mem", [(ins["mem_prompt"][0], c.region(6, k=2, t=D), xm)], D)
            project(c, jobs["xq"][0], jobs["kv"][0], *jobs["xq"][1])
            rms(c, n + "_mem_norm", xm, None, c.vec["norm_mem"][:, layer * KT:], tokens=NMEM, parts=mem_parts)
            project(c, jobs["kv"][0], jobs["xo"][0], *jobs["kv"][1])
            memory_rows(c, n + "_rows", layer, kv, kv_rows)
            sample_memory(c, n + "_sample", layer, s_rows, s_kt)
            cross_attention(c, n, qkv[0], kv, kv_rows, s_kt, s_rows[1], h, 7)
            split_stage(c, n + "_o", o_parts)
            project(c, jobs["xo"][0], jobs["up"], *jobs["xo"][1])
            rms(c, n + "_ffn_norm", x, h, c.vec["norm_ffn"][:, layer * KT:], parts=h_parts)
            gate_and_up(c, n, jobs["up"], jobs["down"], hidden, gated)
            project(c, jobs["down"], nxt, add_to(c, x, units=(2, 5, 8, 11)), {})

        def lora_in_job():
            src = [ins["rw_w1"][0], ins["rw_a1"][0], ins["rw_g1"][0][:, 0:GK], ins["rw_g1"][0][:, GK:GATE]]
            src = [w.rearrange("(k p) m -> p k m", p=P) for w in src]
            mixed = [c.region(3), c.region(4), c.region(5), c.region(5)]
            outs_ = [tanh_w[0:LORA, :], a_low[0:LORA, :], gate_low[0:GK, 0, :], gate_low[0:GK, 1, :]]
            funcs = [ACT.Tanh, ACT.Copy, ACT.Sigmoid, ACT.Sigmoid]

            def emit(s):
                return lambda it, ps: nc.scalar.activation(outs_[s].rearrange("p (a b) -> p a b", a=2), ps, funcs[s])
            return (Job(RING, KT, lambda it, s: src[s], moving=lambda s: mixed[s], m=lambda s: (LORA, LORA, GK, GK)[s]),
                    ({}, {s: emit(s) for s in range(RING)}))

        def lora_out_job(name, low, out, bias):
            def emit(s):
                def run(it, ps):
                    dst = halves(out[:, bass.ds(it * RING + s, 1), :])
                    if bias is None:
                        return nc.scalar.copy(dst, ps)
                    return nc.scalar.activation(dst, ps, ACT.Sigmoid, bias=c.vec[bias][:, bass.ds(it * RING + s, 1)])
                return run
            kt = low.shape[1]
            return (Job(KT, kt, columns(ins[name][0], kp=low.shape[0]), lambda s: low, kp=low.shape[0]),
                    ({}, {s: emit(s) for s in range(RING)}))

        gate_low = c.flat(9, 2 * T).rearrange("p (k t) -> p k t", k=2)
        tanh_w, a_low = c.flat(9, T, at=2 * T), c.flat(9, T, at=3 * T)

        def time_mix_job(w, parts, out):
            return Job(KT, KT, columns(ins[w][0]), parts=lambda u: (parts.high, parts.low)), copy_to(c, out)

        rms(c, "sb_norm", x, h, c.vec["norm_mix"], parts=h_parts)
        for i in range(3):
            nxt = q_job[i + 1][0] if i < 2 else sbo_job[0]
            project(c, q_job[i][0], nxt, *q_job[i][1])
        stick_breaking(c, *qkv, h, 5)
        split_stage(c, "sb_o", o_parts)
        project(c, sbo_job[0], layer_jobs[0]["xq"][0], *sbo_job[1])
        lora_in = lora_in_job()
        memory_attention(0, lora_in[0])
        r_out, k_out, v_out = c.region(3), c.region(4), c.region(5)
        mixes = [Parts(c, 7, 6), Parts(c, 5, 8)]
        time_mix = [time_mix_job("rw_w_r", mixes[0], r_out), time_mix_job("rw_w_k", mixes[1], k_out),
                    time_mix_job("rw_w_v", mixes[0], v_out)]
        lora_w = lora_out_job("rw_w2", tanh_w[0:LORA, :].rearrange("p (o t) -> p o t", o=1), c.region(6), "rw_w0")
        lora_a = lora_out_job("rw_a2", a_low[0:LORA, :].rearrange("p (o t) -> p o t", o=1), c.region(7), "rw_a0")
        lora_g = lora_out_job("rw_g2", gate_low[0:GK], c.region(6), None)
        xx = c.region(2)
        rms(c, "rw_norm", x, h, c.vec["norm_mix"][:, KT:])
        token_shift(c, h, xx, [(1, c.region(3)), (4, c.region(4)), (5, c.region(5))])

        def mix_ahead(m, out):
            mixed = c.sem(f"mixed{m}")

            def run(it, u):
                at, n = it * RING + u, it * (3 * RING) + 3 * u
                full, high, low = (t[:, bass.ds(at, 1), :] for t in (out.full, out.high, out.low))
                nc.vector.scalar_tensor_tensor(
                    out=full, in0=xx[:, bass.ds(at, 1), :], scalar=c.vec["rw_mu"][:, bass.ds(at + m * KT, 1)],
                    in1=h[:, bass.ds(at, 1), :], op0=ALU.mult, op1=ALU.add).then_inc(mixed, 1)
                nc.vector.wait_ge(mixed, n + 1)
                take_high(c, high, full).then_inc(mixed, 1)
                nc.vector.wait_ge(mixed, n + 2)
                take_low(c, low, full, high).then_inc(mixed, 1)
                nc.vector.wait_ge(mixed, n + 3)
            return run
        project(c, lora_in[0], time_mix[0][0], *lora_in[1], beside=mix_ahead(0, mixes[0]))
        project(c, time_mix[0][0], time_mix[1][0], *time_mix[0][1], beside=mix_ahead(2, mixes[1]))
        project(c, time_mix[1][0], time_mix[2][0], *time_mix[1][1], beside=mix_ahead(3, mixes[0]))
        project(c, time_mix[2][0], lora_w[0], *time_mix[2][1])
        project(c, lora_w[0], lora_a[0], *lora_w[1])
        project(c, lora_a[0], None, *lora_a[1])
        key_norms(c, k_out, c.region(8))
        A, B, bonus = c.region(1), c.region(2), c.region(8)
        decay_factors(c, r_out, k_out, v_out, c.region(6), c.region(7), bonus, A, B, 9)
        states, finals = (c.ring_words()[:, i * KT * P:(i + 1) * KT * P].rearrange("p (j n) -> p j n", j=KT) for i in range(2))
        n = 16 * 4 * P
        more = [c.flat(9, 6 * 4 * P, at=2 * T), c.ring_words()[:, 2 * KT * P:], c.high[:].rearrange("p s k n -> p (s k n)"),
                c.tile("more_words", [P, 2 * 4 * P])[:]]
        quads = [Quad([c.flat(6, n)], c.flat(6, 4 * L, at=n)), Quad(more, c.flat(6, 4 * L, at=n + 4 * L))]
        turning = c.region(6, t=P)
        for sample in (False, True):
            if sample:
                load_states(c, states, turning)
            wkv(c, quads, states, finals, A, B, r_out, k_out, v_out, A, sample)
            store_states(c, finals, turning, outs["sample_rwkv_wkv" if sample else "prompt_rwkv_wkv"])
        with c.stage() as block:
            @block.sync
            def _(sp):
                for s in range(RING):
                    load_unit(c, sp, lora_g[0], 0, s)
        out_parts = Parts(c, 4, 3)
        o_job = Job(KT, KT, columns(ins["rw_w_o"][0]), parts=lambda u: (out_parts.high, out_parts.low))
        project(c, lora_g[0], o_job, *lora_g[1])
        group_norm(c, A, bonus, c.region(6), out_parts, (9, 7))
        project(c, o_job, layer_jobs[1]["xq"][0], add_to(c, x), {})
        memory_attention(1, None)
        rms(c, "final_norm", x, h, c.vec["norm_final"])
        rows = outs["y_prompt"][0].rearrange("(g p) d -> g p d", p=P)
        store_rows(c, "y", h, c.region(2, k=5, t=D), [(g * P, P, rows[g]) for g in range(SEQ // P)] + [(SEQ, DEC, outs["y_sample"][0])])


_INS = ["x_prompt", "x_sample", "mem_prompt", "cache_sb_k", "cache_sb_v", "state_rwkv_wkv",
        "state_rwkv_shift", "cache_mem_k", "cache_mem_v", "norm_mix", "norm_xattn", "norm_ffn", "norm_mem",
        "norm_final", "sb_w_qkv", "sb_w_o", "rw_mu", "rw_w_r", "rw_w_k", "rw_w_v", "rw_w_o", "rw_w0",
        "rw_w1", "rw_w2", "rw_a0", "rw_a1", "rw_a2", "rw_g1", "rw_g2", "rw_k_k", "rw_k_a", "rw_r_k",
        "rw_lnx_w", "rw_lnx_b", "xa_w_q", "xa_w_kv", "xa_w_o", "ffn_w_gate_up", "ffn_w_down"]
_OUTS = [("y_prompt", (1, 512, 1024)), ("y_sample", (1, 32, 1024)), ("prompt_sb_k", (1, 1, 512, 16, 64)),
         ("prompt_sb_v", (1, 1, 512, 16, 64)), ("prompt_rwkv_wkv", (1, 1, 16, 64, 64)),
         ("prompt_rwkv_shift", (1, 1, 1024)), ("prompt_mem_k", (2, 1, 256, 4, 256)),
         ("prompt_mem_v", (2, 1, 256, 4, 256)), ("sample_sb_k", (1, 1, 32, 16, 64)),
         ("sample_sb_v", (1, 1, 32, 16, 64)), ("sample_rwkv_wkv", (1, 1, 16, 64, 64)),
         ("sample_rwkv_shift", (1, 1, 1024))]


def kernel(**inputs):
    import numpy as _np
    import concourse.bacc as _bacc
    from concourse import mybir as _mybir
    from concourse.bass_utils import run_bass_kernel_spmd as _run

    nc = _bacc.Bacc("TRN2", target_bir_lowering=False, num_devices=1)
    arrays, ins, outs = {}, {}, {}
    for name in _INS:
        a = _np.ascontiguousarray(inputs[name])
        arrays[f"in_{name}_dram"] = a
        ins[name] = nc.dram_tensor(f"in_{name}_dram", a.shape, _mybir.dt.from_np(a.dtype), kind="ExternalInput").ap()
    for name, shape in _OUTS:
        outs[name] = nc.dram_tensor(f"out_{name}_dram", shape, _mybir.dt.float32, kind="ExternalOutput").ap()
    build(nc, ins, outs)
    r = _run(nc, [arrays], core_ids=[0])
    return tuple(r.results[0][f"out_{name}_dram"] for name, _ in _OUTS)
```

```python
from contextlib import ExitStack, contextmanager

import numpy as np
import concourse.bass as bass
from concourse import mybir

F32 = mybir.dt.float32
F32R = mybir.dt.float32r
I32 = mybir.dt.int32
BF16 = mybir.dt.bfloat16
ALU = mybir.AluOpType
ACT = mybir.ActivationFunctionType
AX_X = mybir.AxisListType.X

P = 128
D = 1024
KT = D // P
SEQ = 512
DEC = 32
T = SEQ + DEC
HALF = T // 2
PAST = 1024
NMEM = 256
HD = 64
PAIRS = D // P
XH = 4
FF = 2816
FT = FF // P
DEPTH = 2
EPS = 1e-6
GN_EPS = 64e-5
L = 64
REGION = KT * T
RING = 4
UNIT_KT = 8
LORA = 64
GATE = 160
GK = GATE // 2
AHEAD = 2
SEMS_KEPT = 60
PRIMED = 1

ROWS_A = [("norm_mix", 16), ("norm_xattn", 16), ("norm_ffn", 16), ("norm_mem", 16), ("norm_final", 8),
          ("rw_w0", 8), ("rw_a0", 8), ("rw_k_k", 8), ("rw_k_a", 8), ("rw_r_k", 8), ("rw_lnx_w", 8), ("rw_lnx_b", 8)]
ROWS_B = [("rw_mu", 48), ("state_rwkv_shift", 8)]


class Job:

    def __init__(self, n, kt, src, moving=None, parts=None, kp=P, m=lambda u: P, slot=lambda u: u,
                 opens=lambda u: True, closes=lambda u: True, tokens=T, per=RING):
        self.n, self.src, self.moving, self.parts, self.kp, self.m = n, src, moving, parts, kp, m
        self.kt = kt if callable(kt) else lambda u: kt
        self.slot, self.opens, self.closes, self.tokens, self.per = slot, opens, closes, tokens, per
        self.iters = n // per
        self.ready = None
        self.rounds = per // RING


class Parts:

    def __init__(self, c, high, low, k=KT, t=T, high_at=0):
        self.high = c.region(high, k, t, high_at, F32R)
        self.full, self.low = c.region(low, k, t), c.region(low, k, t, dtype=F32R)


class Core:

    def __init__(self, nc, ctx, ins, outs):
        self.nc, self.ctx, self.ins, self.outs = nc, ctx, ins, outs
        self.base = self.base_of(nc)
        ctx.enter_context(nc.sbuf_tensor("arena", [P, 10 * REGION], F32))
        self.views = {}
        self.ring, self.ring_r = self.aliased("weight_ring", [P, RING, UNIT_KT, P])
        self.high, self.high_r = self.aliased("weights_high", [P, 2, UNIT_KT, P])
        self.psum = ctx.enter_context(nc.psum_tensor("psum", [P, 8, 512], F32))
        self.stages = 0
        self.stage_sems = []
        self.weights_landed = [nc.alloc_semaphore(f"weights_landed{s}") for s in range(RING)]
        self.weights_high = [nc.alloc_semaphore(f"weights_high{s}") for s in range(RING)]
        self.weights_split = [nc.alloc_semaphore(f"weights_split{s}") for s in range(RING)]
        self.splits = 0
        self.unit_done = [nc.alloc_semaphore(f"unit_done{s}") for s in range(RING)]
        self.slot_emptied = [nc.alloc_semaphore(f"slot_emptied{s}") for s in range(RING)]
        self.rounds = 0
        for sem in self.slot_emptied:
            nc.sync.sem_inc(sem, PRIMED)
        self.emptied = [PRIMED] * RING
        self.jobs = []

    @staticmethod
    def base_of(nc):
        return -(-nc.sbuf_base // 32) * 32

    def aliased(self, name, shape):
        offset = self.base_of(self.nc)
        plain = self.ctx.enter_context(self.nc.sbuf_tensor(name, shape, F32))
        return plain, self.nc.alloc_sbuf_tensor_at(name + "_r", shape, F32R, offset=offset)

    def sem(self, name, primed=False):
        self.stage_sems.append(self.nc.alloc_semaphore(f"{name}_{self.stages}"))
        if primed:
            self.nc.sync.sem_inc(self.stage_sems[-1], PRIMED)
        return self.stage_sems[-1]

    def free_semaphores(self):
        if self.stage_sems:
            self.nc.clear_and_free_semaphores(self.stage_sems)
            self.nc.all_engine_barrier()
            self.stage_sems = []

    @contextmanager
    def stage(self):
        with self.nc.Block() as block:
            yield block
        if len(self.stage_sems) > SEMS_KEPT:
            self.free_semaphores()
        self.stages += 1

    def tile(self, name, shape, dtype=F32):
        return self.ctx.enter_context(self.nc.sbuf_tensor(name, shape, dtype))

    def ring_words(self):
        return self.ring[:].rearrange("p s k n -> p (s k n)")

    def region(self, r, k=KT, t=T, at=0, dtype=F32):
        return self.flat(r, k * t, at, dtype).rearrange("p (k t) -> p k t", k=k)

    def flat(self, r, n, at=0, dtype=F32):
        a = r * REGION + at
        if (a, n, dtype) not in self.views:
            name = f"words_{a}_{n}" + ("_r" if dtype == F32R else "")
            self.views[a, n, dtype] = self.nc.alloc_sbuf_tensor_at(name, [P, n], dtype, offset=self.base + 4 * a, align_bytes=4)
        return self.views[a, n, dtype][:]


def take_high(c, high, full):
    return c.nc.vector.tensor_scalar(high, full, 1.0, None, ALU.mult)


def take_low(c, low, full, high):
    return c.nc.vector.tensor_tensor(low, full, high.bitcast(F32), ALU.subtract)


def load_unit(c, sp, job, it, u):
    s = u % RING
    sp.dma_start(c.ring[0:job.kp, s, 0:job.kt(u), 0:job.m(u)], job.src(it, u)).then_inc(c.weights_landed[s], 16)


def stream_weights(c, sp, job, nxt):
    base = c.rounds
    for u in range(RING, job.per):
        sp.wait_ge(c.unit_done[u % RING], base + u // RING)
        load_unit(c, sp, job, 0, u)
    if job.iters > 1:
        with sp.Fori(1, job.iters) as it:
            for u in range(job.per):
                sp.wait_ge(c.unit_done[u % RING], it * job.rounds + (base + u // RING))
                load_unit(c, sp, job, it, u)
    if nxt is not None:
        for u in range(RING):
            sp.wait_ge(c.unit_done[u], base + job.iters * job.rounds)
            load_unit(c, sp, nxt, 0, u)


def multiply_units(c, pe, job, norm=None):
    nc, base, splits = c.nc, c.rounds, c.splits
    w = job.tokens // 2 if job.tokens > 512 else job.tokens
    units = range(job.per)
    closes = [sum(job.slot(u) == q and job.closes(u) for u in units) for q in range(RING)]
    with pe.Fori(0, job.iters) as it:
        for u in units:
            s, q = u % RING, job.slot(u)
            if job.parts:
                pe.wait_ge(c.weights_split[s], it * job.rounds + (splits + u // RING + 1))
            else:
                pe.wait_ge(c.weights_landed[s], it * (16 * job.rounds) + 16 * (base + u // RING + 1))
            if norm and norm.meaned and u == RING - 1:
                pe.wait_ge(norm.meaned, 1)
            if job.ready and u in job.ready:
                pe.wait_ge(*job.ready[u])
            if job.opens(u):
                before = sum(job.slot(v) == q and job.closes(v) for v in range(u))
                pe.wait_ge(c.slot_emptied[q], it * closes[q] + (c.emptied[q] + before))
            if job.parts:
                high, low = c.high_r[:, s % 2], c.ring_r[:, s]
                x_high, x_low = job.parts(u)
                passes = [(high, x_high), (high, x_low), (low, x_high)]
            else:
                passes = [(c.ring[0:job.kp, s, :, 0:job.m(u)], job.moving(u))]
            n = job.kt(u)
            for k in range(n):
                if norm and u == 0:
                    pe.wait_ge(norm.low, k + 1)
                for h in range(job.tokens // w):
                    for i, (weights, x) in enumerate(passes):
                        last = nc.tensor.matmul(
                            c.psum[0:job.m(u), 2 * q + h, 0:w], weights[:, k, :], x[:, k, h * w:(h + 1) * w],
                            start=job.opens(u) and k == 0 and i == 0,
                            stop=job.closes(u) and k == n - 1 and i == len(passes) - 1)
            last.then_inc(c.unit_done[s], 1)


def split_unit(c, dve, job, it, u):
    s, n = u % RING, job.kt(u)
    full, low, high = c.ring[:, s, 0:n, :], c.ring_r[:, s, 0:n, :], c.high_r[:, s % 2, 0:n, :]
    dve.wait_ge(c.weights_landed[s], it * (16 * job.rounds) + 16 * (c.rounds + u // RING + 1))
    other = (s + 2) % RING
    done = it * job.rounds + (c.rounds + (u - 2 - other) // RING + 1)
    if not isinstance(done, int) or done > 0:
        dve.wait_ge(c.unit_done[other], done)
    split = it * job.rounds + (c.splits + u // RING + 1)
    take_high(c, high, full).then_inc(c.weights_high[s], 1)
    dve.wait_ge(c.weights_high[s], split)
    take_low(c, low, full, high).then_inc(c.weights_split[s], 1)


def split_and_empty(c, dve, job, emits, beside=None, norm=None):
    per = job.per
    for u in range(per):
        split_unit(c, dve, job, 0, u)
        if norm and u == 0:
            norm.vector(dve)
            norm.mean(dve)
        if norm and u == 1:
            norm.invert(dve)
        if beside is not None:
            beside(0, u)
        if u >= AHEAD and u - AHEAD in emits:
            emits[u - AHEAD](0)
    if job.iters > 1:
        with dve.Fori(1, job.iters) as it:
            for u in range(per):
                split_unit(c, dve, job, it, u)
                if beside is not None:
                    beside(it, u)
                v = u - AHEAD
                if v % per in emits:
                    emits[v % per](it if v >= 0 else it - 1)
    for u in range(per - AHEAD, per):
        if u in emits:
            emits[u](job.iters - 1)


class Split:

    def __init__(self, c, name, x):
        self.c, self.x, self.meaned = c, x, None
        self.high, self.low = c.sem(name + "_high"), c.sem(name + "_low")

    def scalar(self, act):
        for k in range(KT):
            self.c.nc.scalar.activation(self.x.high[:, k, :], self.x.full[:, k, :], ACT.Copy).then_inc(self.high, 1)

    def tensor(self, pe):
        pass

    def vector(self, dve):
        for k in range(KT):
            dve.wait_ge(self.high, k + 1)
            take_low(self.c, self.x.low[:, k, :], self.x.full[:, k, :], self.x.high[:, k, :]).then_inc(self.low, 1)

    def mean(self, dve):
        pass

    invert = mean


class Norm:

    def __init__(self, c, name, x, gain, parts, tokens=T):
        self.c, self.x, self.gain, self.parts, self.tokens = c, x, gain, parts, tokens
        self.w = tokens // 2 if tokens > 512 else tokens
        self.nb = tokens // self.w
        self.sq = c.flat(9, 4 * tokens).rearrange("p (k t) -> p k t", k=4)
        self.inv, self.root = c.flat(9, tokens, at=4 * T), c.flat(9, tokens, at=5 * T)
        self.squared, self.summed, self.gained = (c.sem(name + x) for x in ("_squared", "_summed", "_gained"))
        self.high, self.low = c.sem(name + "_high"), c.sem(name + "_low")
        self.meaned, self.rooted, self.inverted = (c.sem(name + x) for x in ("_meaned", "_rooted", "_inverted"))

    def inverse(self):
        return self.inv.rearrange("p (a b) -> p a b", a=self.nb) if self.nb > 1 else self.inv

    def scalar(self, act):
        nc = self.c.nc
        for k in range(KT + 1):
            if k < KT:
                if k >= 4:
                    act.wait_ge(self.summed, k - 3)
                nc.scalar.activation(self.sq[:, k % 4, :], self.x[:, k, :], ACT.Square).then_inc(self.squared, 1)
            if k >= 1:
                act.wait_ge(self.gained, k)
                nc.scalar.activation(self.parts.high[:, k - 1, :], self.parts.full[:, k - 1, :], ACT.Copy).then_inc(self.high, 1)
        act.wait_ge(self.meaned, 1)
        nc.scalar.activation(self.root, self.root, ACT.Sqrt).then_inc(self.rooted, 1)

    def tensor(self, pe):
        c = self.c
        for k in range(KT):
            pe.wait_ge(self.squared, k + 1)
            for b in range(self.nb):
                last = c.nc.tensor.matmul(c.psum[:, 6 + b, 0:self.w], c.ones[:], self.sq[:, k % 4, b * self.w:(b + 1) * self.w],
                                          start=k == 0, stop=k == KT - 1)
            last.then_inc(self.summed, 1)

    def vector(self, dve):
        for k in range(KT + 2):
            if k < KT:
                self.c.nc.vector.tensor_scalar(self.parts.full[:, k, :], self.x[:, k, :], self.gain[:, k:k + 1], None,
                                               ALU.mult).then_inc(self.gained, 1)
            j = k - 2
            if j >= 0:
                dve.wait_ge(self.high, j + 1)
                take_low(self.c, self.parts.low[:, j, :], self.parts.full[:, j, :], self.parts.high[:, j, :]).then_inc(self.low, 1)

    def mean(self, dve):
        c = self.c
        dve.wait_ge(self.summed, KT)
        root = self.root.rearrange("p (a b) -> p a b", a=self.nb)
        c.nc.vector.tensor_scalar(root, c.psum[:, 6:6 + self.nb, 0:self.w], 1.0 / D, EPS, ALU.mult, ALU.add).then_inc(self.meaned, 1)

    def invert(self, dve):
        dve.wait_ge(self.rooted, 1)
        self.c.nc.vector.reciprocal(self.inv, self.root).then_inc(self.inverted, 1)
        dve.wait_ge(self.inverted, 1)


def project(c, job, nxt, by_vector, by_scalar, beside=None, norm=None, by_pool=None, starts=None):
    nc, base = c.nc, c.rounds
    wide = job.tokens > 512

    def view(u):
        q = job.slot(u)
        if wide:
            return c.psum[0:job.m(u), 2 * q:2 * q + 2, 0:HALF]
        return c.psum[0:job.m(u), 2 * q, 0:job.tokens]

    def emptying(eng, emit, u):
        def run(it):
            eng.wait_ge(c.unit_done[u % RING], it * job.rounds + (base + u // RING + 1))
            emit(it, view(u)).then_inc(c.slot_emptied[job.slot(u)], 1)
        return run

    with c.stage() as block:
        @block.sync
        def _(sp):
            stream_weights(c, sp, job, nxt)

        @block.tensor
        def _(pe):
            if norm:
                norm.tensor(pe)
            multiply_units(c, pe, job, norm)

        if by_pool:
            @block.gpsimd
            def _(pool):
                by_pool(pool)

        @block.vector
        def _(dve):
            if job.parts:
                split_and_empty(c, dve, job, {u: emptying(dve, e, u) for u, e in by_vector.items()}, beside, norm)
            elif by_vector:
                with dve.Fori(0, job.iters) as it:
                    for u in sorted(by_vector):
                        emptying(dve, by_vector[u], u)(it)
            if beside is not None and not job.parts:
                for t in range(KT):
                    beside(0, t)

        @block.scalar
        def _(act):
            if starts:
                starts(act)
            if norm:
                norm.scalar(act)
            if by_scalar:
                with act.Fori(0, job.iters) as it:
                    for u in sorted(by_scalar):
                        emptying(act, by_scalar[u], u)(it)
    finish(c, job, list(by_vector) + list(by_scalar))


def finish(c, job, closing):
    for u in closing:
        c.emptied[job.slot(u)] += job.iters
    c.rounds += job.iters * job.rounds
    if job.parts:
        c.splits += job.iters * job.rounds


def halves(ap):
    return ap.rearrange("p o (a b) -> p (o a) b", a=2)


def copy_to(c, dst):
    nc = c.nc

    def emit(s):
        return lambda it, ps: nc.scalar.activation(halves(dst[:, bass.ds(it * RING + s, 1), :]), ps, ACT.Copy)
    return {}, {s: emit(s) for s in range(RING)}


def scaled_to(c, dst, norm, scale=1.0):
    nc = c.nc

    def emit(s):
        def run(it, ps):
            out = dst[:, bass.ds(it * RING + s, 1), :]
            out = halves(out) if dst.shape[-1] == T else out.rearrange("p o t -> p (o t)")
            return nc.vector.scalar_tensor_tensor(out=out, in0=ps, scalar=scale, in1=norm.inverse(), op0=ALU.mult, op1=ALU.mult)
        return run
    return {s: emit(s) for s in range(RING)}, {}


def add_to(c, x, units=(0, 1, 2, 3)):
    nc = c.nc

    def emit(i):
        def run(it, ps):
            out = halves(x[:, bass.ds(it * len(units) + i, 1), :])
            return nc.vector.tensor_tensor(out, ps, out, ALU.add)
        return run
    return {u: emit(i) for i, u in enumerate(units)}


def columns(w, kp=P):
    v = w.rearrange("(k p) m -> p k m", p=kp)
    return lambda it, s: v[:, :, bass.ds(it * (RING * P) + s * P, P)]


class Selects:

    def __init__(self, c, name):
        self.nc, self.done, self.steps = c.nc, c.sem(name), 0

    def step(self, pool, ins):
        ins.then_inc(self.done, 1)
        self.steps += 1
        pool.wait_ge(self.done, self.steps)

    def fill(self, pool, t, value):
        self.step(pool, self.nc.gpsimd.memset(t[:], value))

    def keep(self, pool, ap, pattern, op, base, mult):
        self.step(pool, self.nc.gpsimd.affine_select(out=ap, in_=ap, pattern=pattern, compare_op=op, fill=0.0,
                                                     base=base, channel_multiplier=mult))

    def same_block(self, pool, t, w):
        v = t[:].rearrange("p (b i) -> p b i", i=w)
        self.keep(pool, v, [[-w, P // w], [0, w]], ALU.is_ge, 0, 1)
        self.keep(pool, v, [[w, P // w], [0, w]], ALU.is_ge, w - 1, -1)


def constants(c, loads):
    nc = c.nc
    c.ident = c.tile("ident", [P, P])
    c.ones = c.tile("ones", [P, P])
    c.later = c.tile("later", [P, P])
    c.later_r, c.neg_ones_r = c.tile("later_r", [P, P], F32R), c.tile("neg_ones_r", [P, P], F32R)
    c.ident_bf = c.tile("ident_bf", [P, P], BF16)
    c.barred = c.tile("barred", [P, P], BF16)
    sel, cast = Selects(c, "constant_selected"), c.sem("constant_cast")

    with c.stage() as block:
        @block.scalar
        def _(act):
            loads(act)

        @block.gpsimd
        def _(pool):
            for t, v in ((c.ident, 1.0), (c.ones, 1.0), (c.later, -1.0)):
                sel.fill(pool, t, v)
            sel.keep(pool, c.ident[:], [[-1, P]], ALU.is_equal, 0, 1)
            sel.keep(pool, c.later[:], [[-1, P]], ALU.is_ge, 0, 1)

        @block.vector
        def _(dve):
            dve.wait_ge(sel.done, sel.steps)
            nc.vector.tensor_copy(c.ident_bf[:], c.ident[:]).then_inc(cast, 1)
            nc.vector.tensor_copy(c.later_r[:], c.later[:]).then_inc(cast, 1)
            nc.vector.tensor_scalar(c.neg_ones_r[:], c.ones[:], -1.0, None, ALU.mult).then_inc(cast, 1)
            nc.vector.tensor_scalar(c.barred[:], c.later[:], float(2 ** 100), None, ALU.mult).then_inc(cast, 1)
            dve.wait_ge(cast, 4)


def wkv_constants(c):
    c.head_ones = c.tile("head_ones", [P, P])
    c.in16_up = c.tile("in16_up", [P, P])
    c.in16_lo = c.tile("in16_lo", [P, P])
    c.to32_lo = c.tile("to32_lo", [P, P])
    c.to64_lo = c.tile("to64_lo", [P, P])
    c.strict_up = c.tile("strict_up", [P, P])
    c.incl_up = c.tile("incl_up", [P, L])
    sel = Selects(c, "mask_selected")

    def make(pool):
        for t in (c.head_ones, c.in16_up, c.in16_lo, c.to32_lo, c.to64_lo, c.strict_up, c.incl_up):
            sel.fill(pool, t, 1.0)
        sel.same_block(pool, c.head_ones, HD)
        sel.keep(pool, c.in16_up[:], [[1, P]], ALU.is_gt, 0, -1)
        sel.same_block(pool, c.in16_up, 16)
        sel.keep(pool, c.in16_lo[:], [[-1, P]], ALU.is_gt, 0, 1)
        sel.same_block(pool, c.in16_lo, 16)
        for t, w in ((c.to32_lo, 32), (c.to64_lo, 64)):
            v = t[:].rearrange("p (b h i) -> p b h i", h=2, i=w // 2)
            sel.keep(pool, v, [[0, P // w], [-1, 2], [0, w // 2]], ALU.is_ge, 0, 0)
            sel.same_block(pool, t, w)
            sel.keep(pool, v, [[-w, P // w], [0, 2], [0, w // 2]], ALU.is_ge, -(w // 2), 1)
        sel.keep(pool, c.strict_up[:], [[1, P]], ALU.is_gt, 0, -1)
        sel.same_block(pool, c.strict_up, L)
        sel.keep(pool, c.incl_up[0:L, :], [[1, L]], ALU.is_ge, 0, -1)
        sel.keep(pool, c.incl_up[L:P, :], [[1, L]], ALU.is_ge, 0, -1)
    return make


def vector_rows(c):
    return [c.flat(5, P), c.flat(5, P, at=P)[0:56, :]]


def stack_vectors(c, act, stack, landed):
    c.columns = c.tile("vector_columns", [P, P + 56])
    c.vec = {}
    c.vectors = 0
    for t, rows, base in ((stack[0], ROWS_A, 0), (stack[1], ROWS_B, P)):
        at = 0
        for name, k in rows:
            src = c.ins[name]
            dims = " ".join(f"d{i}" for i in range(len(src.shape)))
            src = src.rearrange(f"{dims} -> ({dims})").rearrange("(k p) -> k p", p=P)
            act.dma_start(t[at:at + k, :], src).then_inc(landed, 16)
            c.vec[name] = c.columns[:, base + at:base + at + k]
            at += k
            c.vectors += 1


def turn_vectors(c, stack, landed):
    nc = c.nc
    turned, copied = c.sem("vectors_turned"), c.sem("vectors_copied")
    with c.stage() as block:
        @block.tensor
        def _(pe):
            pe.wait_ge(landed, 16 * c.vectors)
            nc.tensor.transpose(c.psum[:, 0, 0:P], stack[0], c.ident[:])
            nc.tensor.transpose(c.psum[:, 0, P:P + 56], stack[1], c.ident[0:56, 0:56]).then_inc(turned, 1)

        @block.vector
        def _(dve):
            dve.wait_ge(turned, 1)
            nc.vector.tensor_copy(c.columns[:], c.psum[:, 0, 0:P + 56]).then_inc(copied, 1)
            dve.wait_ge(copied, 1)


def load_rows(act, groups, landed):
    for src, stage, dst in groups:
        n = src.shape[0]
        p = min(n, P)
        act.dma_start(stage[0:p, 0:max(1, n // P), :], src.rearrange("(m p) d -> p m d", p=p)).then_inc(landed, 16)


def load_turned(c, name, groups, landed=None):
    nc = c.nc
    started = landed is not None
    landed = landed or c.sem(name + "_landed")
    turned, copied = c.sem(name + "_turned"), c.sem(name + "_copied")
    steps = []
    for src, stage, dst in groups:
        n = src.shape[0]
        for m in range(max(1, n // P) if dst is not None else 0):
            for k in range(0, KT, 4):
                steps.append((stage[0:min(n, P), m, :], min(n, P), m, k, dst))
    with c.stage() as block:
        @block.scalar
        def _(act):
            if not started:
                load_rows(act, groups, landed)

        @block.tensor
        def _(pe):
            pe.wait_ge(landed, 16 * len(groups))
            for i, (st, p, m, k, dst) in enumerate(steps):
                if i >= 4:
                    pe.wait_ge(copied, i - 3)
                for j in range(4):
                    last = nc.tensor.transpose(c.psum[:, i % 4, j * P:j * P + p], st[:, (k + j) * P:(k + j + 1) * P],
                                               c.ident[0:p, 0:p])
                last.then_inc(turned, 1)

        @block.vector
        def _(dve):
            for i, (st, p, m, k, dst) in enumerate(steps):
                dve.wait_ge(turned, i + 1)
                nc.vector.tensor_copy(dst[:, k:k + 4, m * P:m * P + p],
                                      c.psum[:, i % 4, :].rearrange("p (j t) -> p j t", j=4)[:, :, 0:p]).then_inc(copied, 1)
            dve.wait_ge(copied, len(steps))


def rms(c, name, x, h, gain):
    nc = c.nc
    sq, inv, root = c.region(9, k=4), c.flat(9, T, at=4 * T), c.flat(9, T, at=5 * T)
    BY_VECTOR = (3, 7)
    squared = [c.sem(f"{name}_squared{k}") for k in range(KT)]
    meaned, rooted, inverted, scaled = (c.sem(name + x) for x in ("_meaned", "_rooted", "_inverted", "_scaled"))
    used = c.sem(name + "_square_used")

    nc.scalar.preload_act_table_set("sqrt_and_others")
    with c.stage() as block:
        @block.scalar
        def _(act):
            for k in range(KT):
                if k in BY_VECTOR:
                    continue
                if k >= 4:
                    act.wait_ge(used, k - 3)
                nc.scalar.activation(sq[:, k % 4, :], x[:, k, :], ACT.Square).then_inc(squared[k], 1)
            act.wait_ge(meaned, 1)
            nc.scalar.activation(root, root, ACT.Sqrt).then_inc(rooted, 1)

        @block.tensor
        def _(pe):
            for k in range(KT):
                pe.wait_ge(squared[k], 1)
                for b in range(2):
                    last = nc.tensor.matmul(c.psum[:, b, 0:HALF], c.ones[:], sq[:, k % 4, b * HALF:(b + 1) * HALF],
                                            start=k == 0, stop=k == KT - 1)
                last.then_inc(used, 1)

        @block.vector
        def _(dve):
            for k in BY_VECTOR:
                if k >= 4:
                    dve.wait_ge(used, k - 3)
                nc.vector.tensor_tensor(sq[:, k % 4, :], x[:, k, :], x[:, k, :], ALU.mult).then_inc(squared[k], 1)
            dve.wait_ge(used, KT)
            nc.vector.tensor_scalar(root.rearrange("p (a b) -> p a b", a=2), c.psum[:, 0:2, 0:HALF], 1.0 / D, EPS, ALU.mult, ALU.add).then_inc(meaned, 1)
            dve.wait_ge(rooted, 1)
            nc.vector.reciprocal(inv, root).then_inc(inverted, 1)
            dve.wait_ge(inverted, 1)
            for k in range(KT):
                nc.vector.scalar_tensor_tensor(out=h[:, k, :], in0=x[:, k, :], scalar=gain[:, k:k + 1], in1=inv,
                                               op0=ALU.mult, op1=ALU.mult).then_inc(scaled, 1)
            dve.wait_ge(scaled, KT)


SCORE_AT = {0: 0, 1: 512, 3: 896, 2: 1024}
SCORES = 1280
KEY_TILES = SEQ // P
PAST_TILES = PAST // P
EXP_CAP = 30.0
SAMPLE_SCORES = (PAST_TILES + 1) * 2 * DEC


def stick_breaking(c, q, k, v, o, scratch):
    nc, ins, outs = c.nc, c.ins, c.outs
    at = [0]

    def part(*shape, dtype=F32):
        n = int(np.prod(shape))
        ap = c.flat(scratch, n, at=at[0], dtype=dtype)
        at[0] += n
        return ap if len(shape) == 1 else ap.rearrange("p (a b) -> p a b", a=shape[0])

    k_pair, v_pair = part(T), part(T)
    q_pad = part(2, T)
    k_rows, v_rows, k_rows_new = part(KEY_TILES, P), part(KEY_TILES, P), part(P)
    past_k = part(PAST_TILES, P)
    past_v = part(PAST_TILES + 1, P)
    past_kt = part((PAST_TILES + 1) * P)
    es = [part(SCORES), part(SCORES), part(SAMPLE_SCORES)]
    sizes, sps, lows, highs = (SCORES, SCORES, SAMPLE_SCORES), [], [], []
    for n in sizes:
        lows.append(c.flat(scratch, n, at=at[0], dtype=F32R))
        sps.append(part(n))
        highs.append(part(n, dtype=F32R))
    flat_psum = c.psum[:].rearrange("p b n -> p (b n)")
    zs = [flat_psum[:, 3 * 512:3 * 512 + SCORES], flat_psum[:, 0:SCORES], flat_psum[:, 6 * 512:6 * 512 + SAMPLE_SCORES]]

    queries_staged = c.sem("queries_staged")
    zeroed, pair_staged = c.sem("pads_zeroed"), c.sem("pair_staged")
    past_k_landed, past_v_landed = c.sem("past_k_landed"), c.sem("past_v_landed")
    rows_turned, past_turned = c.sem("rows_turned"), c.sem("past_turned", primed=True)
    k_rows_ready, v_rows_ready, new_rows_ready = c.sem("k_rows_ready"), c.sem("v_rows_ready"), c.sem("new_rows_ready")
    past_kt_lo, past_kt_hi = c.sem("past_kt_lo"), c.sem("past_kt_hi")
    rows_stored = c.sem("rows_stored", primed=True)
    scored = [c.sem(f"scored{u}", primed=True) for u in range(3)]
    capped = [c.sem(f"scores_capped{u}") for u in range(3)]
    exp_taken = [c.sem(f"exp_taken{u}") for u in range(3)]
    log_taken = [c.sem(f"log_taken{u}") for u in range(3)]
    sp_ready = [c.sem(f"softplus_ready{u}") for u in range(3)]
    sp_high = [c.sem(f"softplus_high{u}") for u in range(3)]
    sp_split = [c.sem(f"softplus_split{u}") for u in range(3)]
    summed = [c.sem(f"sums_added{u}") for u in range(3)]
    w_ready = [c.sem(f"weights_ready{u}") for u in range(3)]
    o_done, o_copied = c.sem("o_done"), c.sem("o_copied", primed=True)
    so_done, so_copied = c.sem("sample_o_done", primed=True), c.sem("sample_o_copied", primed=True)

    def rows(ap, w):
        return ap.rearrange("l b (m p) h d -> (l b m) p (h d)", p=w)

    nc.scalar.preload_act_table_set("natural_log_exp_and_others")
    with c.stage() as block:
        @block.sync
        def _(sp):
            with sp.Fori(0, PAIRS) as it:
                cols = bass.ds(it * P, P)
                sp.wait_ge(past_turned, it * 2 + PRIMED)
                sp.dma_start(past_k, rows(ins["cache_sb_k"], P).rearrange("m p n -> p m n")[:, :, cols]).then_inc(past_k_landed, 16)
                sp.wait_ge(so_done, it + PRIMED)
                sp.dma_start(past_v[:, 0:PAST_TILES, :], rows(ins["cache_sb_v"], P).rearrange("m p n -> p m n")[:, :, cols]).then_inc(past_v_landed, 16)
                sp.wait_ge(k_rows_ready, it + 1)
                sp.dma_start(rows(outs["prompt_sb_k"], P).rearrange("m p n -> p m n")[:, :, cols], k_rows).then_inc(rows_stored, 16)
                sp.wait_ge(v_rows_ready, it + 1)
                sp.dma_start(rows(outs["prompt_sb_v"], P).rearrange("m p n -> p m n")[:, :, cols], v_rows).then_inc(rows_stored, 16)
                sp.wait_ge(new_rows_ready, it * 2 + 2)
                sp.dma_start(rows(outs["sample_sb_k"], DEC).rearrange("m p n -> p m n")[:, :, cols], k_rows_new[0:DEC, :].rearrange("p (o n) -> p o n", o=1)).then_inc(rows_stored, 16)
                sp.dma_start(rows(outs["sample_sb_v"], DEC).rearrange("m p n -> p m n")[:, :, cols], past_v[0:DEC, PAST_TILES:PAST_TILES + 1, :]).then_inc(rows_stored, 16)
            sp.wait_ge(rows_stored, PAIRS * 64 + PRIMED)

        @block.gpsimd
        def _(pool):
            nc.gpsimd.memset(q_pad, 0.0).then_inc(zeroed, 1)
            nc.gpsimd.memset(past_kt[:, PAST:], 0.0).then_inc(zeroed, 1)
            nc.gpsimd.memset(past_v[:, PAST_TILES, :], 0.0).then_inc(zeroed, 1)
            pool.wait_ge(zeroed, 3)
            with pool.Fori(0, PAIRS) as it:
                for u in range(3):
                    pool.wait_ge(scored[u], it + PRIMED)
                pair = lambda x: x[:, bass.ds(it, 1), :].rearrange("p o t -> p (o t)")
                nc.gpsimd.tensor_copy(k_pair, pair(k)).then_inc(pair_staged, 1)
                nc.gpsimd.tensor_copy(v_pair, pair(v)).then_inc(pair_staged, 1)
                nc.gpsimd.tensor_copy(past_kt[:, PAST:PAST + DEC], k[:, bass.ds(it, 1), SEQ:T].rearrange("p o t -> p (o t)")).then_inc(pair_staged, 1)

        @block.tensor
        def _(pe):
            with pe.Fori(0, PAIRS) as it:
                def scores(h):
                    for j in (0, 1, 3, 2):
                        a = SCORE_AT[j]
                        nc.tensor.matmul(zs[h][:, a:a + SEQ - j * P], k_pair[:, j * P:(j + 1) * P], q_pad[:, h, j * P:SEQ],
                                         start=j != 3, stop=False, skip_group_check=True)
                        last = nc.tensor.matmul(zs[h][:, a:a + P], c.ident_bf[:], c.barred[:], start=False, stop=False, skip_group_check=True)
                    last.then_inc(scored[h], 1)
                pe.wait_ge(pair_staged, it * 3 + 3)
                pe.wait_ge(queries_staged, it * 2 + 2)
                pe.wait_ge(o_copied, it + PRIMED)
                scores(0)
                for j in range(KEY_TILES):
                    last = nc.tensor.transpose(c.psum[:, 0, j * P:(j + 1) * P], k_pair[:, j * P:(j + 1) * P], c.ident[:])
                last.then_inc(rows_turned, 1)
                for j in range(KEY_TILES):
                    last = nc.tensor.transpose(c.psum[:, 1, j * P:(j + 1) * P], v_pair[:, j * P:(j + 1) * P], c.ident[:])
                last.then_inc(rows_turned, 1)
                nc.tensor.transpose(c.psum[0:DEC, 2, 0:P], k_pair[:, SEQ:T], c.ident[:])
                nc.tensor.transpose(c.psum[0:DEC, 2, P:2 * P], v_pair[:, SEQ:T], c.ident[:]).then_inc(rows_turned, 1)
                pe.wait_ge(past_k_landed, it * 16 + 16)
                pe.wait_ge(so_copied, it * 2 + PRIMED)
                for b in range(2):
                    for j in range(4):
                        last = nc.tensor.transpose(c.psum[:, 6 + b, j * P:(j + 1) * P], past_k[:, 4 * b + j, :], c.ident[:])
                    last.then_inc(past_turned, 1)
                pe.wait_ge(k_rows_ready, it + 1)
                pe.wait_ge(v_rows_ready, it + 1)
                pe.wait_ge(new_rows_ready, it * 2 + 2)
                scores(1)
                pe.wait_ge(past_kt_lo, it + 1)
                pe.wait_ge(past_kt_hi, it + 1)
                for j in range(PAST_TILES + 1):
                    last = nc.tensor.matmul(zs[2][:, j * 2 * DEC:(j + 1) * 2 * DEC], past_kt[:, j * P:(j + 1) * P], q_pad[:, :, SEQ:T],
                                            start=j in (0, PAST_TILES), stop=False, skip_group_check=True)
                for h in range(2):
                    a = PAST_TILES * 2 * DEC + h * DEC
                    last = nc.tensor.matmul(zs[2][:, a:a + DEC], c.ident_bf[:], c.barred[:, 0:DEC], start=False, stop=False, skip_group_check=True)
                last.then_inc(scored[2], 1)
                for h in range(2):
                    pe.wait_ge(sp_split[h], it + 1)
                    for j in (0, 1, 3, 2):
                        a, n = SCORE_AT[j], SEQ - j * P
                        for x in (highs[h], lows[h]):
                            last = nc.tensor.matmul(zs[h][:, a:a + n], c.later_r[:], x[:, a:a + n], start=False,
                                                    stop=j == KEY_TILES - 1 and x is lows[h], skip_group_check=True)
                            for i in range(j + 1, KEY_TILES):
                                b, m = SCORE_AT[i], SEQ - i * P
                                last = nc.tensor.matmul(zs[h][:, a + n - m:a + n], c.neg_ones_r[:], x[:, b:b + m], start=False,
                                                        stop=i == KEY_TILES - 1 and x is lows[h], skip_group_check=True)
                    last.then_inc(summed[h], 1)
                pe.wait_ge(sp_split[2], it + 1)
                for x in (highs[2], lows[2]):
                    nc.tensor.matmul(zs[2][:, 512:], c.later_r[:], x[:, 512:], start=False, stop=x is lows[2], skip_group_check=True)
                    nc.tensor.matmul(zs[2][:, 0:512], c.later_r[:], x[:, 0:512], start=False, stop=False, skip_group_check=True)
                    for j in range(1, PAST_TILES + 1):
                        n = min(PAST_TILES, PAST_TILES + 1 - j) * 2 * DEC
                        last = nc.tensor.matmul(zs[2][:, 0:n], c.neg_ones_r[:], x[:, j * 2 * DEC:j * 2 * DEC + n], start=False,
                                                stop=j == PAST_TILES and x is lows[2], skip_group_check=True)
                last.then_inc(summed[2], 1)
                for h in range(2):
                    r = slice(h * HD, (h + 1) * HD)
                    pe.wait_ge(w_ready[h], it + 1)
                    for j in range(KEY_TILES):
                        a = SCORE_AT[j]
                        last = nc.tensor.matmul(c.psum[r, 3, j * P:SEQ], v_rows[:, j, r], es[h][:, a:a + SEQ - j * P],
                                                start=j == 0, stop=j == KEY_TILES - 1, skip_group_check=True)
                last.then_inc(o_done, 1)
                pe.wait_ge(w_ready[2], it + 1)
                pe.wait_ge(past_v_landed, it * 16 + 16)
                for j in range(PAST_TILES + 1):
                    last = nc.tensor.matmul(c.psum[:, 7, 0:2 * DEC], past_v[:, j, :], es[2][:, j * 2 * DEC:(j + 1) * 2 * DEC],
                                            start=j == 0, stop=j == PAST_TILES)
                last.then_inc(so_done, 1)

        @block.vector
        def _(dve):
            with dve.Fori(0, PAIRS) as it:
                def cap(u):
                    dve.wait_ge(scored[u], it + 1 + PRIMED)
                    nc.vector.tensor_scalar(es[u], zs[u], EXP_CAP, None, ALU.min).then_inc(capped[u], 1)

                def softplus(u):
                    dve.wait_ge(log_taken[u], it + 1)
                    nc.vector.tensor_tensor(sps[u], zs[u], es[u], ALU.max).then_inc(sp_ready[u], 1)

                def low_part(u):
                    dve.wait_ge(sp_high[u], it + 1)
                    take_low(c, lows[u], sps[u], highs[u]).then_inc(sp_split[u], 1)
                cap(0)
                dve.wait_ge(rows_stored, it * 64 + PRIMED)
                dve.wait_ge(rows_turned, it * 3 + 2)
                nc.vector.tensor_copy(v_rows, c.psum[:, 1, :].rearrange("p (j n) -> p j n", j=4)).then_inc(v_rows_ready, 1)
                dve.wait_ge(past_turned, it * 2 + 1 + PRIMED)
                nc.vector.tensor_copy(past_kt[:, 0:512], c.psum[:, 6, :]).then_inc(past_kt_lo, 1)
                for step, u in ((softplus, 0), (cap, 1), (low_part, 0), (cap, 2), (softplus, 1), (low_part, 1),
                                (softplus, 2), (low_part, 2)):
                    step(u)
                dve.wait_ge(o_done, it + 1)
                nc.vector.tensor_scalar(o[:, bass.ds(it, 1), 0:SEQ].rearrange("p o t -> p (o t)"), c.psum[:, 3, :], 1.0, None, ALU.mult).then_inc(o_copied, 1)
                dve.wait_ge(so_done, it + 1 + PRIMED)
                for h in range(2):
                    r = slice(h * HD, (h + 1) * HD)
                    nc.vector.tensor_scalar(o[r, bass.ds(it, 1), SEQ:T].rearrange("p o t -> p (o t)"), c.psum[r, 7, h * DEC:(h + 1) * DEC],
                                            1.0, None, ALU.mult).then_inc(so_copied, 1)

        @block.scalar
        def _(act):
            act.wait_ge(zeroed, 3)
            with act.Fori(0, PAIRS) as it:
                for u in range(3):
                    act.wait_ge(scored[u], it + PRIMED)
                for h in range(2):
                    r = slice(h * HD, (h + 1) * HD)
                    nc.scalar.activation(q_pad[r, h, :], q[r, bass.ds(it, 1), :].rearrange("p o t -> p (o t)"), ACT.Copy,
                                         scale=HD ** -0.5).then_inc(queries_staged, 1)
                act.wait_ge(rows_stored, it * 64 + PRIMED)
                act.wait_ge(rows_turned, it * 3 + 1)
                nc.scalar.copy(k_rows, c.psum[:, 0, :].rearrange("p (j n) -> p j n", j=4)).then_inc(k_rows_ready, 1)
                act.wait_ge(rows_turned, it * 3 + 3)
                nc.scalar.copy(k_rows_new[0:DEC, :], c.psum[0:DEC, 2, 0:P]).then_inc(new_rows_ready, 1)
                nc.scalar.copy(past_v[0:DEC, PAST_TILES, :], c.psum[0:DEC, 2, P:2 * P]).then_inc(new_rows_ready, 1)
                def exp(u):
                    act.wait_ge(capped[u], it + 1)
                    nc.scalar.activation(es[u], es[u], ACT.Exp).then_inc(exp_taken[u], 1)

                def log(u):
                    act.wait_ge(exp_taken[u], it + 1)
                    nc.scalar.activation(es[u], es[u], ACT.Ln, bias=1.0).then_inc(log_taken[u], 1)

                def high_part(u):
                    act.wait_ge(sp_ready[u], it + 1)
                    nc.scalar.activation(highs[u], sps[u], ACT.Copy).then_inc(sp_high[u], 1)
                exp(0)
                log(0)
                act.wait_ge(past_turned, it * 2 + 2 + PRIMED)
                nc.scalar.copy(past_kt[:, 512:PAST], c.psum[:, 7, :]).then_inc(past_kt_hi, 1)
                for step, u in ((high_part, 0), (exp, 1), (log, 1), (exp, 2), (high_part, 1), (log, 2), (high_part, 2)):
                    step(u)
                for u in range(3):
                    act.wait_ge(summed[u], it + 1)
                    nc.scalar.activation(es[u], zs[u], ACT.Exp).then_inc(w_ready[u], 1)


def memory_rows(c, name, layer, kv, k_rows_all, stored):
    nc = c.nc
    turned, copied = c.sem(name + "_turned"), c.sem(name + "_copied")
    steps = [(m, f) for f in range(0, 2 * KT, 4) for m in range(NMEM // P)]
    with c.stage() as block:
        @block.tensor
        def _(pe):
            for i, (m, f) in enumerate(steps):
                if i >= 4:
                    pe.wait_ge(copied, i - 3)
                for j in range(4):
                    last = nc.tensor.transpose(c.psum[:, i % 4, j * P:(j + 1) * P], kv[:, f + j, m * P:(m + 1) * P], c.ident[:])
                last.then_inc(turned, 1)

        @block.vector
        def _(dve):
            for i, (m, f) in enumerate(steps):
                dve.wait_ge(turned, i + 1)
                nc.vector.tensor_copy(k_rows_all[:, m, f * P:(f + 4) * P], c.psum[:, i % 4, :]).then_inc(copied, 1)

        @block.sync
        def _(sp):
            half = len(steps) // 2
            for i, out in enumerate(("prompt_mem_k", "prompt_mem_v")):
                sp.wait_ge(copied, half * (i + 1))
                sp.dma_start(c.outs[out][layer, 0].rearrange("(m p) h d -> p m (h d)", p=P),
                             k_rows_all[:, :, i * D:(i + 1) * D]).then_inc(stored, 16)


def cross_attention(c, name, q, kv, kv_rows, s_kt, s_v, o, scratch, rows_stored):
    nc = c.nc
    MT = NMEM // P
    QT = SEQ // P
    at = [0]

    def part(*shape):
        n = int(np.prod(shape))
        ap = c.flat(scratch, n, at=at[0])
        at[0] += n
        return ap if len(shape) == 1 else ap.rearrange("p (a b) -> p a b", a=shape[0])

    class Head:

        def __init__(self, g):
            self.q, self.v, self.s_v = part(2, T), part(MT, 2 * P), part(MT, 2 * P)
            self.prob, self.prob_s = part(QT, NMEM), part(NMEM)[0:DEC, :]
            self.prob_t, self.prob_ts = part(MT, SEQ), part(MT, DEC)
            self.neg_max, self.total, self.inverse = part(QT + 1), part(QT + 1), part(QT + 1)
            bank = [c.psum[:, 4 * g + b, :] for b in range(4)]
            self.z = c.psum[:, 4 * g:4 * g + 2, :].rearrange("p b (i n) -> p (b i) n", i=2)
            self.wide = bank[0:2]
            self.z_s = bank[2][0:DEC, 0:NMEM]
            self.turned_s, self.o_s = bank[3][:, 0:MT * DEC], bank[3][:, MT * DEC:MT * DEC + 2 * DEC]
            self.sems = {}
            for x in ("q_staged", "v_staged", "s_v_staged", "scored", "maxed", "maxed_s", "exped", "exped_s", "inverted",
                      "scaled", "turned", "copied", "turned_s", "copied_s"):
                self.sems[x] = c.sem(f"{name}_{x}{g}")
            for x in ("scored_s", "weighed", "weighed_s", "o_copied", "o_s_copied"):
                self.sems[x] = c.sem(f"{name}_{x}{g}", primed=True)

    heads = [Head(g) for g in range(2)]
    assert at[0] <= 3 * REGION

    def s(x, g):
        return heads[g].sems[x]

    with c.stage() as block:
        @block.sync
        def _(sp):
            sp.wait_ge(rows_stored, 32)

        @block.gpsimd
        def _(pool):
            with pool.Fori(0, XH // 2) as it:
                for g, hd in enumerate(heads):
                    pool.wait_ge(s("scored_s", g), it + PRIMED)
                    nc.gpsimd.tensor_copy(hd.q, q[:, bass.ds(it * 4 + 2 * g, 2), :]).then_inc(s("q_staged", g), 1)
                for g, hd in enumerate(heads):
                    pool.wait_ge(s("weighed", g), it * 2 + PRIMED)
                    nc.gpsimd.tensor_copy(hd.v, kv_rows[:, :, bass.ds(it * 4 * P + (D + 2 * g * P), 2 * P)]).then_inc(s("v_staged", g), 1)
                    pool.wait_ge(s("weighed_s", g), it + PRIMED)
                    nc.gpsimd.tensor_copy(hd.s_v, s_v[:, :, bass.ds(it * 4 * P + 2 * g * P, 2 * P)]).then_inc(s("s_v_staged", g), 1)

        @block.tensor
        def _(pe):
            with pe.Fori(0, XH // 2) as it:
                def keys(t, g, kk):
                    return t[:, bass.ds(it * 4 + (2 * g + kk), 1), :].rearrange("p o n -> p (o n)")
                for g, hd in enumerate(heads):
                    pe.wait_ge(s("q_staged", g), it + 1)
                    pe.wait_ge(s("o_copied", g), it * 2 + PRIMED)
                    for i in range(QT):
                        for kk in range(2):
                            last = nc.tensor.matmul(hd.z[:, i, :], hd.q[:, kk, i * P:(i + 1) * P], keys(kv, g, kk),
                                                    start=kk == 0 and i % 2 == 0, stop=kk == 1, skip_group_check=True)
                    last.then_inc(s("scored", g), 1)
                    for kk in range(2):
                        last = nc.tensor.matmul(hd.z_s, hd.q[:, kk, SEQ:T], keys(s_kt, g, kk), start=kk == 0, stop=kk == 1)
                    last.then_inc(s("scored_s", g), 1)
                for g, hd in enumerate(heads):
                    pe.wait_ge(s("o_s_copied", g), it + PRIMED)
                    pe.wait_ge(s("scaled", g), it * (QT + 1) + QT + 1)
                    for m in range(MT):
                        for i in range(QT):
                            last = nc.tensor.transpose(hd.wide[m][:, i * P:(i + 1) * P], hd.prob[:, i, m * P:(m + 1) * P], c.ident[:])
                        last.then_inc(s("turned", g), 1)
                    for m in range(MT):
                        last = nc.tensor.transpose(hd.turned_s[:, m * DEC:(m + 1) * DEC], hd.prob_s[:, m * P:(m + 1) * P], c.ident[0:DEC, 0:DEC])
                    last.then_inc(s("turned_s", g), 1)
                for g, hd in enumerate(heads):
                    pe.wait_ge(s("copied", g), it * 2 + 2)
                    pe.wait_ge(s("v_staged", g), it + 1)
                    for e in range(2):
                        for m in range(MT):
                            last = nc.tensor.matmul(hd.wide[e], hd.v[:, m, e * P:(e + 1) * P], hd.prob_t[:, m, :],
                                                    start=m == 0, stop=m == MT - 1)
                        last.then_inc(s("weighed", g), 1)
                    pe.wait_ge(s("copied_s", g), it + 1)
                    pe.wait_ge(s("s_v_staged", g), it + 1)
                    for e in range(2):
                        for m in range(MT):
                            last = nc.tensor.matmul(hd.o_s[:, e * DEC:(e + 1) * DEC], hd.s_v[:, m, e * P:(e + 1) * P], hd.prob_ts[:, m, :],
                                                    start=m == 0 and e == 0, stop=m == MT - 1, skip_group_check=True)
                    last.then_inc(s("weighed_s", g), 1)

        @block.vector
        def _(dve):
            with dve.Fori(0, XH // 2) as it:
                for g, hd in enumerate(heads):
                    dve.wait_ge(s("scored", g), it + 1)
                    nc.vector.tensor_reduce(hd.neg_max[:, 0:QT], hd.z, AX_X, ALU.max, negate=True).then_inc(s("maxed", g), 1)
                    dve.wait_ge(s("scored_s", g), it + 1 + PRIMED)
                    nc.vector.tensor_reduce(hd.neg_max[0:DEC, QT:QT + 1], hd.z_s, AX_X, ALU.max, negate=True).then_inc(s("maxed_s", g), 1)
                for g, hd in enumerate(heads):
                    dve.wait_ge(s("exped", g), it * QT + QT)
                    nc.vector.reciprocal(hd.inverse[:, 0:QT], hd.total[:, 0:QT]).then_inc(s("inverted", g), 1)
                    dve.wait_ge(s("exped_s", g), it + 1)
                    nc.vector.reciprocal(hd.inverse[0:DEC, QT:QT + 1], hd.total[0:DEC, QT:QT + 1]).then_inc(s("inverted", g), 1)
                    dve.wait_ge(s("inverted", g), it * 2 + 2)
                    for i in range(QT):
                        nc.vector.tensor_scalar(hd.prob[:, i, :], hd.prob[:, i, :], hd.inverse[:, i:i + 1], None, ALU.mult).then_inc(s("scaled", g), 1)
                    nc.vector.tensor_scalar(hd.prob_s, hd.prob_s, hd.inverse[0:DEC, QT:QT + 1], None, ALU.mult).then_inc(s("scaled", g), 1)
                for g, hd in enumerate(heads):
                    dve.wait_ge(s("turned", g), it * 2 + 1)
                    nc.vector.tensor_copy(hd.prob_t[:, 0, :], hd.wide[0]).then_inc(s("copied", g), 1)
                for g, hd in enumerate(heads):
                    dve.wait_ge(s("weighed", g), it * 2 + 1 + PRIMED)
                    nc.vector.tensor_scalar(o[:, bass.ds(it * 4 + 2 * g, 1), 0:SEQ].rearrange("p o t -> p (o t)"), hd.wide[0],
                                            1.0, None, ALU.mult).then_inc(s("o_copied", g), 1)
                    dve.wait_ge(s("weighed_s", g), it + 1 + PRIMED)
                    nc.vector.tensor_scalar(o[:, bass.ds(it * 4 + 2 * g, 2), SEQ:T], hd.o_s.rearrange("p (e t) -> p e t", e=2),
                                            1.0, None, ALU.mult).then_inc(s("o_s_copied", g), 1)

        @block.scalar
        def _(act):
            with act.Fori(0, XH // 2) as it:
                for g, hd in enumerate(heads):
                    act.wait_ge(s("maxed", g), it + 1)
                    for i in range(QT):
                        nc.scalar.activation(hd.prob[:, i, :], hd.z[:, i, :], ACT.Exp, bias=hd.neg_max[:, i:i + 1],
                                             accum_out=hd.total[:, i:i + 1]).then_inc(s("exped", g), 1)
                    act.wait_ge(s("maxed_s", g), it + 1)
                    nc.scalar.activation(hd.prob_s, hd.z_s, ACT.Exp, bias=hd.neg_max[0:DEC, QT:QT + 1],
                                         accum_out=hd.total[0:DEC, QT:QT + 1]).then_inc(s("exped_s", g), 1)
                for g, hd in enumerate(heads):
                    act.wait_ge(s("turned", g), it * 2 + 2)
                    nc.scalar.copy(hd.prob_t[:, 1, :], hd.wide[1]).then_inc(s("copied", g), 1)
                    act.wait_ge(s("turned_s", g), it + 1)
                    nc.scalar.copy(hd.prob_ts, hd.turned_s.rearrange("p (m t) -> p m t", m=MT)).then_inc(s("copied_s", g), 1)
                for g, hd in enumerate(heads):
                    act.wait_ge(s("weighed", g), it * 2 + 2 + PRIMED)
                    nc.scalar.copy(o[:, bass.ds(it * 4 + (2 * g + 1), 1), 0:SEQ].rearrange("p o t -> p (o t)"), hd.wide[1]).then_inc(s("o_copied", g), 1)


def gate_and_up(c, name, job, nxt, norm, hidden, gated):
    nc, base = c.nc, c.rounds
    silu_taken, multiplied, high, low = (c.sem(name + x) for x in (
        "_silu_taken", "_multiplied", "_hidden_high", "_hidden_low"))

    def two(ap):
        return ap.rearrange("p (a b) -> p a b", a=2)

    def gate(i):
        def run(it):
            nc.vector.wait_ge(c.unit_done[2 * i], it + (base + 1))
            nc.vector.tensor_tensor(two(gated[:, i, :]), c.psum[:, 4 * i:4 * i + 2, 0:HALF], norm.inverse(),
                                    ALU.mult).then_inc(c.slot_emptied[2 * i], 1)
        return run

    def up(i):
        def run(it):
            full, tile_high, tile_low = (t[:, bass.ds(it * 2 + i, 1), :] for t in (hidden.full, hidden.high, hidden.low))
            nc.vector.wait_ge(c.unit_done[2 * i + 1], it + (base + 1))
            nc.vector.tensor_tensor(halves(full), c.psum[:, 4 * i + 2:4 * i + 4, 0:HALF], norm.inverse(),
                                    ALU.mult).then_inc(c.slot_emptied[2 * i + 1], 1)
            nc.vector.wait_ge(c.slot_emptied[2 * i + 1], it + (c.emptied[2 * i + 1] + 1))
            nc.vector.wait_ge(silu_taken, it * 2 + (i + 1))
            nc.vector.tensor_tensor(full, full, gated[:, i:i + 1, :], ALU.mult).then_inc(multiplied, 1)
            nc.vector.wait_ge(multiplied, it * 2 + (i + 1))
            take_high(c, tile_high, full).then_inc(high, 1)
            nc.vector.wait_ge(high, it * 2 + (i + 1))
            take_low(c, tile_low, full, tile_high).then_inc(low, 1)
        return run

    with c.stage() as block:
        @block.sync
        def _(sp):
            stream_weights(c, sp, job, nxt)

        @block.tensor
        def _(pe):
            norm.tensor(pe)
            multiply_units(c, pe, job, norm)

        @block.scalar
        def _(act):
            norm.scalar(act)
            with act.Fori(0, job.iters) as it:
                for i in range(2):
                    act.wait_ge(c.slot_emptied[2 * i], it + (c.emptied[2 * i] + 1))
                    nc.scalar.activation(gated[:, i, :], gated[:, i, :], ACT.Silu).then_inc(silu_taken, 1)

        @block.vector
        def _(dve):
            split_and_empty(c, dve, job, {0: gate(0), 1: up(0), 2: gate(1), 3: up(1)}, norm=norm)
            dve.wait_ge(low, job.iters * 2)
    finish(c, job, range(RING))


def token_shift(c, h, xx, mixes):
    nc = c.nc
    shift_rows = c.flat(9, 2 * P)[0:KT, :].rearrange("p (i n) -> p i n", i=2)
    shifted, mixed = c.sem("tokens_shifted"), c.sem("tokens_mixed")
    turned, copied, stored = c.sem("shift_turned"), c.sem("shift_copied"), c.sem("shift_stored")
    with c.stage() as block:
        @block.vector
        def _(dve):
            nc.vector.tensor_tensor(xx[:, 0:5, 1:T], h[:, 0:5, 0:T - 1], h[:, 0:5, 1:T], ALU.subtract).then_inc(shifted, 1)
            dve.wait_ge(shifted, 2)
            nc.vector.tensor_scalar(xx[:, :, 0:1], h[:, :, 0:1], -1.0, None, ALU.mult).then_inc(shifted, 1)
            nc.vector.tensor_tensor(xx[:, :, SEQ:SEQ + 1], c.vec["state_rwkv_shift"].rearrange("p (k o) -> p k o", o=1),
                                    h[:, :, SEQ:SEQ + 1], ALU.subtract).then_inc(shifted, 1)
            dve.wait_ge(shifted, 4)
            for m, out in mixes:
                mix_tokens(c, h, xx, m, out, mixed)
            dve.wait_ge(mixed, KT * len(mixes))

        @block.gpsimd
        def _(pool):
            nc.gpsimd.tensor_tensor(xx[:, 5:KT, 1:T], h[:, 5:KT, 0:T - 1], h[:, 5:KT, 1:T], ALU.subtract).then_inc(shifted, 1)

        @block.tensor
        def _(pe):
            for i, t in enumerate((SEQ - 1, T - 1)):
                last = nc.tensor.transpose(c.psum[0:KT, 0, i * P:(i + 1) * P], h[:, :, t], c.ident[:])
            last.then_inc(turned, 1)

        @block.scalar
        def _(act):
            act.wait_ge(turned, 1)
            nc.scalar.copy(shift_rows, c.psum[0:KT, 0, 0:2 * P].rearrange("p (i n) -> p i n", i=2)).then_inc(copied, 1)

        @block.sync
        def _(sp):
            sp.wait_ge(copied, 1)
            for i, out in enumerate(("prompt_rwkv_shift", "sample_rwkv_shift")):
                sp.dma_start(c.outs[out].rearrange("l b (k p) -> (l b k) p", p=P), shift_rows[:, i, :]).then_inc(stored, 16)
            sp.wait_ge(stored, 32)


def mix_tokens(c, h, xx, m, out, done):
    mu = c.vec["rw_mu"]
    for k in range(KT):
        c.nc.vector.scalar_tensor_tensor(out=out[:, k, :], in0=xx[:, k, :], scalar=mu[:, m * KT + k:m * KT + k + 1],
                                         in1=h[:, k, :], op0=ALU.mult, op1=ALU.add).then_inc(done, 1)


def key_norms(c, k, norm, scratch_at):
    nc = c.nc
    s = {x: c.sem("key_" + x, primed=x in ("summed", "bounded")) for x in ("squared", "summed", "bounded", "rooted")}
    sq = [c.flat(9, T, at=scratch_at + g * T) for g in range(2)]
    nc.scalar.preload_act_table_set("sqrt_and_others")
    with c.stage() as block:
        @block.scalar
        def _(act):
            with act.Fori(0, PAIRS // 2) as it:
                for g in range(2):
                    act.wait_ge(s["summed"], it * 2 + PRIMED)
                    nc.scalar.activation(sq[g], k[:, bass.ds(it * 2 + g, 1), :].rearrange("p o t -> p (o t)"), ACT.Square,
                                         scale=c.vec["rw_k_k"][:, bass.ds(it * 2 + g, 1)]).then_inc(s["squared"], 1)
            for p in range(PAIRS):
                act.wait_ge(s["bounded"], p + 1 + PRIMED)
                nc.scalar.activation(norm[:, p, :], norm[:, p, :], ACT.Sqrt).then_inc(s["rooted"], 1)

        @block.tensor
        def _(pe):
            with pe.Fori(0, PAIRS // 2) as it:
                for g in range(2):
                    pe.wait_ge(s["bounded"], it * 2 + PRIMED)
                    pe.wait_ge(s["squared"], it * 2 + (g + 1))
                    for b in range(2):
                        last = nc.tensor.matmul(c.psum[:, 2 * g + b, 0:HALF], c.head_ones[:], sq[g][:, b * HALF:(b + 1) * HALF], start=True, stop=True)
                    last.then_inc(s["summed"], 1)

        @block.vector
        def _(dve):
            with dve.Fori(0, PAIRS // 2) as it:
                for g in range(2):
                    dve.wait_ge(s["summed"], it * 2 + (g + 1 + PRIMED))
                    nc.vector.tensor_scalar(halves(norm[:, bass.ds(it * 2 + g, 1), :]), c.psum[:, 2 * g:2 * g + 2, 0:HALF],
                                            1e-24, None, ALU.max).then_inc(s["bounded"], 1)


def decay_factors(c, r, k, v, sw, a, inv, a_out, b_out):
    nc = c.nc
    G = 4
    c.chunk_decay = c.tile("chunk_decay", [P, PAIRS, SEQ // L + 1])
    c.one_minus_ka = c.tile("one_minus_ka", [P, KT])
    words = [c.ring_words()[:, i * T:(i + 1) * T] for i in range(7)] + [c.flat(9, T, at=(2 + i) * T) for i in range(6)]
    kk, kka, rk, goes_on = words[0:G], words[G:2 * G], words[2 * G:3 * G], words[3 * G]
    s = {x: c.sem("decay_" + x, primed=x in ("a_out", "b_out", "bonus", "kka", "bonus_sum")) for x in (
        "ready", "log", "cum", "prev", "e_cum", "e_prev", "e_neg", "kk", "kka", "kmul", "kmod", "rk",
        "bonus_sum", "bonus", "a_out", "b_out", "k", "r", "ends")}
    minus = -float(np.exp(-0.5))

    def tile(t, it, g):
        return t[:, bass.ds(it * G + g, 1), :].rearrange("p o t -> p (o t)")

    def col(name, it, g):
        return c.vec[name][:, bass.ds(it * G + g, 1)]

    def wait(eng, name, count):
        eng.wait_ge(s[name], count + (PRIMED if name in ("a_out", "b_out", "bonus", "kka", "bonus_sum") else 0))

    with c.stage() as block:
        @block.scalar
        def _(act):
            with act.Fori(0, PAIRS // G) as it:
                for g in range(G):
                    nc.scalar.activation(tile(sw, it, g), tile(sw, it, g), ACT.Copy, scale=minus).then_inc(s["log"], 1)
                for g in range(G):
                    wait(act, "prev", it * G + (g + 1))
                    nc.scalar.activation(tile(sw, it, g), tile(b_out, it, g), ACT.Exp, scale=-1.0).then_inc(s["e_neg"], 1)
                    wait(act, "e_neg", it * G + (g + 1))
                    nc.scalar.activation(tile(a_out, it, g), tile(a_out, it, g), ACT.Exp).then_inc(s["e_prev"], 1)
                    nc.scalar.activation(tile(b_out, it, g), tile(b_out, it, g), ACT.Exp).then_inc(s["e_cum"], 1)
                for g in range(G):
                    wait(act, "e_cum", it * G + (g + 1))
                    ends = tile(b_out, it, g)[:, 0:SEQ].rearrange("p (n l) -> p n l", l=L)[:, :, L - 1]
                    nc.scalar.copy(c.chunk_decay[:, bass.ds(it * G + g, 1), 0:SEQ // L].rearrange("p o n -> p (o n)"), ends).then_inc(s["ends"], 1)
                    nc.scalar.copy(c.chunk_decay[:, bass.ds(it * G + g, 1), SEQ // L:].rearrange("p o n -> p (o n)"), tile(b_out, it, g)[:, T - 1:T]).then_inc(s["ends"], 1)

        @block.gpsimd
        def _(pool):
            nc.gpsimd.memset(goes_on, 1.0).then_inc(s["ready"], 1)
            pool.wait_ge(s["ready"], 1)
            nc.gpsimd.memset(goes_on.rearrange("p (n l) -> p n l", l=DEC)[:, 0::2, 0], 0.0).then_inc(s["ready"], 1)
            with pool.Fori(0, PAIRS // G) as it:
                for g in range(G):
                    wait(pool, "cum", it * G + (g + 1))
                    nc.gpsimd.tensor_tensor(tile(a_out, it, g), tile(b_out, it, g), tile(sw, it, g), ALU.subtract).then_inc(s["prev"], 1)
                for g in range(G):
                    wait(pool, "rk", it * G + (g + 1))
                    wait(pool, "e_cum", it * G + (g + 1))
                    nc.gpsimd.tensor_tensor(tile(r, it, g), tile(r, it, g), tile(b_out, it, g), ALU.mult).then_inc(s["r"], 1)
                for g in range(G):
                    nc.gpsimd.tensor_tensor(tile(k, it, g), tile(k, it, g), tile(sw, it, g), ALU.mult).then_inc(s["k"], 1)

        @block.tensor
        def _(pe):
            with pe.Fori(0, PAIRS // G) as it:
                for g in range(G):
                    wait(pe, "rk", it * G + (g + 1))
                    wait(pe, "bonus", it * G)
                    for b in range(2):
                        last = nc.tensor.matmul(c.psum[:, 2 * g + b, 0:HALF], c.head_ones[:], rk[g][:, b * HALF:(b + 1) * HALF], start=True, stop=True)
                    last.then_inc(s["bonus_sum"], 1)

        @block.vector
        def _(dve):
            dve.wait_ge(s["ready"], 2)
            nc.vector.tensor_scalar(c.one_minus_ka[:], c.vec["rw_k_a"], -1.0, 1.0, ALU.mult, ALU.add).then_inc(s["ready"], 1)
            dve.wait_ge(s["ready"], 3)
            with dve.Fori(0, PAIRS // G) as it:
                wait(dve, "a_out", it * G)
                wait(dve, "b_out", it * G)
                wait(dve, "bonus_sum", it * G)
                for g in range(G):
                    wait(dve, "log", it * G + (g + 1))
                    nc.vector.tensor_tensor_scan(tile(b_out, it, g), goes_on, tile(sw, it, g), 0.0, ALU.mult, ALU.add).then_inc(s["cum"], 1)
                for g in range(G):
                    nc.vector.scalar_tensor_tensor(out=kk[g], in0=tile(k, it, g), scalar=col("rw_k_k", it, g), in1=tile(inv, it, g),
                                                   op0=ALU.mult, op1=ALU.mult).then_inc(s["kk"], 1)
                for g in range(G):
                    wait(dve, "kk", it * G + (g + 1))
                    nc.vector.tensor_tensor(kka[g], kk[g], tile(a, it, g), ALU.mult).then_inc(s["kka"], 1)
                for g in range(G):
                    wait(dve, "kka", it * G + (g + 1))
                    nc.vector.tensor_scalar(tile(a, it, g), tile(a, it, g), col("rw_k_a", it, g), c.one_minus_ka[:, bass.ds(it * G + g, 1)],
                                            ALU.mult, ALU.add).then_inc(s["kmul"], 1)
                for g in range(G):
                    wait(dve, "kmul", it * G + (g + 1))
                    nc.vector.tensor_tensor(tile(k, it, g), tile(k, it, g), tile(a, it, g), ALU.mult).then_inc(s["kmod"], 1)
                for g in range(G):
                    wait(dve, "kmod", it * G + (g + 1))
                    nc.vector.scalar_tensor_tensor(out=rk[g], in0=tile(r, it, g), scalar=col("rw_r_k", it, g), in1=tile(k, it, g),
                                                   op0=ALU.mult, op1=ALU.mult).then_inc(s["rk"], 1)
                for g in range(G):
                    wait(dve, "e_prev", it * G + (g + 1))
                    nc.vector.scalar_tensor_tensor(out=tile(a_out, it, g), in0=kk[g], scalar=-1.0, in1=tile(a_out, it, g),
                                                   op0=ALU.mult, op1=ALU.mult).then_inc(s["a_out"], 1)
                for g in range(G):
                    wait(dve, "bonus_sum", it * G + (g + 1))
                    nc.vector.tensor_tensor(halves(inv[:, bass.ds(it * G + g, 1), :]), c.psum[:, 2 * g:2 * g + 2, 0:HALF], halves(v[:, bass.ds(it * G + g, 1), :]),
                                            ALU.mult).then_inc(s["bonus"], 1)
                for g in range(G):
                    wait(dve, "r", it * G + (g + 1))
                    wait(dve, "ends", it * (2 * G) + (2 * g + 2))
                    wait(dve, "kka", it * G + (g + 1))
                    nc.vector.tensor_tensor(tile(b_out, it, g), kka[g], tile(sw, it, g), ALU.mult).then_inc(s["b_out"], 1)


class Quad:

    def __init__(self, spaces, tail):
        n = 4 * P
        buf = [w[:, i * n:(i + 1) * n].rearrange("p (j n) -> p j n", j=4)
               for w in spaces for i in range(w.shape[-1] // n)]
        (self.A, self.B, self.K, self.V, self.m16t, self.m16, self.to32, self.to64, self.q, self.ak,
         self.rbk, self.A_rows, self.B_rows, self.K_rows, self.V_rows, self.mv) = buf[0:16]
        self.R = tail.rearrange("p (j n) -> p j n", j=4)
        self.m2, self.m2t, self.m4, self.m4t, self.m8 = self.A, self.B, self.K, self.V, self.ak
        self.x, self.turned = self.m16, self.m16t
        self.Pa, self.U0, self.phi, self.Rh = self.A, self.B, self.K, self.mv[:, :, 0:L]


def wkv(c, quads, states, finals, A, B, R, K, V, y, sample):
    nc = c.nc
    n_it = 1 if sample else PAIRS
    names = ("zeroed ready_v ready_s ready_p ab_done am_done ak_done rbk_done am_copied m16t_ready m16_ready joins_ready "
             "ak_ready rbk_ready q0_ready rowsA_done rowsB_done rowsK_done rowsV_done rowsA rowsB rowsK rowsV m2_done m2_ready m2t_done m2t_ready "
             "mv_done mv_ready q_done q_ready m4_done m4_ready m4t_done m4t_ready m8_done m8_ready x_done x_ready "
             "turned_done turned_ready pa_done pa_ready u_done u_ready rh_done rh_ready phi_done phi_ready "
             "s_done s_ready y_done y_ready").split()
    s = [{x: c.sem(f"wkv{q}_{x}", primed=x in ("y_done", "s_ready", "y_ready")) for x in names} for q in range(2)]
    rows64 = [slice(0, HD), slice(HD, P)]

    def bank(q, b):
        return c.psum[:, 4 * q + b, :].rearrange("p (j n) -> p j n", j=4)

    def tokens(t, it, q, rows):
        if sample:
            return t[rows, 4 * q:4 * q + 4, SEQ:T]
        return t[rows, bass.ds(it, 1), q * 4 * L:(q + 1) * 4 * L].rearrange("p o (j n) -> p (o j) n", j=4)
    W = DEC if sample else L

    def loop(eng, body):
        if sample:
            body(0)
        else:
            with eng.Fori(0, n_it) as it:
                body(it)

    with c.stage() as block:
        @block.gpsimd
        def _(pool):
            for q in range(2):
                for t in (quads[q].A, quads[q].B, quads[q].K, quads[q].V, quads[q].R):
                    nc.gpsimd.memset(t, 0.0).then_inc(s[q]["zeroed"], 1)
            if not sample:
                nc.gpsimd.memset(states[:, 0, :], 0.0).then_inc(s[0]["zeroed"], 1)
            pool.wait_ge(s[0]["zeroed"], 5 if sample else 6)
            pool.wait_ge(s[1]["zeroed"], 5)

            def body(it):
                for q in range(2):
                    z = quads[q]
                    pool.wait_ge(s[q]["y_done"], it + PRIMED)
                    nc.gpsimd.tensor_copy(z.R[:, :, 0:W], tokens(R, it, q, slice(0, P))).then_inc(s[q]["ready_p"], 1)
                for q in range(2):
                    z = quads[q]
                    pool.wait_ge(s[q]["m16t_ready"], it + 1)
                    nc.gpsimd.tensor_tensor(z.q, z.m16t, c.ident[:].rearrange("p (o n) -> p o n", o=1).broadcast_to([P, 4, P]), ALU.add).then_inc(s[q]["q0_ready"], 1)
                for q in range(2):
                    z = quads[q]
                    pool.wait_ge(s[q]["am_copied"], it + 1)
                    nc.gpsimd.tensor_tensor(z.to64, z.to32, c.to64_lo[:].rearrange("p (o n) -> p o n", o=1).broadcast_to([P, 4, P]), ALU.mult).then_inc(s[q]["joins_ready"], 1)
                    pool.wait_ge(s[q]["joins_ready"], it * 2 + 1)
                    nc.gpsimd.tensor_tensor(z.to32, z.to32, c.to32_lo[:].rearrange("p (o n) -> p o n", o=1).broadcast_to([P, 4, P]), ALU.mult).then_inc(s[q]["joins_ready"], 1)
            loop(pool, body)

        @block.vector
        def _(dve):
            def spread(m, n=P):
                return m[:].rearrange("p (o n) -> p o n", o=1).broadcast_to([P, 4, n])

            def body(it):
                for q in range(2):
                    z, e = quads[q], s[q]
                    dve.wait_ge(e["zeroed"], 5)
                    dve.wait_ge(e["y_done"], it + PRIMED)
                    for src, dst in ((A, z.A), (B, z.B)):
                        for h, r in enumerate(rows64):
                            nc.vector.tensor_scalar(dst[r, :, h * L:h * L + W], tokens(src, it, q, r), 1.0, None, ALU.mult).then_inc(e["ready_v"], 1)
                for q in range(2):
                    z, e = quads[q], s[q]
                    dve.wait_ge(e["ab_done"], it + 1)
                    nc.vector.tensor_tensor(z.m16t, bank(q, 0), spread(c.in16_up), ALU.mult).then_inc(e["m16t_ready"], 1)
                    dve.wait_ge(e["am_done"], it + 1)
                    dve.wait_ge(e["am_copied"], it + 1)
                    nc.vector.tensor_tensor(z.m16, bank(q, 1), spread(c.in16_lo), ALU.mult).then_inc(e["m16_ready"], 1)
                    dve.wait_ge(e["ak_done"], it + 1)
                    nc.vector.tensor_tensor(z.ak, bank(q, 2), spread(c.strict_up), ALU.mult).then_inc(e["ak_ready"], 1)
                    dve.wait_ge(e["rbk_done"], it + 1)
                    nc.vector.tensor_tensor(z.rbk.rearrange("p j (u n) -> p (j u) n", u=2), bank(q, 3).rearrange("p j (u n) -> p (j u) n", u=2),
                                            c.incl_up[:].rearrange("p (o n) -> p o n", o=1).broadcast_to([P, 8, L]), ALU.mult).then_inc(e["rbk_ready"], 1)
                for q in range(2):
                    z, e = quads[q], s[q]
                    dve.wait_ge(e["rowsK_done"], it + 1)
                    nc.vector.tensor_copy(z.K_rows, bank(q, 2)).then_inc(e["rowsK"], 1)
                for q in range(2):
                    z, e = quads[q], s[q]
                    dve.wait_ge(e["m2_done"], it + 1)
                    nc.vector.tensor_copy(z.m2, bank(q, 0)).then_inc(e["m2_ready"], 1)

                def add_q(step):
                    for q in range(2):
                        z, e = quads[q], s[q]
                        dve.wait_ge(e["q0_ready"], it + 1)
                        dve.wait_ge(e["q_done"], it * 5 + step)
                        nc.vector.tensor_tensor(z.q, bank(q, 3), z.q, ALU.add).then_inc(e["q_ready"], 1)
                add_q(1)
                for q in range(2):
                    z, e = quads[q], s[q]
                    dve.wait_ge(e["m4t_done"], it + 1)
                    nc.vector.tensor_copy(z.m4t, bank(q, 1)).then_inc(e["m4t_ready"], 1)
                add_q(2)
                add_q(3)
                for join in range(2):
                    for q in range(2):
                        z, e = quads[q], s[q]
                        dve.wait_ge(e["turned_done"], it * 2 + join + 1)
                        nc.vector.tensor_copy(z.turned, bank(q, 1)).then_inc(e["turned_ready"], 1)
                    add_q(4 + join)
                for q in range(2):
                    z, e = quads[q], s[q]
                    dve.wait_ge(e["u_done"], it + 1)
                    nc.vector.tensor_copy(z.U0, bank(q, 1)).then_inc(e["u_ready"], 1)
                for q in range(2):
                    z, e = quads[q], s[q]
                    dve.wait_ge(e["phi_done"], it + 1)
                    nc.vector.tensor_tensor(z.phi, bank(q, 3), spread(c.ident), ALU.add).then_inc(e["phi_ready"], 1)
                    dve.wait_ge(e["rh_done"], it + 1)
                    nc.vector.tensor_tensor(z.Rh, bank(q, 2)[:, :, 0:L], z.R, ALU.add).then_inc(e["rh_ready"], 1)
                for q in range(2):
                    z, e = quads[q], s[q]
                    dve.wait_ge(e["y_done"], it + 1 + PRIMED)
                    out = tokens(y, it, q, slice(0, P))
                    nc.vector.tensor_scalar(out, bank(q, 1)[:, :, 0:W], 1.0, None, ALU.mult).then_inc(e["y_ready"], 1)
            loop(dve, body)

        @block.scalar
        def _(act):
            def body(it):
                for q in range(2):
                    z, e = quads[q], s[q]
                    act.wait_ge(e["zeroed"], 5)
                    act.wait_ge(e["y_done"], it + PRIMED)
                    for src, dst in ((K, z.K), (V, z.V)):
                        for h, r in enumerate(rows64):
                            nc.scalar.copy(dst[r, :, h * L:h * L + W], tokens(src, it, q, r)).then_inc(e["ready_s"], 1)
                for q in range(2):
                    z, e = quads[q], s[q]
                    act.wait_ge(e["am_done"], it + 1)
                    nc.scalar.copy(z.to32, bank(q, 1)).then_inc(e["am_copied"], 1)
                for q in range(2):
                    z, e = quads[q], s[q]
                    act.wait_ge(e["rowsA_done"], it + 1)
                    nc.scalar.copy(z.A_rows, bank(q, 0)).then_inc(e["rowsA"], 1)
                    act.wait_ge(e["rowsB_done"], it + 1)
                    nc.scalar.copy(z.B_rows, bank(q, 1)).then_inc(e["rowsB"], 1)
                    act.wait_ge(e["rowsV_done"], it + 1)
                    nc.scalar.copy(z.V_rows, bank(q, 3)).then_inc(e["rowsV"], 1)
                for q in range(2):
                    z, e = quads[q], s[q]
                    act.wait_ge(e["mv_done"], it + 1)
                    nc.scalar.copy(z.mv, bank(q, 2)).then_inc(e["mv_ready"], 1)
                    act.wait_ge(e["m2t_done"], it + 1)
                    nc.scalar.copy(z.m2t, bank(q, 1)).then_inc(e["m2t_ready"], 1)
                for q in range(2):
                    z, e = quads[q], s[q]
                    act.wait_ge(e["m4_done"], it + 1)
                    nc.scalar.copy(z.m4, bank(q, 0)).then_inc(e["m4_ready"], 1)
                for q in range(2):
                    z, e = quads[q], s[q]
                    act.wait_ge(e["m8_done"], it + 1)
                    nc.scalar.copy(z.m8, bank(q, 0)).then_inc(e["m8_ready"], 1)
                for join in range(2):
                    for q in range(2):
                        z, e = quads[q], s[q]
                        act.wait_ge(e["x_done"], it * 2 + join + 1)
                        nc.scalar.copy(z.x, bank(q, 0)).then_inc(e["x_ready"], 1)
                for q in range(2):
                    z, e = quads[q], s[q]
                    act.wait_ge(e["pa_done"], it + 1)
                    nc.scalar.copy(z.Pa, bank(q, 0)).then_inc(e["pa_ready"], 1)
                for q in range(2):
                    e = s[q]
                    for j in range(4):
                        act.wait_ge(e["s_done"], it * 4 + j + 1)
                        unit = 4 * q + j
                        if sample:
                            out, decay = finals[:, unit, :], c.chunk_decay[:, unit, SEQ // L:]
                        else:
                            out = states[:, unit + 1, :] if unit < 7 else finals[:, bass.ds(it, 1), :].rearrange("p o n -> p (o n)")
                            decay = c.chunk_decay[:, bass.ds(it, 1), unit:unit + 1].rearrange("p a b -> p (a b)")
                        nc.scalar.activation(out, bank(q, 0)[:, j, :], ACT.Copy, scale=decay).then_inc(e["s_ready"], 1)
            loop(act, body)

        @block.tensor
        def _(pe):
            mm, tr = nc.tensor.matmul, nc.tensor.transpose

            def four(dst, lhs, rhs):
                for j in range(4):
                    last = mm(dst[:, j, :], lhs[:, j, :], rhs[:, j, :], start=j == 0, stop=True, skip_group_check=True)
                return last

            def turn(dst, src):
                for j in range(4):
                    last = tr(dst[:, j, :], src[:, j, :], c.ident[:])
                return last

            def body(it):
                for q in range(2):
                    z, e = quads[q], s[q]
                    pe.wait_ge(e["ready_v"], it * 4 + 4)
                    pe.wait_ge(e["s_ready"], it * 4 + PRIMED)
                    pe.wait_ge(e["y_ready"], it + PRIMED)
                    four(bank(q, 0), z.B, z.A).then_inc(e["ab_done"], 1)
                    four(bank(q, 1), z.A, z.B).then_inc(e["am_done"], 1)
                    pe.wait_ge(e["ready_s"], it * 4 + 4)
                    pe.wait_ge(e["ready_p"], it + 1)
                    four(bank(q, 2), z.K, z.A).then_inc(e["ak_done"], 1)
                    for j in range(4):
                        mm(bank(q, 3)[:, j, 0:L], z.B[:, j, :], z.R[:, j, :], start=j == 0, stop=True, skip_group_check=True)
                        last = mm(bank(q, 3)[:, j, L:P], z.K[:, j, :], z.R[:, j, :], start=False, stop=True, skip_group_check=True)
                    last.then_inc(e["rbk_done"], 1)
                for q in range(2):
                    z, e = quads[q], s[q]
                    pe.wait_ge(e["m16t_ready"], it + 1)
                    turn(bank(q, 0), z.A).then_inc(e["rowsA_done"], 1)
                    pe.wait_ge(e["m16_ready"], it + 1)
                    turn(bank(q, 1), z.B).then_inc(e["rowsB_done"], 1)
                    pe.wait_ge(e["ak_ready"], it + 1)
                    turn(bank(q, 2), z.K).then_inc(e["rowsK_done"], 1)
                    pe.wait_ge(e["rbk_ready"], it + 1)
                    turn(bank(q, 3), z.V).then_inc(e["rowsV_done"], 1)
                for q in range(2):
                    z, e = quads[q], s[q]
                    pe.wait_ge(e["rowsA"], it + 1)
                    four(bank(q, 0), z.m16t, z.m16).then_inc(e["m2_done"], 1)
                    pe.wait_ge(e["rowsB"], it + 1)
                    four(bank(q, 1), z.m16, z.m16t).then_inc(e["m2t_done"], 1)
                    pe.wait_ge(e["rowsV"], it + 1)
                    pe.wait_ge(e["rowsK"], it + 1)
                    four(bank(q, 2), z.ak, z.V_rows).then_inc(e["mv_done"], 1)
                for q in range(2):
                    z, e = quads[q], s[q]
                    pe.wait_ge(e["m2_ready"], it + 1)
                    pe.wait_ge(e["q0_ready"], it + 1)
                    four(bank(q, 3), z.m2, z.q).then_inc(e["q_done"], 1)
                    pe.wait_ge(e["m2t_ready"], it + 1)
                    four(bank(q, 0), z.m2t, z.m2).then_inc(e["m4_done"], 1)
                    four(bank(q, 1), z.m2, z.m2t).then_inc(e["m4t_done"], 1)
                for q in range(2):
                    z, e = quads[q], s[q]
                    pe.wait_ge(e["m4_ready"], it + 1)
                    pe.wait_ge(e["q_ready"], it * 5 + 1)
                    four(bank(q, 3), z.m4, z.q).then_inc(e["q_done"], 1)
                    pe.wait_ge(e["m4t_ready"], it + 1)
                    pe.wait_ge(e["mv_ready"], it + 1)
                    four(bank(q, 0), z.m4t, z.m4).then_inc(e["m8_done"], 1)
                for q in range(2):
                    z, e = quads[q], s[q]
                    pe.wait_ge(e["m8_ready"], it + 1)
                    pe.wait_ge(e["q_ready"], it * 5 + 2)
                    four(bank(q, 3), z.m8, z.q).then_inc(e["q_done"], 1)
                for join in range(2):
                    for q in range(2):
                        z, e = quads[q], s[q]
                        pe.wait_ge(e["q_ready"], it * 5 + 3 + join)
                        pe.wait_ge(e["joins_ready"], it * 2 + 2)
                        turn(bank(q, 1), z.q).then_inc(e["turned_done"], 1)
                        four(bank(q, 0), (z.to32, z.to64)[join], z.q).then_inc(e["x_done"], 1)
                    for q in range(2):
                        z, e = quads[q], s[q]
                        pe.wait_ge(e["x_ready"], it * 2 + join + 1)
                        pe.wait_ge(e["turned_ready"], it * 2 + join + 1)
                        four(bank(q, 3), z.turned, z.x).then_inc(e["q_done"], 1)
                for q in range(2):
                    z, e = quads[q], s[q]
                    pe.wait_ge(e["q_ready"], it * 5 + 5)
                    four(bank(q, 0), z.q, z.A_rows).then_inc(e["pa_done"], 1)
                    pe.wait_ge(e["mv_ready"], it + 1)
                    four(bank(q, 1), z.q, z.mv).then_inc(e["u_done"], 1)
                for q in range(2):
                    z, e = quads[q], s[q]
                    pe.wait_ge(e["pa_ready"], it + 1)
                    four(bank(q, 3), z.Pa, z.B_rows).then_inc(e["phi_done"], 1)
                    for j in range(4):
                        last = mm(bank(q, 2)[:, j, 0:L], z.Pa[:, j, :], z.rbk[:, j, 0:L], start=j == 0, stop=True, skip_group_check=True)
                    last.then_inc(e["rh_done"], 1)
                for q in range(2):
                    z, e = quads[q], s[q]
                    pe.wait_ge(e["u_ready"], it + 1)
                    for j in range(4):
                        mm(bank(q, 0)[:, j, :], z.B_rows[:, j, :], z.U0[:, j, :], start=j == 0, stop=False, skip_group_check=True)
                        mm(bank(q, 0)[:, j, :], z.K_rows[:, j, :], z.V_rows[:, j, :], start=False, stop=False, skip_group_check=True)
                for q in range(2):
                    z, e = quads[q], s[q]
                    pe.wait_ge(e["phi_ready"], it + 1)
                    pe.wait_ge(e["rh_ready"], it + 1)
                    for j in range(4):
                        state = states[:, 4 * q + j, :]
                        if j:
                            pe.wait_ge(e["s_ready"], it * 4 + j + PRIMED)
                        elif q and not sample:
                            pe.wait_ge(s[0]["s_ready"], it * 4 + 4 + PRIMED)
                        mm(bank(q, 0)[:, j, :], z.phi[:, j, :], state, start=False, stop=True, skip_group_check=True).then_inc(e["s_done"], 1)
                        mm(bank(q, 1)[:, j, 0:L], z.U0[:, j, :], z.rbk[:, j, 0:L], start=j == 0, stop=False, skip_group_check=True)
                        mm(bank(q, 1)[:, j, 0:L], z.V_rows[:, j, :], z.rbk[:, j, L:P], start=False, stop=False, skip_group_check=True)
                        last = mm(bank(q, 1)[:, j, 0:L], state, z.Rh[:, j, :], start=False, stop=True, skip_group_check=True)
                    last.then_inc(e["y_done"], 1)
            pe.wait_ge(s[0]["zeroed"], 5 if sample else 6)
            loop(pe, body)


def load_states(c, states, stage):
    nc = c.nc
    zeroed, landed, turned, copied = (c.sem("state_" + x) for x in ("zeroed", "landed", "turned", "copied"))
    with c.stage() as block:
        @block.gpsimd
        def _(pool):
            nc.gpsimd.memset(stage, 0.0).then_inc(zeroed, 1)

        @block.sync
        def _(sp):
            sp.wait_ge(zeroed, 1)
            heads = c.ins["state_rwkv_wkv"][0, 0].rearrange("(p h) i j -> h i p j", h=2)
            for h in range(2):
                sp.dma_start(stage[h * HD:(h + 1) * HD, :, h * HD:(h + 1) * HD], heads[h]).then_inc(landed, 16)

        @block.tensor
        def _(pe):
            pe.wait_ge(landed, 32)
            for b in range(2):
                for j in range(4):
                    last = nc.tensor.transpose(c.psum[:, b, j * P:(j + 1) * P], stage[:, 4 * b + j, :], c.ident[:])
                last.then_inc(turned, 1)

        @block.vector
        def _(dve):
            for b in range(2):
                dve.wait_ge(turned, b + 1)
                nc.vector.tensor_copy(states[:, 4 * b:4 * b + 4, :], c.psum[:, b, :].rearrange("p (j n) -> p j n", j=4)).then_inc(copied, 1)
            dve.wait_ge(copied, 2)


def store_states(c, finals, stage, out):
    nc = c.nc
    turned, copied, stored = (c.sem("final_" + x) for x in ("turned", "copied", "stored"))
    with c.stage() as block:
        @block.tensor
        def _(pe):
            for b in range(2):
                for j in range(4):
                    last = nc.tensor.transpose(c.psum[:, b, j * P:(j + 1) * P], finals[:, 4 * b + j, :], c.ident[:])
                last.then_inc(turned, 1)

        @block.vector
        def _(dve):
            for b in range(2):
                dve.wait_ge(turned, b + 1)
                nc.vector.tensor_copy(stage[:, 4 * b:4 * b + 4, :], c.psum[:, b, :].rearrange("p (j n) -> p j n", j=4)).then_inc(copied, 1)

        @block.sync
        def _(sp):
            sp.wait_ge(copied, 2)
            heads = out[0, 0].rearrange("(p h) i j -> h i p j", h=2)
            for h in range(2):
                sp.dma_start(heads[h], stage[h * HD:(h + 1) * HD, :, h * HD:(h + 1) * HD]).then_inc(stored, 16)
            sp.wait_ge(stored, 32)


def head_selectors(c, gather, spread):
    sel = Selects(c, "selector_made")

    def make(pool):
        sel.step(pool, c.nc.gpsimd.memset(gather, 1.0))
        sel.step(pool, c.nc.gpsimd.memset(spread, 1.0))
        v = gather.rearrange("p k (h i) -> p k h i", i=8)
        for half in range(2):
            sel.keep(pool, v[half * HD:(half + 1) * HD], [[-2, KT], [1, P // 8], [0, 8]], ALU.is_equal, -half, 0)
        v = spread.rearrange("p k (h i) -> p k h i", i=HD)
        sel.keep(pool, v, [[-16, KT], [-8, 2], [0, HD]], ALU.is_equal, 0, 1)
    return make


def group_norm(c, y, bonus, gate, out, sq, work, gather, spread):
    nc = c.nc
    dev, inv = work[:, 0, :], work[:, 1, :]
    s = {x: c.sem("gn_" + x, primed=x == "d") for x in (
        "mean", "d", "d2", "gathered", "var", "root", "inv", "spread", "n1", "n2", "n3", "full", "high", "low")}

    def tile(t, it, g):
        return t[:, bass.ds(it * 2 + g, 1), :].rearrange("p o t -> p (o t)")

    def banks(g):
        return c.psum[:, 2 * g:2 * g + 2, 0:HALF]

    def over(eng, source, done, step):
        with eng.Fori(0, PAIRS // 2) as it:
            for g in range(2):
                eng.wait_ge(s[source], it * 2 + (g + 1) + (PRIMED if source == "d" else 0))
                step(it, g).then_inc(s[done], 1)

    nc.scalar.preload_act_table_set("sqrt_and_others")
    with c.stage() as block:
        @block.tensor
        def _(pe):
            with pe.Fori(0, PAIRS // 2) as it:
                pe.wait_ge(s["d"], it * 2 + PRIMED)
                for g in range(2):
                    for b in range(2):
                        last = nc.tensor.matmul(c.psum[:, 2 * g + b, 0:HALF], c.head_ones[:], tile(y, it, g)[:, b * HALF:(b + 1) * HALF],
                                                start=True, stop=True)
                    last.then_inc(s["mean"], 1)
            for p in range(PAIRS):
                pe.wait_ge(s["d2"], p + 1)
                for b in range(2):
                    last = nc.tensor.matmul(c.psum[:, 4 + b, 0:HALF], gather[:, p, :], sq[:, p, b * HALF:(b + 1) * HALF],
                                            start=p == 0, stop=p == PAIRS - 1)
            last.then_inc(s["gathered"], 1)
            pe.wait_ge(s["d"], PAIRS + PRIMED)
            pe.wait_ge(s["inv"], 1)
            for p in range(PAIRS):
                if p >= 2:
                    pe.wait_ge(s["n1"], p - 1)
                for b in range(2):
                    last = nc.tensor.matmul(c.psum[:, 2 * (p % 2) + b, 0:HALF], spread[:, p, :], inv[:, b * HALF:(b + 1) * HALF],
                                            start=True, stop=True)
                last.then_inc(s["spread"], 1)

        @block.vector
        def _(dve):
            over(dve, "mean", "d", lambda it, g: nc.vector.scalar_tensor_tensor(
                out=halves(y[:, bass.ds(it * 2 + g, 1), :]), in0=banks(g), scalar=-1.0 / HD,
                in1=halves(y[:, bass.ds(it * 2 + g, 1), :]), op0=ALU.mult, op1=ALU.add))
            dve.wait_ge(s["gathered"], 1)
            nc.vector.tensor_scalar(dev.rearrange("p (a b) -> p a b", a=2), c.psum[:, 4:6, 0:HALF], 1.0 / HD, GN_EPS,
                                    ALU.mult, ALU.add).then_inc(s["var"], 1)
            dve.wait_ge(s["root"], 1)
            nc.vector.reciprocal(inv, dev).then_inc(s["inv"], 1)
            over(dve, "spread", "n1", lambda it, g: nc.vector.tensor_tensor(
                halves(y[:, bass.ds(it * 2 + g, 1), :]), banks(g), halves(y[:, bass.ds(it * 2 + g, 1), :]), ALU.mult))
            over(dve, "high", "low", lambda it, g: take_low(c, tile(out.low, it, g), tile(out.full, it, g), tile(out.high, it, g)))

        @block.scalar
        def _(act):
            over(act, "d", "d2", lambda it, g: nc.scalar.activation(tile(sq, it, g), tile(y, it, g), ACT.Square))
            act.wait_ge(s["var"], 1)
            nc.scalar.activation(dev, dev, ACT.Sqrt).then_inc(s["root"], 1)
            over(act, "n1", "n2", lambda it, g: nc.scalar.activation(
                tile(y, it, g), tile(y, it, g), ACT.Identity, bias=c.vec["rw_lnx_b"][:, bass.ds(it * 2 + g, 1)],
                scale=c.vec["rw_lnx_w"][:, bass.ds(it * 2 + g, 1)]))
            over(act, "full", "high", lambda it, g: nc.scalar.activation(tile(out.high, it, g), tile(out.full, it, g), ACT.Copy))

        @block.gpsimd
        def _(pool):
            with pool.Fori(0, PAIRS // 2) as it:
                for g in range(2):
                    pool.wait_ge(s["n2"], it * 2 + (g + 1))
                    nc.gpsimd.tensor_tensor(tile(y, it, g), tile(y, it, g), tile(bonus, it, g), ALU.add).then_inc(s["n3"], 1)
                    pool.wait_ge(s["n3"], it * 2 + (g + 1))
                    nc.gpsimd.tensor_tensor(tile(out.full, it, g), tile(y, it, g), tile(gate, it, g), ALU.mult).then_inc(s["full"], 1)


def store_rows(c, name, x, stage, groups):
    nc = c.nc
    turned, copied, stored = c.sem(name + "_turned"), c.sem(name + "_copied"), c.sem(name + "_stored")
    steps = [(g, k) for g in range(len(groups)) for k in range(0, KT, 4)]
    with c.stage() as block:
        @block.tensor
        def _(pe):
            for i, (g, k) in enumerate(steps):
                t0, n, _ = groups[g]
                if i >= 4:
                    pe.wait_ge(copied, i - 3)
                for j in range(4):
                    last = nc.tensor.transpose(c.psum[0:n, i % 4, j * P:(j + 1) * P], x[:, k + j, t0:t0 + n], c.ident[:])
                last.then_inc(turned, 1)

        @block.vector
        def _(dve):
            for i, (g, k) in enumerate(steps):
                n = groups[g][1]
                dve.wait_ge(turned, i + 1)
                nc.vector.tensor_copy(stage[0:n, g, k * P:(k + 4) * P], c.psum[0:n, i % 4, :]).then_inc(copied, 1)

        @block.sync
        def _(sp):
            for g, (_, n, out) in enumerate(groups):
                sp.wait_ge(copied, 2 * g + 2)
                sp.dma_start(out, stage[0:n, g, :]).then_inc(stored, 16)
            sp.wait_ge(stored, 16 * len(groups))


def build(nc, ins, outs):
    with ExitStack() as ctx:
        c = Core(nc, ctx, ins, outs)
        x, h = c.region(0), c.region(1)
        h_parts, o_parts = Parts(c, 8, 1), Parts(c, 5, 1)
        xm = c.region(7, t=NMEM)
        mem_parts = Parts(c, 8, 8, t=NMEM, high_at=KT * NMEM)
        qkv, xq = c.region(2, k=3 * KT), c.region(2)
        hidden = Parts(c, 5, 2, k=FT)
        kv = c.region(3, k=2 * KT, t=NMEM)
        kv_rows = c.region(4, k=2, t=2 * D)
        s_rows = [c.region(5, k=2, t=D), c.region(5, k=2, t=D, at=2 * D)]
        s_kt = c.region(6, t=NMEM, at=2 * D)
        gated = c.region(9, k=2, at=6 * T)

        w_qkv = ins["sb_w_qkv"][0]

        def square_job(w, parts):
            return Job(w.shape[1] // P, KT, columns(w), parts=lambda u: (parts.high, parts.low))

        def kv_job(layer):
            return Job(2 * KT, KT, columns(ins["xa_w_kv"][layer]), parts=lambda u: (mem_parts.high, mem_parts.low), tokens=NMEM)

        def up_job(layer):
            w = ins["ffn_w_gate_up"][layer].rearrange("(k p) m -> p k m", p=P)
            return Job(2 * FT, KT, lambda it, u: w[:, :, bass.ds(it * (2 * P) + (u // 2) * P + (u % 2) * FF, P)],
                       parts=lambda u: (h_parts.high, h_parts.low))

        def down_job(layer):
            w = ins["ffn_w_down"][layer].rearrange("(k p) m -> p k m", p=P)
            cuts = [0, 8, 15, FT]

            def part(u):
                return tuple(t[:, cuts[u % 3]:cuts[u % 3 + 1], :] for t in (hidden.high, hidden.low))
            return Job(3 * KT, lambda u: cuts[u % 3 + 1] - cuts[u % 3],
                       lambda it, u: w[:, cuts[u % 3]:cuts[u % 3 + 1], bass.ds(it * (4 * P) + (u // 3) * P, P)],
                       parts=part, slot=lambda u: u // 3, opens=lambda u: u % 3 == 0,
                       closes=lambda u: u % 3 == 2, per=3 * RING)

        qkv_job = square_job(w_qkv, h_parts)
        sbo_job = square_job(ins["sb_w_o"][0], o_parts)
        layer_jobs = []
        for layer in range(DEPTH):
            layer_jobs.append(dict(
                kv=kv_job(layer), xq=square_job(ins["xa_w_q"][layer], h_parts),
                xo=square_job(ins["xa_w_o"][layer], o_parts), up=up_job(layer), down=down_job(layer)))

        x_groups = [(ins["x_prompt"][0], c.region(2, k=4, t=D), x[:, :, 0:SEQ]),
                    (ins["x_sample"][0], c.region(3, k=1, t=D), x[:, :, SEQ:T])]
        stack, x_landed, vectors_landed = vector_rows(c), nc.alloc_semaphore("x_landed"), nc.alloc_semaphore("vectors_landed")
        constants(c, lambda act: (load_rows(act, x_groups, x_landed), stack_vectors(c, act, stack, vectors_landed)))
        turn_vectors(c, stack, vectors_landed)
        load_turned(c, "x", x_groups, x_landed)
        with c.stage() as block:
            @block.sync
            def _(sp):
                for s in range(RING):
                    load_unit(c, sp, qkv_job, 0, s)

        residual = add_to(c, x), {}
        mem_landed, cached_landed, mem_stored = ([nc.alloc_semaphore(f"{name}_landed{layer}") for layer in range(DEPTH)] for name in ("mem", "cached", "mem_rows"))
        mem_groups = [(ins["mem_prompt"][0], c.region(6, k=2, t=D), xm)]

        def load_memory(layer):
            return lambda act: load_rows(act, mem_groups, mem_landed[layer])

        def cached_groups(layer):
            s_k, s_v = (ins[name][layer, 0].rearrange("m h d -> m (h d)") for name in ("cache_mem_k", "cache_mem_v"))
            return [(s_k, s_rows[0], s_kt), (s_v, s_rows[1], None)]

        def memory_attention(layer, nxt):
            jobs = layer_jobs[layer]
            n = f"xa{layer}"
            load_turned(c, n + "_mem", mem_groups, mem_landed[layer])
            norm = Norm(c, n + "_norm", x, c.vec["norm_xattn"][:, layer * KT:], h_parts)
            project(c, jobs["xq"], jobs["kv"], *scaled_to(c, xq, norm, (D // XH) ** -0.5), norm=norm,
                    starts=lambda act: load_rows(act, cached_groups(layer), cached_landed[layer]))
            norm = Norm(c, n + "_mem_norm", xm, c.vec["norm_mem"][:, layer * KT:], mem_parts, NMEM)
            project(c, jobs["kv"], jobs["xo"], *scaled_to(c, kv, norm), norm=norm)
            memory_rows(c, n + "_rows", layer, kv, kv_rows, mem_stored[layer])
            load_turned(c, n + "_cached", cached_groups(layer), cached_landed[layer])
            cross_attention(c, n, xq, kv, kv_rows, s_kt, s_rows[1], h, 7, mem_stored[layer])
            project(c, jobs["xo"], jobs["up"], *residual, norm=Split(c, n + "_o", o_parts))
            norm = Norm(c, n + "_ffn_norm", x, c.vec["norm_ffn"][:, layer * KT:], h_parts)
            gate_and_up(c, n, jobs["up"], jobs["down"], norm, hidden, gated)
            project(c, jobs["down"], nxt, add_to(c, x, units=(2, 5, 8, 11)), {})

        def lora_in_job():
            src = [ins["rw_w1"][0], ins["rw_a1"][0], ins["rw_g1"][0][:, 0:GK], ins["rw_g1"][0][:, GK:GATE]]
            src = [w.rearrange("(k p) m -> p k m", p=P) for w in src]
            mixed = [c.region(3), c.region(4), c.region(5), c.region(5)]
            outs_ = [tanh_w[0:LORA, :], a_low[0:LORA, :], gate_low[0:GK, 0, :], gate_low[0:GK, 1, :]]
            funcs = [ACT.Tanh, ACT.Copy, ACT.Sigmoid, ACT.Sigmoid]

            def emit(s):
                return lambda it, ps: nc.scalar.activation(outs_[s].rearrange("p (a b) -> p a b", a=2), ps, funcs[s])
            return (Job(RING, KT, lambda it, s: src[s], moving=lambda s: mixed[s], m=lambda s: (LORA, LORA, GK, GK)[s]),
                    ({}, {s: emit(s) for s in range(RING)}))

        def lora_out_job(name, low, out, bias):
            def emit(s):
                def run(it, ps):
                    dst = halves(out[:, bass.ds(it * RING + s, 1), :])
                    if bias is None:
                        return nc.scalar.copy(dst, ps)
                    return nc.scalar.activation(dst, ps, ACT.Sigmoid, bias=c.vec[bias][:, bass.ds(it * RING + s, 1)])
                return run
            kt = low.shape[1]
            return (Job(KT, kt, columns(ins[name][0], kp=low.shape[0]), lambda s: low, kp=low.shape[0]),
                    ({}, {s: emit(s) for s in range(RING)}))

        gate_low = c.flat(9, 2 * T).rearrange("p (k t) -> p k t", k=2)
        tanh_w, a_low = c.flat(9, T, at=2 * T), c.flat(9, T, at=3 * T)

        def time_mix_job(w, parts, out):
            return Job(KT, KT, columns(ins[w][0]), parts=lambda u: (parts.high, parts.low)), copy_to(c, out)

        norm = Norm(c, "sb_norm", x, c.vec["norm_mix"], h_parts)
        project(c, qkv_job, sbo_job, *scaled_to(c, qkv, norm), norm=norm, by_pool=wkv_constants(c))
        stick_breaking(c, *(qkv[:, i * KT:(i + 1) * KT, :] for i in range(3)), h, 5)
        project(c, sbo_job, layer_jobs[0]["xq"], *residual, starts=load_memory(0), norm=Split(c, "sb_o", o_parts))
        lora_in = lora_in_job()
        memory_attention(0, lora_in[0])
        r_out, k_out, v_out = c.region(3), c.region(4), c.region(5)
        mixes = [Parts(c, 7, 6), Parts(c, 5, 8)]
        time_mix = [time_mix_job("rw_w_r", mixes[0], r_out), time_mix_job("rw_w_k", mixes[1], k_out),
                    time_mix_job("rw_w_v", mixes[0], v_out)]
        lora_w = lora_out_job("rw_w2", tanh_w[0:LORA, :].rearrange("p (o t) -> p o t", o=1), c.region(6), "rw_w0")
        lora_a = lora_out_job("rw_a2", a_low[0:LORA, :].rearrange("p (o t) -> p o t", o=1), c.region(7), "rw_a0")
        lora_g = lora_out_job("rw_g2", gate_low[0:GK], c.region(6), None)
        xx = c.region(2)
        rms(c, "rw_norm", x, h, c.vec["norm_mix"][:, KT:])
        token_shift(c, h, xx, [(1, c.region(3))])

        def mix_ahead(m, out):
            mixed = c.sem(f"mixed{m}")

            def run(it, u):
                at, n = it * RING + u, it * (3 * RING) + 3 * u
                full, high, low = (t[:, bass.ds(at, 1), :] for t in (out.full, out.high, out.low))
                nc.vector.scalar_tensor_tensor(
                    out=full, in0=xx[:, bass.ds(at, 1), :], scalar=c.vec["rw_mu"][:, bass.ds(at + m * KT, 1)],
                    in1=h[:, bass.ds(at, 1), :], op0=ALU.mult, op1=ALU.add).then_inc(mixed, 1)
                nc.vector.wait_ge(mixed, n + 1)
                take_high(c, high, full).then_inc(mixed, 1)
                nc.vector.wait_ge(mixed, n + 2)
                take_low(c, low, full, high).then_inc(mixed, 1)
                nc.vector.wait_ge(mixed, n + 3)
            return run
        lora_mixed = c.sem("lora_mixed")
        lora_in[0].ready = {1: (lora_mixed, KT), 2: (lora_mixed, 2 * KT)}
        mix_r = mix_ahead(0, mixes[0])

        def mix_lora(it, u):
            if u == 0:
                mix_tokens(c, h, xx, 4, c.region(4), lora_mixed)
                mix_tokens(c, h, xx, 5, c.region(5), lora_mixed)
            mix_r(it, u)
        project(c, lora_in[0], time_mix[0][0], *lora_in[1], beside=mix_lora)
        project(c, time_mix[0][0], time_mix[1][0], *time_mix[0][1], beside=mix_ahead(2, mixes[1]))
        project(c, time_mix[1][0], time_mix[2][0], *time_mix[1][1], beside=mix_ahead(3, mixes[0]))
        key_norms(c, k_out, c.region(8), 4 * T)

        inverted = c.sem("norms_inverted")

        def invert_norms(it, u):
            norm = c.region(8)[:, bass.ds(it * RING + u, 1), :]
            return nc.vector.reciprocal(norm, norm).then_inc(inverted, 1)
        project(c, time_mix[2][0], lora_w[0], *time_mix[2][1], beside=invert_norms)
        project(c, lora_w[0], lora_a[0], *lora_w[1])
        project(c, lora_a[0], None, *lora_a[1])
        A, B, bonus = c.region(1), c.region(2), c.region(8)
        decay_factors(c, r_out, k_out, v_out, c.region(6), c.region(7), bonus, A, B)
        states, finals = (c.ring_words()[:, i * KT * P:(i + 1) * KT * P].rearrange("p (j n) -> p j n", j=KT) for i in range(2))
        n = 16 * 4 * P
        more = [c.flat(9, 6 * 4 * P, at=2 * T), c.ring_words()[:, 2 * KT * P:], c.high[:].rearrange("p s k n -> p (s k n)"),
                c.tile("more_words", [P, 2 * 4 * P])[:]]
        quads = [Quad([c.flat(6, n)], c.flat(6, 4 * L, at=n)), Quad(more, c.flat(6, 4 * L, at=n + 4 * L))]
        turning = c.region(6, t=P)
        for sample in (False, True):
            if sample:
                load_states(c, states, turning)
            c.free_semaphores()
            wkv(c, quads, states, finals, A, B, r_out, k_out, v_out, A, sample)
            store_states(c, finals, turning, outs["sample_rwkv_wkv" if sample else "prompt_rwkv_wkv"])
        with c.stage() as block:
            @block.sync
            def _(sp):
                for s in range(RING):
                    load_unit(c, sp, lora_g[0], 0, s)
        out_parts = Parts(c, 4, 3)
        o_job = Job(KT, KT, columns(ins["rw_w_o"][0]), parts=lambda u: (out_parts.high, out_parts.low))
        gather, spread = c.region(2, t=P), c.region(5, t=P)
        project(c, lora_g[0], o_job, *lora_g[1], by_pool=head_selectors(c, gather, spread))
        group_norm(c, A, bonus, c.region(6), out_parts, c.region(9), c.region(7, k=2), gather, spread)
        project(c, o_job, layer_jobs[1]["xq"], *residual, starts=load_memory(1))
        memory_attention(1, None)
        rms(c, "final_norm", x, h, c.vec["norm_final"])
        rows = outs["y_prompt"][0].rearrange("(g p) d -> g p d", p=P)
        store_rows(c, "y", h, c.region(2, k=5, t=D), [(g * P, P, rows[g]) for g in range(SEQ // P)] + [(SEQ, DEC, outs["y_sample"][0])])


_INS = ["x_prompt", "x_sample", "mem_prompt", "cache_sb_k", "cache_sb_v", "state_rwkv_wkv",
        "state_rwkv_shift", "cache_mem_k", "cache_mem_v", "norm_mix", "norm_xattn", "norm_ffn", "norm_mem",
        "norm_final", "sb_w_qkv", "sb_w_o", "rw_mu", "rw_w_r", "rw_w_k", "rw_w_v", "rw_w_o", "rw_w0",
        "rw_w1", "rw_w2", "rw_a0", "rw_a1", "rw_a2", "rw_g1", "rw_g2", "rw_k_k", "rw_k_a", "rw_r_k",
        "rw_lnx_w", "rw_lnx_b", "xa_w_q", "xa_w_kv", "xa_w_o", "ffn_w_gate_up", "ffn_w_down"]
_OUTS = [("y_prompt", (1, 512, 1024)), ("y_sample", (1, 32, 1024)), ("prompt_sb_k", (1, 1, 512, 16, 64)),
         ("prompt_sb_v", (1, 1, 512, 16, 64)), ("prompt_rwkv_wkv", (1, 1, 16, 64, 64)),
         ("prompt_rwkv_shift", (1, 1, 1024)), ("prompt_mem_k", (2, 1, 256, 4, 256)),
         ("prompt_mem_v", (2, 1, 256, 4, 256)), ("sample_sb_k", (1, 1, 32, 16, 64)),
         ("sample_sb_v", (1, 1, 32, 16, 64)), ("sample_rwkv_wkv", (1, 1, 16, 64, 64)),
         ("sample_rwkv_shift", (1, 1, 1024))]


def kernel(**inputs):
    import numpy as _np
    import concourse.bacc as _bacc
    from concourse import mybir as _mybir
    from concourse.bass_utils import run_bass_kernel_spmd as _run

    nc = _bacc.Bacc("TRN2", target_bir_lowering=False, num_devices=1)
    arrays, ins, outs = {}, {}, {}
    for name in _INS:
        a = _np.ascontiguousarray(inputs[name])
        arrays[f"in_{name}_dram"] = a
        ins[name] = nc.dram_tensor(f"in_{name}_dram", a.shape, _mybir.dt.from_np(a.dtype), kind="ExternalInput").ap()
    for name, shape in _OUTS:
        outs[name] = nc.dram_tensor(f"out_{name}_dram", shape, _mybir.dt.float32, kind="ExternalOutput").ap()
    build(nc, ins, outs)
    r = _run(nc, [arrays], core_ids=[0])
    return tuple(r.results[0][f"out_{name}_dram"] for name, _ in _OUTS)
```
